# Optimizing a Trainium2 kernel written in Bass

```python
import math
import jax, jax.numpy as jnp
from jax import lax
import numpy as np

D_MODEL = 1024
BATCH = 1
SEQ = 256
DEPTH = 1

D_MIX = D_MODEL
ATTN_WIDTH = D_MIX // 2
HGRN_WIDTH = D_MIX - ATTN_WIDTH
ATTN_HEAD_DIM = 64
N_Q_HEADS = ATTN_WIDTH // ATTN_HEAD_DIM
N_KV_HEADS = 2
KV_WIDTH = N_KV_HEADS * ATTN_HEAD_DIM
WINDOW = 128
ATTN_BLOCK = 128
HGRN_HEAD_DIM = 128
N_HGRN_HEADS = HGRN_WIDTH // HGRN_HEAD_DIM
HGRN_CHUNK = 64
N_EXPERTS = 32
TOP_K = 4
D_EXPERT = D_MODEL
SWIGLU_LIMIT = 7.0
SWIGLU_ALPHA = 1.702
LN_EPS = 1e-5
RMS_EPS = 1e-6
DEEPNORM_ALPHA = (2.0 * DEPTH) ** 0.25
DEEPNORM_BETA = (8.0 * DEPTH) ** -0.25
IN_WIDTHS = (ATTN_WIDTH, KV_WIDTH, KV_WIDTH, HGRN_WIDTH, HGRN_WIDTH, HGRN_WIDTH, HGRN_WIDTH, HGRN_WIDTH)
IN_COLS = sum(IN_WIDTHS)
IN_SPLITS = tuple(int(c) for c in np.cumsum(IN_WIDTHS)[:-1])

kernel_name = 'hymba_swa_hgrn2_moe_encoder'

def layer_norm(x, g, b):
    xf = x.astype(jnp.float32)
    mu = jnp.mean(xf, axis=-1, keepdims=True)
    var = jnp.mean(jnp.square(xf - mu), axis=-1, keepdims=True)
    y = (xf - mu) * lax.rsqrt(var + LN_EPS) * g.astype(jnp.float32) + b.astype(jnp.float32)
    return y.astype(x.dtype)

def alibi_slopes(n):
    return jnp.asarray([2.0 ** (-8.0 * (h + 1) / n) for h in range(n)], jnp.float32)

def windowed_gqa(q, k, v, sink):
    b, s = q.shape[0], q.shape[1]
    nb = s // ATTN_BLOCK
    g, r = N_KV_HEADS, N_Q_HEADS // N_KV_HEADS
    qb = q.reshape(b, nb, ATTN_BLOCK, g, r, ATTN_HEAD_DIM)
    pad = ((0, 0), (ATTN_BLOCK, ATTN_BLOCK), (0, 0), (0, 0))

    def band(t):
        tp = jnp.pad(t, pad).reshape(b, nb + 2, ATTN_BLOCK, g, ATTN_HEAD_DIM)
        return jnp.concatenate([tp[:, :-2], tp[:, 1:-1], tp[:, 2:]], axis=2)

    kb, vb = band(k), band(v)
    scores = jnp.einsum('bnqgrd,bnkgd->bgrnqk', qb, kb).astype(jnp.float32) * (1.0 / math.sqrt(ATTN_HEAD_DIM))
    qpos = jnp.arange(nb)[:, None, None] * ATTN_BLOCK + jnp.arange(ATTN_BLOCK)[None, :, None]
    kpos = jnp.arange(nb)[:, None, None] * ATTN_BLOCK - ATTN_BLOCK + jnp.arange(3 * ATTN_BLOCK)[None, None, :]
    dist = jnp.abs(kpos - qpos)
    valid = (dist <= WINDOW) & (kpos >= 0) & (kpos < s)
    slopes = alibi_slopes(N_Q_HEADS).reshape(g, r)[:, :, None, None, None]
    scores = jnp.where(valid, scores - slopes * dist.astype(jnp.float32), -jnp.inf)
    sink_l = sink.astype(jnp.float32).reshape(g, r)[None, :, :, None, None, None]
    m = jnp.maximum(jnp.max(scores, axis=-1, keepdims=True), sink_l)
    e = jnp.exp(scores - m)
    p = e / (jnp.sum(e, axis=-1, keepdims=True) + jnp.exp(sink_l - m))
    out = jnp.einsum('bgrnqk,bnkgd->bnqgrd', p.astype(vb.dtype), vb)
    return out.reshape(b, s, N_Q_HEADS * ATTN_HEAD_DIM)

def gated_linear_scan(q, k, v, log_f):
    b, s, h, dk = q.shape
    dv = v.shape[-1]
    c = HGRN_CHUNK
    n = s // c
    rs = lambda t: t.reshape(b, n, c, h, t.shape[-1])
    q, k, v, log_f = rs(q), rs(k), rs(v), rs(log_f)
    cum = jnp.cumsum(log_f, axis=2)
    last = cum[:, :, -1]
    ref = cum[:, :, c // 2][:, :, None]
    q_rel = q * jnp.exp(cum - ref)
    k_rel = k * jnp.exp(ref - cum)
    lower = jnp.tril(jnp.ones((c, c), dtype=bool))
    a = jnp.einsum('bnthd,bnshd->bnhts', q_rel, k_rel)
    a = jnp.where(lower, a, 0.0)
    o_intra = jnp.einsum('bnhts,bnshv->bnthv', a, v)
    chunk_kv = jnp.einsum('bnshd,bnshv->bnhdv', k * jnp.exp(last[:, :, None] - cum), v)
    decay = jnp.exp(last)

    def step(state, inp):
        dec, kv = inp
        return dec[..., None] * state + kv, state

    init = jnp.zeros((b, h, dk, dv), jnp.float32)
    _, s_prev = lax.scan(step, init, (jnp.swapaxes(decay, 0, 1), jnp.swapaxes(chunk_kv, 0, 1)))
    s_prev = jnp.swapaxes(s_prev, 0, 1)
    o_inter = jnp.einsum('bnthd,bnhdv->bnthv', q * jnp.exp(cum), s_prev)
    return (o_intra + o_inter).reshape(b, s, h, dv)

def hgrn2_bidirectional(q, i, zf_fwd, zf_bwd, z_g, lb, norm_g):
    b, s = q.shape[0], q.shape[1]
    heads = lambda t: t.astype(jnp.float32).reshape(b, s, N_HGRN_HEADS, HGRN_HEAD_DIM)
    qh, vh = heads(q), heads(i)

    def gate(zf, lb_d):
        f = lb_d + (1.0 - lb_d) * jax.nn.sigmoid(zf.astype(jnp.float32))
        f = heads(f)
        return jnp.log(f), 1.0 - f

    log_ff, k_f = gate(zf_fwd, lb[0])
    log_fb, k_b = gate(zf_bwd, lb[1])
    flip = lambda t: jnp.flip(t, axis=1)
    o_f = gated_linear_scan(qh, k_f, vh, log_ff)
    o_b = flip(gated_linear_scan(flip(qh), flip(k_b), flip(vh), flip(log_fb)))
    o = o_f + o_b
    o = o * lax.rsqrt(jnp.mean(jnp.square(o), axis=-1, keepdims=True) + RMS_EPS)
    o = o.reshape(b, s, HGRN_WIDTH) * norm_g.astype(jnp.float32) * jax.nn.silu(z_g.astype(jnp.float32))
    return o.astype(q.dtype)

def hybrid_mixer(h, w_in, sink, lb, norm_g, w_out):
    b, s, _ = h.shape
    proj = h @ w_in
    q_a, k_a, v_a, q_h, i_h, zf_fwd, zf_bwd, z_g = jnp.split(proj, IN_SPLITS, axis=-1)
    attn = windowed_gqa(q_a.reshape(b, s, N_Q_HEADS, ATTN_HEAD_DIM),
                        k_a.reshape(b, s, N_KV_HEADS, ATTN_HEAD_DIM),
                        v_a.reshape(b, s, N_KV_HEADS, ATTN_HEAD_DIM), sink)
    rec = hgrn2_bidirectional(q_h, i_h, zf_fwd, zf_bwd, z_g, lb, norm_g)
    return jnp.concatenate([attn.astype(h.dtype), rec], axis=-1) @ w_out

def moe_ffn(x, w_router, b_router, w_up, b_up, w_down, b_down):
    logits = (x @ w_router + b_router).astype(jnp.float32)
    top_v, top_i = lax.top_k(logits, TOP_K)
    gates = jax.nn.softmax(top_v, axis=-1)
    gate_full = jnp.sum(jax.nn.one_hot(top_i, N_EXPERTS, dtype=jnp.float32) * gates[..., None], axis=1)
    gate_full = gate_full.astype(x.dtype)
    out = jnp.zeros_like(x)
    for e in range(N_EXPERTS):
        hid = x @ w_up[e] + b_up[e]
        x_glu = jnp.minimum(hid[..., ::2], SWIGLU_LIMIT)
        x_lin = jnp.clip(hid[..., 1::2], -SWIGLU_LIMIT, SWIGLU_LIMIT)
        act = x_glu * jax.nn.sigmoid(SWIGLU_ALPHA * x_glu) * (x_lin + 1.0)
        out = out + gate_full[:, e:e + 1] * (act @ w_down[e] + b_down[e])
    return out

def setup_inputs(seed: int = 0) -> dict:
    key = jax.random.key(seed)
    ks = jax.random.split(key, 20)
    f32 = jnp.float32
    nrm = lambda k, shape, sc: jax.random.normal(k, shape, f32) * sc
    col_scale = jnp.concatenate([
        jnp.full((w,), sc, f32) for w, sc in zip(
            IN_WIDTHS, (1.0, 1.0, DEEPNORM_BETA, 1.0, DEEPNORM_BETA, 1.0, 1.0, 1.0))])
    return {
        'x': nrm(ks[0], (BATCH, SEQ, D_MODEL), 1.0),
        'emb_ln_g': 1.0 + nrm(ks[1], (D_MODEL,), 0.02),
        'emb_ln_b': nrm(ks[2], (D_MODEL,), 0.02),
        'w_in': nrm(ks[3], (DEPTH, D_MODEL, IN_COLS), D_MODEL ** -0.5) * col_scale,
        'attn_sink': nrm(ks[4], (DEPTH, N_Q_HEADS), 0.5),
        'hgrn_lb_logits': nrm(ks[5], (2, DEPTH + 1, HGRN_WIDTH), 0.1),
        'hgrn_norm_g': 1.0 + nrm(ks[6], (DEPTH, HGRN_WIDTH), 0.02),
        'w_out': nrm(ks[7], (DEPTH, D_MIX, D_MODEL), D_MIX ** -0.5 * DEEPNORM_BETA),
        'ln1_g': 1.0 + nrm(ks[8], (DEPTH, D_MODEL), 0.02),
        'ln1_b': nrm(ks[9], (DEPTH, D_MODEL), 0.02),
        'w_router': nrm(ks[10], (DEPTH, D_MODEL, N_EXPERTS), D_MODEL ** -0.5),
        'b_router': nrm(ks[11], (DEPTH, N_EXPERTS), 0.01),
        'w_up': nrm(ks[12], (DEPTH, N_EXPERTS, D_MODEL, 2 * D_EXPERT), D_MODEL ** -0.5),
        'b_up': nrm(ks[13], (DEPTH, N_EXPERTS, 2 * D_EXPERT), 0.01),
        'w_down': nrm(ks[14], (DEPTH, N_EXPERTS, D_EXPERT, D_MODEL), D_EXPERT ** -0.5 * DEEPNORM_BETA),
        'b_down': nrm(ks[15], (DEPTH, N_EXPERTS, D_MODEL), 0.01),
        'ln2_g': 1.0 + nrm(ks[16], (DEPTH, D_MODEL), 0.02),
        'ln2_b': nrm(ks[17], (DEPTH, D_MODEL), 0.02),
    }

def reference(x, emb_ln_g, emb_ln_b, w_in, attn_sink, hgrn_lb_logits, hgrn_norm_g, w_out,
              ln1_g, ln1_b, w_router, b_router, w_up, b_up, w_down, b_down, ln2_g, ln2_b):
    h = layer_norm(x, emb_ln_g, emb_ln_b)
    lb_all = jnp.cumsum(jax.nn.softmax(hgrn_lb_logits.astype(jnp.float32), axis=1), axis=1)
    for l in range(DEPTH):
        mix = hybrid_mixer(h, w_in[l], attn_sink[l], lb_all[:, l], hgrn_norm_g[l], w_out[l])
        h = layer_norm(DEEPNORM_ALPHA * h + mix, ln1_g[l], ln1_b[l])
        ffn = moe_ffn(h.reshape(-1, D_MODEL), w_router[l], b_router[l], w_up[l], b_up[l],
                      w_down[l], b_down[l]).reshape(h.shape)
        h = layer_norm(DEEPNORM_ALPHA * h + ffn, ln2_g[l], ln2_b[l])
    return h


_drawn_inputs = setup_inputs


def setup_inputs(seed=0):
    import zlib

    import numpy as np

    out = dict(_drawn_inputs(seed))
    spreads = {}
    factors = {'attn_sink': 4.59,
     'hgrn_norm_g': 4.64,
     'b_router': 2.935,
     'b_up': 8.0,
     'b_down': 8.0,
     'ln2_g': 2.864,
     'ln2_b': 2.874}
    for name, (base, spread) in spreads.items():
        noise = np.random.default_rng([zlib.crc32(name.encode()), seed]).standard_normal(out[name].shape)
        drawn = base * np.exp(spread * noise) if base else spread * noise
        out[name] = __import__('jax').numpy.asarray(drawn.astype(out[name].dtype))
    for name, factor in factors.items():
        out[name] = (out[name] * factor).astype(out[name].dtype)
    return out
```

```python
from contextlib import ExitStack

import concourse.bass as bass
from concourse import mybir

F32 = mybir.dt.float32
I32 = mybir.dt.int32
U32 = mybir.dt.uint32
ALU = mybir.AluOpType
ACT = mybir.ActivationFunctionType
AX_X = mybir.AxisListType.X

P = 128
TOPK = 4
WINDOW = 128
HG_CHUNK = 64
LIMIT, SIG_ALPHA = 7.0, 1.702
LN_EPS, RMS_EPS = 1e-5, 1e-6
DEEP_ALPHA = 2.0 ** 0.25
FAR = 1e30
NOT_HERE = 4096.0
SLOTS = 64


def counted(eng, sem):
    state = {"n": 0}

    def link(ins):
        state["n"] += 1
        ins.then_inc(sem, 1)
        eng.wait_ge(sem, state["n"])

    return link, state


def encoder_layer(nc, x, emb_ln_g, emb_ln_b, w_in, attn_sink, hgrn_lb_logits, hgrn_norm_g, w_out,
                  ln1_g, ln1_b, w_router, b_router, w_up, b_up, w_down, b_down, ln2_g, ln2_b, out):
    D = x.shape[2]
    KT = D // P
    TT = x.shape[1] // P
    TOK = TT * P
    NE = w_router.shape[2]
    FF = w_down.shape[2]
    HQ = attn_sink.shape[1]
    DH, NG = 64, 2
    QPG = HQ // NG
    HW = hgrn_norm_g.shape[1]
    NH = HW // P
    NC = TOK // HG_CHUNK
    NPASS = NE + TOK * TOPK // (SLOTS + 1) + 1
    NPASS += NPASS % 2
    UPC, DNC = KT, KT // 2
    CHUNKS = UPC + DNC
    CW = 2 * FF

    A0, K0, Q0 = 0, HQ * DH, HQ * DH + 2 * NG * DH
    GROUPS = [("zf0", Q0 + 2 * HW, HW), ("zf1", Q0 + 3 * HW, HW), ("qh", Q0, HW), ("ih", Q0 + HW, HW),
              ("qa", A0, HQ * DH), ("kv", K0, 2 * NG * DH), ("zg", Q0 + 4 * HW, HW)]
    GI = {g[0]: n for n, g in enumerate(GROUPS)}
    WBUF = 3

    with ExitStack() as ctx:
        def sb(name, shape, dt=F32):
            return ctx.enter_context(nc.sbuf_tensor(name, shape, dt))

        def sem(name):
            return ctx.enter_context(nc.semaphore(name))

        bank = [ctx.enter_context(nc.psum_tensor(f"bank{i}", [P, 512], F32)) for i in range(8)]

        ring = sb("ring", [P, CHUNKS, CW])
        wbuf = sb("wbuf", [P, WBUF, 4096])
        half = ring[:, :, :].rearrange("p c (a n) -> p (c a) n", a=2)

        def wide(i):
            return half[:, i, :]

        hg = [dict(k=wide(8 + d * 8), C=wide(9 + d * 8), A=wide(10 + d * 8), Dl=wide(11 + d * 8),
                   qrel=wide(12 + d * 8), krel=wide(13 + d * 8), kp=wide(14 + d * 8), qe=wide(15 + d * 8))
              for d in range(2)]
        score = [wide(0), wide(1)]
        probT = [wide(2), wide(3)]
        state = ring[:, 2, :].rearrange("p (d i n) -> p d i n", d=2, i=2)
        state3 = ring[:, 3, 0:1024].rearrange("p (d n) -> p d n", d=2)

        scanm = wide(7)

        def S(d, i):
            return state[:, d, i, :] if i < 2 else state3[:, d, :]

        acc = wbuf[:, 0, 0:TT * D].rearrange("p (t n) -> p t n", t=TT)
        glu, lin, sig, act_ = (wbuf[:, 0, TT * D + i * 512:TT * D + (i + 1) * 512] for i in range(4))
        bup = wbuf[:, 2, 0:2 * FF]
        ysb = wbuf[:, 2, 2048:3072]
        xT = wbuf[:, 2, 3072:3584].rearrange("p (k s) -> p k s", k=KT)
        actT = wbuf[:, 2, 3584:4096]

        tmp4 = wbuf[:, 1, 0:512].rearrange("p (t m j e) -> p t m j e", t=TT, m=2, j=TOPK)
        pick = wbuf[:, 1, 512:512 + TT * SLOTS].rearrange("p (t n) -> p t n", t=TT)
        gpick = wbuf[:, 1, 1024:1024 + TT * 2 * SLOTS].rearrange("p (t n) -> p t n", t=TT)

        keyp, gatep = (wbuf[:, 1, o:o + TT * NPASS].rearrange("p (t n) -> p t n", t=TT) for o in (1536, 1792))
        keyT = wbuf[0:NE, 1, 2048:2048 + TOK]
        dlt = wbuf[0:NE, 1, 2304:2304 + 3 * NPASS].rearrange("p (i n) -> p i n", i=3)

        kpad = wbuf[:, 2, 3072:4096].rearrange("p (g o n) -> p g o n", g=NG, o=2)

        X = sb("X", [P, TT, D])
        hT = sb("hT", [P, KT, TOK])
        lnp = sb("lnp", [P, 2, D])
        cat = sb("cat", [P, TT, D])
        qhT = sb("qhT", [P, NH * TOK])
        ih = sb("ih", [P, TT, HW])
        gz = sb("gz", [P, TT, HW])
        qaT = sb("qaT", [P, HQ // 2, TOK])
        va = sb("va", [P, TT, P])
        ident = sb("ident", [P, P])
        ones = sb("ones", [P, P])
        below = sb("below", [P, P])
        maskF = sb("maskF", [P, P])
        maskB = sb("maskB", [P, P])
        dist = sb("dist", [P, TT, TOK])
        iota_s = sb("iota_s", [P, 2, SLOTS])
        part = sb("part", [P, 1])
        epsc = sb("epsc", [P, 2])
        normg = sb("normg", [P, HW])
        wr = sb("wr", [P, KT, NE])
        br = sb("br", [P, NE])
        sink = sb("sink", [P, HQ])
        lbrow = sb("lbrow", [16, P])
        lbt = sb("lbt", [P, 2, 2, NH])
        lb = sb("lb", [P, 2, NH])
        oml = sb("oml", [P, 2, NH])
        lbs = sb("lbs", [P, 2, NH])
        lbe = sb("lbe", [P, 2, 2, NH])
        st = sb("st", [P, TT, 2, 6])
        mv = sb("mv", [P, TT, 2])
        rstd = sb("rstd", [P, TT])
        mx = sb("mx", [P, QPG])
        nm, den, es, rden = (sb(n, [P, 2, QPG]) for n in ("nm", "den", "es", "rden"))
        decay = sb("decay", [P, 2, NH * NC])
        ssq = sb("ssq", [P, TT, NH])
        rr = sb("rr", [P, TT, NH])
        lg = sb("lg", [P, TT, NE])
        m8 = sb("m8", [P, TT, 8])
        i8 = sb("i8", [P, TT, 8], U32)
        i8f = sb("i8f", [P, TT, 8])
        nm0 = sb("nm0", [P, TT])
        g4 = sb("g4", [P, TT, TOPK])
        gs = sb("gs", [P, TT])
        gm = sb("gm", [P, TT, 2, NE])
        key = sb("key", [P, TT, NE])
        cnt = sb("cnt", [NE, 8])
        esel = sb("esel", [P, NPASS])
        base = sb("base", [NE, NPASS])
        plan = sb("plan", [1, NPASS + 2], I32)
        bsel = sb("bsel", [P, SLOTS])
        putT = sb("putT", [P, TOK])

        names = ("x_in emb_in ln1_in ln2_in par_in wout_in bias_in zeroed consts h_ready hT_ps hT_ready "
                 "lb_ps proj_done job_done attn_done hgrn_done logf_ready logf_in exps_in k_ready "
                 "var_ready std_ready qh_ready qa_ready kv_ready ih_ready zg_sig gz_ready score_ready mx_ready "
                 "prob_ready sink_ready attn_cat rec_cat sq_ready rms_in rms_std mix_done x1_ready "
                 "logit_done top_ready g4_ready mask_ready rank_done ex_ready route_done "
                 "key_ready sel_ready plan_ps plan_ready lbm_ready lb_exp kpT_ready aT_ready S_ready "
                 "chunk_used picked put_ps gath_done actT_ps scat_done scat_read put_ready xT_ready "
                 "actT_ready y_ready glu_ready sig_ready act_ready acc_ready stored dve_step act_step pool_step tail_step").split()
        s = {n: sem(n) for n in names}
        win_in = [sem(f"win_in{i}") for i in range(WBUF)]
        proj_read = [sem(f"proj_read{i}") for i in range(len(GROUPS))]
        job_read = [sem(f"job_read{i}") for i in range(4)]
        chunk_in = [sem(f"chunk_in{i}") for i in range(CHUNKS)]

        jobs = [("kpT", 0, 0), ("kpT", 0, 1), ("aT", 0, 0), ("aT", 0, 1),
                ("kpT", 1, 0), ("kpT", 1, 1), ("aT", 1, 0), ("aT", 1, 1)]
        jobs += [("kv", d, i) for i in range(NC - 1) for d in range(2)]
        BATCH = [(t, g) for t in range(TT) for g in range(NG)]
        order = []
        for b in range(len(BATCH) + 1):
            if b < len(BATCH):
                order += [("score", b, 0), ("score", b, 1)]
            if b >= 1:
                order += [("pT", b - 1, 0), ("pT", b - 1, 1)]
        jobs += order
        jobs += [("catT", i, 0) for i in range(4)] + [("x1T", i, 0) for i in range(4)]
        J = {j: n for n, j in enumerate(jobs)}

        def chunk_of(d, i):
            return i if d == 0 else NC - 1 - i

        w_in_v = w_in[0].rearrange("(k p) n -> p k n", p=P)
        w_out_v = w_out[0].rearrange("(k p) n -> p k n", p=P)
        up_v = w_up[0].rearrange("e (k p) n -> e k p n", p=P)
        dn_v = w_down[0].rearrange("e (a i p) n -> e i p a n", a=2, p=P)
        x_v = x[0].rearrange("(t p) n -> p t n", p=P)
        out_v = out[0].rearrange("(t p) n -> p t n", p=P)

        block = ctx.enter_context(nc.Block())

        def load_chunk(sp, e, c):
            dst = ring[:, c, :]
            if c < UPC:
                src = up_v[e, c] if isinstance(e, int) else up_v[bass.ds(e, 1), c].rearrange("a p n -> (a p) n")
            else:
                dst = dst.rearrange("p (a n) -> p a n", a=2)
                src = dn_v[e, c - UPC] if isinstance(e, int) else \
                    dn_v[bass.ds(e, 1), c - UPC].rearrange("o p a n -> (o p) a n")
            sp.dma_start(dst, src).then_inc(chunk_in[c], 16)

        @block.sync
        def _(sp):
            sp.dma_start(X[:, :, :], x_v).then_inc(s["x_in"], 16)
            for g, (_, c0, w) in enumerate(GROUPS):
                if g >= WBUF:
                    sp.wait_ge(s["proj_done"], g - WBUF + 1)
                sp.dma_start(wbuf[:, g % WBUF, 0:KT * w].rearrange("p (k n) -> p k n", k=KT),
                             w_in_v[:, :, c0:c0 + w]).then_inc(win_in[g % WBUF], 16)
            sp.wait_ge(s["h_ready"], TT)
            sp.dma_start(lnp[:, 0, :], ln1_g[0].partition_broadcast(P)).then_inc(s["ln1_in"], 16)
            sp.dma_start(lnp[:, 1, :], ln1_b[0].partition_broadcast(P)).then_inc(s["ln1_in"], 16)
            for i, b in enumerate((1, 0)):
                sp.wait_ge(s["proj_done"], 5 + 2 * i)
                sp.dma_start(wbuf[:, b, :].rearrange("p (k n) -> p k n", k=4),
                             w_out_v[:, 4 * i:4 * i + 4, :]).then_inc(s["wout_in"], 16)
            sp.wait_ge(s["attn_cat"], len(BATCH))
            sp.wait_ge(s["rec_cat"], TT)
            for c in range(CHUNKS):
                load_chunk(sp, 0, c)
            sp.wait_ge(s["zeroed"], 3)
            sp.dma_start(bup[0:NE, :], b_up[0]).then_inc(s["bias_in"], 16)
            sp.dma_start(ysb[0:NE, :], b_down[0]).then_inc(s["bias_in"], 16)
            sp.wait_ge(s["x1_ready"], TT)
            sp.dma_start(lnp[:, 0, :], ln2_g[0].partition_broadcast(P)).then_inc(s["ln2_in"], 16)
            sp.dma_start(lnp[:, 1, :], ln2_b[0].partition_broadcast(P)).then_inc(s["ln2_in"], 16)
            sp.wait_ge(s["plan_ready"], 2)
            npass = sp.value_load(plan[0:1, NPASS:NPASS + 1], min_val=NE, max_val=NPASS - 1)
            with sp.Fori(1, npass) as p:
                e = sp.value_load(plan[0:1, bass.ds(p, 1)], min_val=0, max_val=NE - 1)
                for c in range(CHUNKS):
                    sp.wait_ge(s["chunk_used"], (p - 1) * CHUNKS + c + 1)
                    load_chunk(sp, e, c)
            sp.wait_ge(s["acc_ready"], TT)
            sp.dma_start(out_v, acc).then_inc(s["stored"], 16)
            sp.wait_ge(s["stored"], 16)

        @block.gpsimd
        def _(pool):
            link, _ = counted(pool, s["pool_step"])
            const, _ = counted(pool, s["consts"])
            g = nc.gpsimd
            link(g.memset(ident[:, :], 0.0))
            const(g.affine_select(out=ident[:, :], in_=ident[:, :], compare_op=ALU.not_equal, fill=1.0, base=0,
                            pattern=[[-1, P]], channel_multiplier=1))
            const(g.memset(epsc[:, 0:1], LN_EPS))
            const(g.memset(epsc[:, 1:2], RMS_EPS))
            link(g.memset(ones[:, :], 1.0))
            link(g.memset(scanm, 1.0))
            const(g.memset(scanm.rearrange("p (c n) -> p c n", n=HG_CHUNK)[:, :, 0:1], 0.0))
            link(g.affine_select(out=maskF[:, :], in_=ones[:, :], compare_op=ALU.is_ge, fill=0.0, base=0,
                                 pattern=[[1, P]], channel_multiplier=-1))
            const(g.memset(maskF[0:HG_CHUNK, HG_CHUNK:P], 0.0))
            link(g.affine_select(out=maskB[:, :], in_=ones[:, :], compare_op=ALU.is_ge, fill=0.0, base=0,
                                 pattern=[[-1, P]], channel_multiplier=1))
            const(g.memset(maskB[HG_CHUNK:P, 0:HG_CHUNK], 0.0))
            const(g.affine_select(out=below[:, :], in_=ones[:, :], compare_op=ALU.is_gt, fill=0.0, base=0,
                            pattern=[[1, P]], channel_multiplier=-1))
            link(g.iota(dist[:, :, :], pattern=[[-P, TT], [1, TOK]], base=0, channel_multiplier=-1,
                        allow_small_or_imprecise_dtypes=True))
            link(g.affine_select(out=dist[:, :, :], in_=dist[:, :, :], compare_op=ALU.is_ge, fill=FAR,
                                 base=WINDOW, pattern=[[P, TT], [-1, TOK]], channel_multiplier=1))
            const(g.affine_select(out=dist[:, :, :], in_=dist[:, :, :], compare_op=ALU.is_ge, fill=-FAR,
                            base=WINDOW, pattern=[[-P, TT], [1, TOK]],
                            channel_multiplier=-1))
            const(g.iota(iota_s[:, :, :], pattern=[[0, 2], [1, SLOTS]], base=0, channel_multiplier=0,
                   allow_small_or_imprecise_dtypes=True))
            const(g.iota(part[:, :], pattern=[[0, 1]], base=0, channel_multiplier=1,
                   allow_small_or_imprecise_dtypes=True))
            const(g.memset(esel[:, :], 0.0))
            const(g.memset(putT[:, :], 0.0))
            pool.wait_ge(s["proj_done"], GI["kv"] + 1)
            zero, _ = counted(pool, s["zeroed"])
            zero(g.memset(kpad, 0.0))
            zero(g.memset(bup, 0.0))
            zero(g.memset(ysb, 0.0))

        CONSTS = 12

        @block.scalar
        def _(act):
            a = nc.scalar
            link, astate = counted(act, s["act_step"])
            for i, v in enumerate((emb_ln_g, emb_ln_b)):
                act.dma_start(lnp[:, i, :], v.partition_broadcast(P)).then_inc(s["emb_in"], 16)
            act.dma_start(lbrow[:, :], hgrn_lb_logits.rearrange("d i (h p) -> (d i h) p", p=P)).then_inc(s["par_in"], 16)
            act.dma_start(sink[:, :], attn_sink[0].partition_broadcast(P)).then_inc(s["par_in"], 16)
            act.dma_start(normg[:, :], hgrn_norm_g[0].partition_broadcast(P)).then_inc(s["par_in"], 16)
            act.dma_start(wr[:, :, :], w_router[0].rearrange("(k p) n -> p k n", p=P)).then_inc(s["par_in"], 16)
            act.dma_start(br[:, :], b_router[0].partition_broadcast(P)).then_inc(s["par_in"], 16)

            def ln_std(n):
                act.wait_ge(s["var_ready"], n)
                a.activation(rstd[:, :], mv[:, :, 1], ACT.Sqrt, bias=epsc[:, 0:1]).then_inc(s["std_ready"], 1)

            act.wait_ge(s["consts"], CONSTS)
            ln_std(1)
            for i in (1, 3):
                act.wait_ge(s["hT_ps"], i + 1)
                a.copy(hT[:, 2 * i:2 * i + 2, :].rearrange("p k n -> p (k n)"), bank[i][:, :]).then_inc(s["hT_ready"], 1)
            act.wait_ge(s["lbm_ready"], 1)
            a.activation(lbe[:, :, :, :], lbe[:, :, :, :], ACT.Exp).then_inc(s["lb_exp"], 1)

            def gate(d):
                act.wait_ge(s["proj_done"], d + 1)
                for i in range(2):
                    ins = a.activation(hg[d]["k"][:, i * 512:(i + 1) * 512], bank[2 * d + i][:, :], ACT.Sigmoid)
                    if i == 0:
                        link(ins)
                    else:
                        ins.then_inc(proj_read[d], 1)

            def exps(d):
                act.wait_ge(s["logf_ready"], d + 1)
                a.activation(hg[d]["C"], hg[d]["qe"], ACT.Ln).then_inc(s["logf_in"], 1)
                act.wait_ge(s["exps_in"], 2 * d + 1)
                a.activation(hg[d]["qrel"], hg[d]["A"], ACT.Exp).then_inc(s["k_ready"], 1)
                a.activation(hg[d]["krel"], hg[d]["A"], ACT.Exp, scale=-1.0).then_inc(s["k_ready"], 1)
                act.wait_ge(s["exps_in"], 2 * d + 2)
                a.activation(hg[d]["kp"], hg[d]["Dl"], ACT.Exp).then_inc(s["k_ready"], 1)
                a.activation(hg[d]["qe"], hg[d]["C"], ACT.Exp).then_inc(s["k_ready"], 1)

            gate(0)
            exps(0)
            gate(1)
            exps(1)
            act.wait_ge(s["proj_done"], GI["ih"] + 1)
            link(a.copy(ih[:, 0, :], bank[6][:, :]))
            a.copy(ih[:, 1, :], bank[7][:, :]).then_inc(proj_read[GI["ih"]], 1)
            act.wait_ge(s["proj_done"], GI["qa"] + 1)
            link(a.copy(qaT[:, 0:2, :].rearrange("p k n -> p (k n)"), bank[0][:, :]))
            a.copy(qaT[:, 2:4, :].rearrange("p k n -> p (k n)"), bank[1][:, :]).then_inc(proj_read[GI["qa"]], 1)
            act.wait_ge(s["proj_done"], GI["zg"] + 1)
            link(a.activation(gz[:, 0, :], bank[4][:, :], ACT.Sigmoid))
            a.activation(gz[:, 1, :], bank[5][:, :], ACT.Sigmoid).then_inc(s["zg_sig"], 1)

            for j, (kind, d, t) in enumerate(jobs):
                if kind == "kpT":
                    act.wait_ge(s["job_done"], j + 1)
                    a.copy(hg[d]["Dl"].rearrange("p (t n) -> p t n", t=TT)[:, t, :], bank[j % 4][:, :]).then_inc(job_read[j % 4], 1)

            def probs(b):
                act.wait_ge(s["mx_ready"], b + 1)
                for j in range(QPG):
                    sc = score[b % 2][:, j * TOK:(j + 1) * TOK]
                    link(a.activation(sc, sc, ACT.Exp, bias=nm[:, b % 2, j:j + 1], scale=DH ** -0.5,
                                      accum_out=den[:, b % 2, j:j + 1]))
                a.activation(es[:, b % 2, :], es[:, b % 2, :], ACT.Exp).then_inc(s["prob_ready"], 1)

            def probs_turned(b):
                if b >= 2:
                    act.wait_ge(s["attn_done"], b - 1)
                for h in range(2):
                    j = J["pT", b, h]
                    act.wait_ge(s["job_done"], j + 1)
                    a.copy(probT[b % 2][:, h * 512:(h + 1) * 512], bank[j % 4][:, :]).then_inc(job_read[j % 4], 1)

            probs(0)
            for b in range(len(BATCH)):
                if b + 1 < len(BATCH):
                    probs(b + 1)
                probs_turned(b)

            for t in range(TT):
                act.wait_ge(s["hgrn_done"], t + 1)
                for h in range(NH):
                    ins = a.activation(hg[0]["k"][:, h * P:(h + 1) * P], bank[6 + t][:, h * P:(h + 1) * P], ACT.Square,
                                       accum_out=ssq[:, t, h:h + 1])
                    if h < NH - 1 or t < TT - 1:
                        link(ins)
                if t == TT - 1:
                    ins.then_inc(s["rms_in"], 1)
            act.wait_ge(s["rms_in"], 1)
            a.activation(rr[:, :, :], ssq[:, :, :], ACT.Sqrt, bias=epsc[:, 1:2], scale=1.0 / P).then_inc(s["rms_std"], 1)

            def turned(kind, dst):
                for i in (1, 3):
                    j = J[kind, i, 0]
                    act.wait_ge(s["job_done"], j + 1)
                    a.copy(dst[:, 2 * i:2 * i + 2, :].rearrange("p k n -> p (k n)"), bank[j % 4][:, :]).then_inc(job_read[j % 4], 1)

            turned("catT", hT)
            ln_std(2)
            turned("x1T", hT)
            act.wait_ge(s["top_ready"], 1)
            link(a.activation(g4[:, 0, :], m8[:, 0, 0:TOPK], ACT.Exp, bias=nm0[:, 0:1], accum_out=gs[:, 0:1]))
            a.activation(g4[:, 1, :], m8[:, 1, 0:TOPK], ACT.Exp, bias=nm0[:, 1:2], accum_out=gs[:, 1:2]).then_inc(s["g4_ready"], 1)

            act.wait_ge(s["gath_done"], 1)
            a.copy(xT, bank[0][:, :].rearrange("p (k s) -> p k s", k=KT)).then_inc(s["xT_ready"], 1)
            act.wait_ge(s["plan_ready"], 2)
            act.wait_ge(s["bias_in"], 32)
            act.sem_inc(s["put_ready"], 1)
            act.sem_inc(s["y_ready"], 2)
            npass = act.value_load(plan[0:1, NPASS:NPASS + 1], min_val=NE, max_val=NPASS - 1)
            with act.Fori(0, npass) as p:
                for n in range(2):
                    act.wait_ge(s["glu_ready"], 2 * p + n + 1)
                    w = slice(n * 256, n * 256 + 256)
                    a.activation(sig[:, w], glu[:, w], ACT.Sigmoid, scale=SIG_ALPHA).then_inc(s["sig_ready"], 1)
                act.wait_ge(s["put_ps"], p + 2)
                a.copy(putT[:, :], bank[2][:, 0:TOK]).then_inc(s["put_ready"], 1)
                act.wait_ge(s["actT_ps"], p + 1)
                a.copy(actT, bank[3][:, :]).then_inc(s["actT_ready"], 1)
                act.wait_ge(s["gath_done"], p + 2)
                a.copy(xT, bank[0][:, :].rearrange("p (k s) -> p k s", k=KT)).then_inc(s["xT_ready"], 1)
                act.wait_ge(s["chunk_used"], (p + 1) * CHUNKS)
                for n in range(2):
                    a.copy(ysb[:, n * 512:(n + 1) * 512], bank[2 + n][:, :]).then_inc(s["y_ready"], 1)
            ln_std(3)

        @block.vector
        def _(dve):
            v = nc.vector
            link, vstate = counted(dve, s["dve_step"])

            def norm_stats(src, n, link=link):
                for t in range(TT):
                    for h in range(2):
                        link(v.bn_stats(st[:, t, h, :], src[:, t, h * 512:(h + 1) * 512]))
                for t in range(TT):
                    ins = v.bn_aggr(mv[:, t, :], st[:, t, :, :])
                    if t < TT - 1:
                        link(ins)
                ins.then_inc(s["var_ready"], 1)
                dve.wait_ge(s["std_ready"], n)
                link(v.reciprocal(rstd[:, :], rstd[:, :]))

            def norm_apply(dst, params, count, ready, link=link):
                dve.wait_ge(s[params], count)
                for t in range(TT):
                    link(v.scalar_tensor_tensor(out=dst[:, t, :], in0=dst[:, t, :], scalar=mv[:, t, 0:1],
                                                in1=lnp[:, 0, :], op0=ALU.subtract, op1=ALU.mult))
                    v.scalar_tensor_tensor(out=dst[:, t, :], in0=dst[:, t, :], scalar=rstd[:, t:t + 1],
                                           in1=lnp[:, 1, :], op0=ALU.mult, op1=ALU.add).then_inc(s[ready], 1)

            dve.wait_ge(s["x_in"], 16)
            norm_stats(X, 1)
            norm_apply(X, "emb_in", 32, "h_ready")
            dve.wait_ge(s["consts"], CONSTS)
            link(v.scalar_tensor_tensor(out=dist[:, :, :], in0=dist[:, :, :], scalar=-1.0, in1=dist[:, :, :],
                                        op0=ALU.mult, op1=ALU.min))
            dve.wait_ge(s["lb_ps"], 1)
            link(v.tensor_copy(lbt[:, :, :, :], bank[7][:, 0:16].rearrange("p (d i h) -> p d i h", d=2, i=2)))
            link(v.tensor_tensor(lbs[:, :, :], lbt[:, :, 0, :], lbt[:, :, 1, :], ALU.max))
            v.tensor_tensor(lbe[:, :, :, :], lbt[:, :, :, :],
                            lbs[:, :, :].unsqueeze(2).broadcast_to([P, 2, 2, NH]), ALU.subtract).then_inc(s["lbm_ready"], 1)
            for i in (0, 2):
                dve.wait_ge(s["hT_ps"], i + 1)
                v.tensor_copy(hT[:, 2 * i:2 * i + 2, :].rearrange("p k n -> p (k n)"), bank[i][:, :]).then_inc(s["hT_ready"], 1)
            dve.wait_ge(s["lb_exp"], 1)
            link(v.tensor_tensor(lbs[:, :, :], lbe[:, :, 0, :], lbe[:, :, 1, :], ALU.add))
            link(v.reciprocal(lbs[:, :, :], lbs[:, :, :]))
            link(v.tensor_tensor(lb[:, :, :], lbe[:, :, 0, :], lbs[:, :, :], ALU.mult))
            link(v.tensor_scalar(oml[:, :, :], lb[:, :, :], -1.0, 1.0, ALU.mult, ALU.add))

            def hseq(ap):
                return ap.rearrange("p (h n) -> p h n", h=NH)

            def cseq(ap):
                return ap.rearrange("p (c n) -> p c n", n=HG_CHUNK)

            def gates(d):
                dve.wait_ge(proj_read[d], 1)
                B = hg[d]
                for h in range(NH):
                    link(v.tensor_scalar(hseq(B["qe"])[:, h, :], hseq(B["k"])[:, h, :], oml[:, d, h:h + 1],
                                         lb[:, d, h:h + 1], ALU.mult, ALU.add))
                v.tensor_scalar(B["k"], B["qe"], -1.0, 1.0, ALU.mult, ALU.add).then_inc(s["logf_ready"], 1)
                dve.wait_ge(s["logf_ready"], d + 1)

            def rescaled(d):
                B = hg[d]
                dve.wait_ge(s["logf_in"], d + 1)
                if d == 0:
                    link(v.tensor_tensor_scan(B["C"], scanm, B["C"], 0.0, ALU.mult, ALU.add))
                else:
                    link(v.tensor_tensor_scan(B["C"][:, ::-1], scanm, B["C"][:, ::-1], 0.0, ALU.mult, ALU.add))
                last, ref = (HG_CHUNK - 1, HG_CHUNK // 2) if d == 0 else (0, HG_CHUNK - 1 - HG_CHUNK // 2)
                C3 = cseq(B["C"])
                shape = [P, NH * NC, HG_CHUNK]
                v.tensor_tensor(cseq(B["A"]), C3, C3[:, :, ref:ref + 1].broadcast_to(shape),
                                ALU.subtract).then_inc(s["exps_in"], 1)
                v.tensor_tensor(cseq(B["Dl"]), C3[:, :, last:last + 1].broadcast_to(shape), C3,
                                ALU.subtract).then_inc(s["exps_in"], 1)

            def scaled(d):
                B = hg[d]
                dve.wait_ge(s["k_ready"], 4 * d + 4)
                if d == 0:
                    dve.wait_ge(s["proj_done"], GI["qh"] + 1)
                    link(v.tensor_copy(qhT[:, 0:512], bank[4][:, :]))
                    v.tensor_copy(qhT[:, 512:1024], bank[5][:, :]).then_inc(proj_read[GI["qh"]], 1)
                    dve.wait_ge(proj_read[GI["qh"]], 1)
                last = HG_CHUNK - 1 if d == 0 else 0
                link(v.tensor_copy(decay[:, d, :], cseq(B["qe"])[:, :, last]))
                v.tensor_tensor(B["qrel"], B["qrel"], qhT[:, :], ALU.mult).then_inc(s["kpT_ready"], 1)
                v.tensor_tensor(B["krel"], B["krel"], B["k"], ALU.mult).then_inc(s["kpT_ready"], 1)
                v.tensor_tensor(B["kp"], B["kp"], B["k"], ALU.mult).then_inc(s["kpT_ready"], 1)
                v.tensor_tensor(B["qe"], B["qe"], qhT[:, :], ALU.mult).then_inc(s["kpT_ready"], 1)

            gates(0)
            rescaled(0)
            gates(1)
            scaled(0)
            rescaled(1)
            scaled(1)
            for d in range(2):
                link(v.memset(hg[d]["A"], 0.0))
            dve.wait_ge(s["proj_done"], GI["kv"] + 1)
            dve.wait_ge(s["zeroed"], 1)
            for g in range(NG):
                for o in range(2):
                    r = slice(o * DH, (o + 1) * DH)
                    link(v.tensor_copy(kpad[r, g, o, :], bank[2][r, g * TOK:(g + 1) * TOK]))
            v.tensor_copy(va[:, :, :], bank[3][:, 0:TOK].rearrange("p (t n) -> p t n", t=TT)).then_inc(proj_read[GI["kv"]], 1)
            dve.wait_ge(s["par_in"], 80)
            dve.wait_ge(s["zg_sig"], 1)
            for t in range(TT):
                link(v.tensor_tensor(gz[:, t, :], gz[:, t, :], bank[4 + t][:, :], ALU.mult))
            for t in range(TT):
                ins = v.tensor_tensor(gz[:, t, :], gz[:, t, :], normg[:, :], ALU.mult)
                if t == 0:
                    link(ins)
            ins.then_inc(proj_read[GI["zg"]], 1)

            for j, (kind, d, i) in enumerate(jobs):
                if kind == "aT":
                    dve.wait_ge(s["job_done"], j + 1)
                    mask = (maskF, maskB)[d]
                    v.copy_predicated(hg[d]["A"].rearrange("p (t h n) -> p t h n", t=TT, h=NH)[:, i, :, :],
                                      mask[:, :].bitcast(I32).unsqueeze(1).broadcast_to([P, NH, P]),
                                      bank[j % 4][:, :].rearrange("p (h n) -> p h n", h=NH)).then_inc(job_read[j % 4], 1)
                if kind == "kv":
                    dve.wait_ge(s["job_done"], j + 1)
                    c = chunk_of(d, i)
                    if i == 0:
                        ins = v.tensor_copy(S(d, 0), bank[j % 4][:, :])
                    else:
                        for h in range(NH):
                            ins = (v.scalar_tensor_tensor(
                                out=S(d, i)[:, h * P:(h + 1) * P], in0=S(d, i - 1)[:, h * P:(h + 1) * P],
                                scalar=decay[:, d, h * NC + c:h * NC + c + 1], in1=bank[j % 4][:, h * P:(h + 1) * P],
                                op0=ALU.mult, op1=ALU.add))
                    ins.then_inc(job_read[j % 4], 1)
                    dve.wait_ge(job_read[j % 4], j // 4 + 1)

            def scores(b):
                t, g = BATCH[b]
                for h in range(2):
                    j = J["score", b, h]
                    dve.wait_ge(s["job_done"], j + 1)
                    if h == 0 and b >= 2:
                        dve.wait_ge(s["job_done"], J["pT", b - 2, 1] + 1)
                    for q in range(2):
                        head = g * QPG + 2 * h + q
                        slope = 2.0 ** (-8.0 * (head + 1) / HQ)
                        ins = v.scalar_tensor_tensor(
                            out=score[b % 2][:, (2 * h + q) * TOK:(2 * h + q + 1) * TOK], in0=dist[:, t, :],
                            scalar=slope * DH ** 0.5, in1=bank[j % 4][:, q * TOK:(q + 1) * TOK], op0=ALU.mult, op1=ALU.add)
                        if q == 0:
                            link(ins)
                    ins.then_inc(job_read[j % 4], 1)
                    dve.wait_ge(job_read[j % 4], j // 4 + 1)
                link(v.tensor_reduce(mx[:, :], score[b % 2].rearrange("p (j n) -> p j n", j=QPG), AX_X, ALU.max))
                link(v.scalar_tensor_tensor(out=mx[:, :], in0=mx[:, :], scalar=DH ** -0.5,
                                            in1=sink[:, g * QPG:(g + 1) * QPG], op0=ALU.mult, op1=ALU.max))
                link(v.tensor_tensor(es[:, b % 2, :], sink[:, g * QPG:(g + 1) * QPG], mx[:, :], ALU.subtract))
                v.tensor_scalar(nm[:, b % 2, :], mx[:, :], -1.0, None, ALU.mult).then_inc(s["mx_ready"], 1)

            def mixed(b):
                t, g = BATCH[b]
                dve.wait_ge(s["prob_ready"], b + 1)
                link(v.tensor_tensor(den[:, b % 2, :], den[:, b % 2, :], es[:, b % 2, :], ALU.add))
                link(v.reciprocal(rden[:, b % 2, :], den[:, b % 2, :]))
                dve.wait_ge(s["attn_done"], b + 1)
                w = slice(g * QPG * DH, (g + 1) * QPG * DH)
                v.tensor_tensor(cat[:, t, w].rearrange("p (j n) -> p j n", j=QPG),
                                bank[4 + b % 2][:, w].rearrange("p (j n) -> p j n", j=QPG),
                                rden[:, b % 2, :].unsqueeze(2).broadcast_to([P, QPG, DH]), ALU.mult).then_inc(s["attn_cat"], 1)

            scores(0)
            for b in range(len(BATCH)):
                if b + 1 < len(BATCH):
                    scores(b + 1)
                mixed(b)

            dve.wait_ge(s["rms_std"], 1)
            link(v.reciprocal(rr[:, :, :], rr[:, :, :]))
            for t in range(TT):
                for h in range(NH):
                    ins = v.scalar_tensor_tensor(
                        out=cat[:, t, HQ * DH + h * P:HQ * DH + (h + 1) * P], in0=bank[6 + t][:, h * P:(h + 1) * P],
                        scalar=rr[:, t, h:h + 1], in1=gz[:, t, h * P:(h + 1) * P], op0=ALU.mult, op1=ALU.mult)
                    if h < NH - 1:
                        link(ins)
                ins.then_inc(s["rec_cat"], 1)

            def turned(kind, dst):
                for i in (0, 2):
                    j = J[kind, i, 0]
                    dve.wait_ge(s["job_done"], j + 1)
                    v.tensor_copy(dst[:, 2 * i:2 * i + 2, :].rearrange("p k n -> p (k n)"),
                                  bank[j % 4][:, :]).then_inc(job_read[j % 4], 1)

            turned("catT", hT)
            for t in range(TT):
                for n in range(2):
                    dve.wait_ge(s["mix_done"], 2 * t + n + 1)
                    w = slice(n * 512, n * 512 + 512)
                    link(v.scalar_tensor_tensor(out=X[:, t, w], in0=X[:, t, w], scalar=DEEP_ALPHA,
                                                in1=bank[4 + 2 * t + n][:, :], op0=ALU.mult, op1=ALU.add))
            norm_stats(X, 2)
            norm_apply(X, "ln1_in", 32, "x1_ready")
            turned("x1T", hT)

            dve.wait_ge(s["logit_done"], 1)
            for t in range(TT):
                link(v.tensor_tensor(lg[:, t, :], bank[4][:, t * NE:(t + 1) * NE], br[:, :], ALU.add))
                link(v.max(m8[:, t, :], lg[:, t, :]))
                link(v.max_index(i8[:, t, :], m8[:, t, :], lg[:, t, :]))
            link(v.tensor_copy(i8f[:, :, :], i8[:, :, :]))
            v.tensor_scalar(nm0[:, :], m8[:, :, 0], -1.0, None, ALU.mult).then_inc(s["top_ready"], 1)
            dve.wait_ge(s["g4_ready"], 1)
            link(v.reciprocal(gs[:, :], gs[:, :]))
            link(v.tensor_tensor(g4[:, :, :], g4[:, :, :], gs[:, :].unsqueeze(2).broadcast_to([P, TT, TOPK]), ALU.mult))
            for t in range(TT):
                for j in range(TOPK):
                    link(v.tensor_scalar(tmp4[:, t, 0, j, :], iota_s[:, 0, 0:NE], i8f[:, t, j:j + 1], None, ALU.is_equal))
                    link(v.tensor_scalar(tmp4[:, t, 1, j, :], iota_s[:, 0, 0:NE], i8f[:, t, j:j + 1],
                                         g4[:, t, j:j + 1], ALU.is_equal, ALU.mult))
            for t in range(TT):
                ins = v.tensor_reduce(gm[:, t, :, :], tmp4[:, t, :, :, :].rearrange("p m j e -> p m e j"), AX_X, ALU.add)
                if t == 0:
                    link(ins)
            ins.then_inc(s["mask_ready"], 1)
            dve.wait_ge(s["mask_ready"], 1)
            dve.wait_ge(s["rank_done"], 1)
            link(v.scalar_tensor_tensor(out=key[:, :, :], in0=bank[5][:, 0:TT * NE].rearrange("p (t e) -> p t e", t=TT),
                                        scalar=NOT_HERE, in1=gm[:, :, 0, :], op0=ALU.add, op1=ALU.mult))
            v.tensor_scalar(key[:, :, :], key[:, :, :], -NOT_HERE, None, ALU.add).then_inc(s["key_ready"], 1)
            link(v.tensor_copy(cnt[:, 0:1], bank[6][0:NE, 0:1]))
            for i in range(1, TOK // SLOTS):
                link(v.tensor_scalar(cnt[:, i:i + 1], cnt[:, 0:1], float(SLOTS * i + 1), None, ALU.is_ge))
            v.tensor_reduce(cnt[:, 4:5], cnt[:, 1:4], AX_X, ALU.add).then_inc(s["ex_ready"], 1)
            dve.wait_ge(s["route_done"], 1)
            link(v.tensor_scalar(cnt[:, 5:6], bank[6][0:NE, 1:2], float(NE), None, ALU.add))
            link(v.tensor_scalar(dlt[:, 0, :], iota_s[0:NE, 0, 0:NPASS], cnt[:, 5:6], None, ALU.subtract))
            link(v.tensor_scalar(dlt[:, 1, :], dlt[:, 0, :], 0.0, None, ALU.is_ge))
            link(v.scalar_tensor_tensor(out=dlt[:, 2, :], in0=dlt[:, 0, :], scalar=cnt[:, 4:5], in1=dlt[:, 1, :],
                                        op0=ALU.is_lt, op1=ALU.mult))
            link(v.tensor_scalar(dlt[:, 0, :], dlt[:, 0, :], 1.0, -float(SLOTS), ALU.add, ALU.mult))
            link(v.tensor_tensor(base[:, :], dlt[:, 0, :], dlt[:, 2, :], ALU.mult))
            link(v.tensor_copy(esel[0:NE, NE:NPASS], dlt[:, 2, NE:NPASS]))
            link(v.tensor_copy(esel[0:NE, 0:NE], ident[0:NE, 0:NE]))
            link(v.tensor_copy(keyT, bank[7][0:NE, 0:TOK]))
            v.tensor_copy(putT[0:NE, :], bank[7][0:NE, TOK:2 * TOK]).then_inc(s["sel_ready"], 1)
            dve.wait_ge(s["plan_ps"], 1)
            link(v.tensor_copy(keyp[:, :, :], bank[5][:, 128:128 + TT * NPASS].rearrange("p (t n) -> p t n", t=TT)))
            link(v.tensor_copy(gatep[:, :, :], bank[5][:, 256:256 + TT * NPASS].rearrange("p (t n) -> p t n", t=TT)))
            v.tensor_copy(plan[0:1, 0:NPASS], bank[6][0:1, 8:8 + NPASS]).then_inc(s["plan_ready"], 1)
            v.tensor_scalar(plan[0:1, NPASS:NPASS + 1], bank[6][0:1, 8 + NPASS:9 + NPASS], float(NE), None,
                            ALU.add).then_inc(s["plan_ready"], 1)

            def picks(col):
                for t in range(TT):
                    v.tensor_scalar(pick[:, t, :], iota_s[:, 0, :], keyp[:, t, col], None, ALU.is_equal).then_inc(s["picked"], 1)
                v.tensor_copy(bsel[:, :], esel[:, col].broadcast_to([P, SLOTS])).then_inc(s["picked"], 1)

            picks(slice(0, 1))
            for t in range(TT):
                ins = v.tensor_scalar(acc[:, t, :], X[:, t, :], DEEP_ALPHA, None, ALU.mult)
                if t == 0:
                    link(ins)
            ins.then_inc(s["scat_read"], 1)
            dve.wait_ge(s["plan_ready"], 2)
            npass = dve.value_load(plan[0:1, NPASS:NPASS + 1], min_val=NE, max_val=NPASS - 1)

            def scattered(n0):
                dve.wait_ge(s["scat_read"], n0 + 1)
                for q in range(4):
                    dve.wait_ge(s["scat_done"], n0 + q + 1)
                    w = slice((q % 2) * 512, (q % 2) * 512 + 512)
                    v.tensor_tensor(acc[:, q // 2, w], acc[:, q // 2, w], bank[4 + q][:, :], ALU.add).then_inc(s["scat_read"], 1)

            done = vstate["n"]
            with dve.Fori(0, npass) as p:
                dve.wait_ge(s["put_ps"], p + 1)
                for t in range(TT):
                    v.tensor_scalar(gpick[:, t, :], iota_s[:, :, :].rearrange("p a n -> p (a n)"),
                                    keyp[:, t, bass.ds(p, 1)], gatep[:, t, bass.ds(p, 1)],
                                    ALU.is_equal, ALU.mult).then_inc(s["picked"], 1)
                dve.wait_ge(s["gath_done"], p + 1)
                dve.wait_ge(s["chunk_used"], p * CHUNKS + 1)
                picks(bass.ds(p + 1, 1))
                for n in range(2):
                    dve.wait_ge(s["chunk_used"], p * CHUNKS + UPC)
                    pair = bank[n][:, :].rearrange("p (f two) -> p f two", two=2)
                    w = slice(n * 256, n * 256 + 256)
                    v.tensor_scalar(glu[:, w], pair[:, :, 0], LIMIT, None, ALU.min).then_inc(s["glu_ready"], 1)
                    v.tensor_scalar(lin[:, w], pair[:, :, 1], LIMIT, -LIMIT, ALU.min, ALU.max).then_inc(s["dve_step"], 1)
                for n in range(2):
                    w = slice(n * 256, n * 256 + 256)
                    dve.wait_ge(s["dve_step"], done + 4 * p + 2 + n)
                    dve.wait_ge(s["glu_ready"], 2 * p + n + 1)
                    v.scalar_tensor_tensor(out=lin[:, w], in0=lin[:, w], scalar=1.0, in1=glu[:, w],
                                           op0=ALU.add, op1=ALU.mult).then_inc(s["dve_step"], 1)
                    dve.wait_ge(s["dve_step"], done + 4 * p + 3 + n)
                    dve.wait_ge(s["sig_ready"], 2 * p + n + 1)
                    v.tensor_tensor(act_[:, w], lin[:, w], sig[:, w], ALU.mult).then_inc(s["act_ready"], 1)
                scattered(4 * p)
            scattered(4 * npass)
            dve.wait_ge(s["scat_read"], 4 * npass + 5)
            link, _ = counted(dve, s["tail_step"])
            norm_stats(acc, 3, link)
            norm_apply(acc, "ln2_in", 32, "acc_ready", link)

        @block.tensor
        def _(pe):
            mm = nc.tensor.matmul
            tr = nc.tensor.transpose
            pe.wait_ge(s["consts"], CONSTS)
            pe.wait_ge(s["par_in"], 80)
            tr(bank[7][:, 0:16], lbrow[:, :], ident[0:16, 0:16]).then_inc(s["lb_ps"], 1)

            def turn(src, i, b):
                for k in range(2):
                    for t in range(TT):
                        ins = tr(bank[b][:, k * TOK + t * P:k * TOK + (t + 1) * P],
                                 src[:, t, (2 * i + k) * P:(2 * i + k + 1) * P], ident[:, :])
                return ins

            pe.wait_ge(s["h_ready"], TT)
            for i in range(4):
                turn(X, i, i).then_inc(s["hT_ps"], 1)
            pe.wait_ge(s["hT_ready"], 4)

            for g, (name, _, w) in enumerate(GROUPS):
                pe.wait_ge(win_in[g % WBUF], 16 * (g // WBUF + 1))
                b0 = 2 * (g % 4)
                if g == 3:
                    pe.wait_ge(s["lbm_ready"], 1)
                if g >= 4:
                    pe.wait_ge(proj_read[g - 4], 1)
                wv = wbuf[:, g % WBUF, 0:KT * w].rearrange("p (k n) -> p k n", k=KT)
                if name in ("zf0", "zf1", "qh", "qa"):
                    for c in range(4):
                        for k in range(KT):
                            lhs = wv[:, k, c * P:(c + 1) * P]
                            ins = mm(bank[b0 + c // 2][:, (c % 2) * TOK:(c % 2 + 1) * TOK], lhs, hT[:, k, :],
                                     start=(k == 0), stop=(k == KT - 1))
                elif name == "kv":
                    for gr in range(NG):
                        for k in range(KT):
                            for o in range(2):
                                mm(bank[b0][o * DH:(o + 1) * DH, gr * TOK:(gr + 1) * TOK], wv[:, k, gr * DH:(gr + 1) * DH],
                                   hT[:, k, :], start=(k == 0), stop=(k == KT - 1))
                    for t in range(TT):
                        for k in range(KT):
                            ins = mm(bank[b0 + 1][:, t * P:(t + 1) * P], hT[:, k, t * P:(t + 1) * P], wv[:, k, P:2 * P],
                                     start=(k == 0), stop=(k == KT - 1))
                else:
                    for t in range(TT):
                        for k in range(KT):
                            ins = mm(bank[b0 + t][:, :], hT[:, k, t * P:(t + 1) * P], wv[:, k, :],
                                     start=(k == 0), stop=(k == KT - 1))
                ins.then_inc(s["proj_done"], 1)

            def attn_out(b):
                t, g = BATCH[b]
                pe.wait_ge(proj_read[GI["zg"]], 1)
                if b >= 2:
                    pe.wait_ge(s["attn_cat"], b - 1)
                for h in range(2):
                    j = J["pT", b, h]
                    pe.wait_ge(job_read[j % 4], j // 4 + 1)
                for q in range(QPG):
                    head = g * QPG + q
                    for kt in range(TT):
                        ins = mm(bank[4 + b % 2][:, head * DH:(head + 1) * DH],
                                 probT[b % 2][:, q * TOK + kt * P:q * TOK + (kt + 1) * P],
                                 va[:, kt, g * DH:(g + 1) * DH], start=(kt == 0), stop=(kt == TT - 1))
                ins.then_inc(s["attn_done"], 1)

            def hgrn_out():
                for kd in range(2):
                    for t in range(TT):
                        for kind in ("kpT", "aT"):
                            j = J[kind, kd, t]
                            pe.wait_ge(job_read[j % 4], j // 4 + 1)
                for j in (J["kv", 0, NC - 2], J["kv", 1, NC - 2]):
                    pe.wait_ge(job_read[j % 4], j // 4 + 1)
                for t in range(TT):
                    for h in range(NH):
                        w = slice(h * P, (h + 1) * P)
                        o = bank[6 + t]
                        aT = [hg[d]["A"].rearrange("p (t h n) -> p t h n", t=TT, h=NH)[:, t, h, :] for d in range(2)]
                        mm(o[:, w], aT[0], ih[:, t, w], start=True, stop=False)
                        parts = [(d, i) for d in range(2) for i in range(1, NC) if chunk_of(d, i) // 2 == t]
                        for d, i in parts:
                            c = chunk_of(d, i)
                            r = slice(HG_CHUNK * (c % 2), HG_CHUNK * (c % 2) + HG_CHUNK)
                            mm(o[r, w], hg[d]["qe"][:, h * TOK + c * HG_CHUNK:h * TOK + (c + 1) * HG_CHUNK],
                               S(d, i - 1)[:, w], start=False, stop=False)
                        ins = mm(o[:, w], aT[1], ih[:, t, w], start=False, stop=True)
                    ins.then_inc(s["hgrn_done"], 1)

            for g in range(len(GROUPS) - 1):
                pe.wait_ge(proj_read[g], 1)
            for j, (kind, d, i) in enumerate(jobs):
                b = j % 4
                if kind == "x1T" and d == 0:
                    pe.wait_ge(s["x1_ready"], TT)
                if kind == "catT" and d == 0:
                    pe.wait_ge(s["attn_cat"], len(BATCH))
                    pe.wait_ge(s["rec_cat"], TT)
                if j >= 4:
                    pe.wait_ge(job_read[b], j // 4)
                if kind == "kpT":
                    pe.wait_ge(s["kpT_ready"], 4 * d + 4)
                    for h in range(NH):
                        ins = tr(bank[b][:, h * P:(h + 1) * P], hg[d]["kp"][:, h * TOK + i * P:h * TOK + (i + 1) * P], ident[:, :])
                elif kind == "aT":
                    for h in range(NH):
                        w = slice(h * TOK + i * P, h * TOK + (i + 1) * P)
                        ins = mm(bank[b][:, h * P:(h + 1) * P], hg[d]["krel"][:, w], hg[d]["qrel"][:, w], start=True, stop=True)
                elif kind == "kv":
                    c = chunk_of(d, i)
                    jk = J["kpT", d, c // 2]
                    pe.wait_ge(job_read[jk % 4], jk // 4 + 1)
                    r = slice(HG_CHUNK * (c % 2), HG_CHUNK * (c % 2) + HG_CHUNK)
                    kpt = hg[d]["Dl"].rearrange("p (t n) -> p t n", t=TT)
                    for h in range(NH):
                        w = slice(h * P, (h + 1) * P)
                        ins = mm(bank[b][:, w], kpt[r, c // 2, w], ih[r, c // 2, w], start=True, stop=True)
                elif kind == "score":
                    t, g = BATCH[d]
                    for q in range(2):
                        head = g * QPG + 2 * i + q
                        ins = mm(bank[b][:, q * TOK:(q + 1) * TOK], qaT[:, head // 2, t * P:(t + 1) * P], kpad[:, g, head % 2, :],
                                 start=True, stop=True)
                elif kind == "pT":
                    pe.wait_ge(s["prob_ready"], d + 1)
                    for q in range(2):
                        for kt in range(TT):
                            src = score[d % 2][:, (2 * i + q) * TOK + kt * P:(2 * i + q) * TOK + (kt + 1) * P]
                            ins = tr(bank[b][:, q * TOK + kt * P:q * TOK + (kt + 1) * P], src, ident[:, :])
                elif kind == "catT":
                    ins = turn(cat, d, b)
                elif kind == "x1T":
                    ins = turn(X, d, b)
                ins.then_inc(s["job_done"], 1)
                if kind == "kv" and (d, i) == (1, NC - 2):
                    hgrn_out()
                if kind == "pT" and i == 1:
                    attn_out(d)
                if kind == "catT" and d == 3:
                    for q in range(4):
                        jj = J["catT", q, 0]
                        pe.wait_ge(job_read[jj % 4], jj // 4 + 1)
                    pe.wait_ge(s["wout_in"], 32)
                    for t in range(TT):
                        for n in range(2):
                            for k in range(KT):
                                wv = wbuf[:, 1 - k // 4, (k % 4) * D + n * 512:(k % 4) * D + (n + 1) * 512]
                                ins = mm(bank[4 + 2 * t + n][:, :], hT[:, k, t * P:(t + 1) * P], wv,
                                         start=(k == 0), stop=(k == KT - 1))
                            ins.then_inc(s["mix_done"], 1)

            for q in range(4):
                jj = J["x1T", q, 0]
                pe.wait_ge(job_read[jj % 4], jj // 4 + 1)
            for t in range(TT):
                for k in range(KT):
                    ins = mm(bank[4][:, t * NE:(t + 1) * NE], hT[:, k, t * P:(t + 1) * P], wr[:, k, :],
                             start=(k == 0), stop=(k == KT - 1))
            ins.then_inc(s["logit_done"], 1)
            pe.wait_ge(s["mask_ready"], 1)
            mm(bank[5][:, 0:NE], below[:, :], gm[:, 0, 0, :], start=True, stop=True)
            mm(bank[5][:, NE:2 * NE], ones[:, :], gm[:, 0, 0, :], start=True, stop=False)
            mm(bank[5][:, NE:2 * NE], below[:, :], gm[:, 1, 0, :], start=False, stop=True)
            for t in range(TT):
                ins = mm(bank[6][0:NE, 0:1], gm[:, t, 0, :], ones[:, 0:1], start=(t == 0), stop=(t == TT - 1))
            ins.then_inc(s["rank_done"], 1)
            pe.wait_ge(s["key_ready"], 1)
            pe.wait_ge(s["ex_ready"], 1)
            for t in range(TT):
                tr(bank[7][0:NE, t * P:(t + 1) * P], key[:, t, :], ident[:, :])
                tr(bank[7][0:NE, TOK + t * P:TOK + (t + 1) * P], gm[:, t, 1, :], ident[:, :])
            mm(bank[6][0:NE, 1:2], below[0:NE, 0:NE], cnt[:, 4:5], start=True, stop=True).then_inc(s["route_done"], 1)
            pe.wait_ge(s["sel_ready"], 1)
            for t in range(TT):
                w = slice(t * P, (t + 1) * P)
                o = slice(128 + t * NPASS, 128 + (t + 1) * NPASS)
                mm(bank[5][:, o], keyT[:, w], esel[0:NE, :], start=True, stop=False)
                mm(bank[5][:, o], ones[0:NE, :], base[:, :], start=False, stop=True)
                mm(bank[5][:, 256 + t * NPASS:256 + (t + 1) * NPASS], putT[0:NE, w], esel[0:NE, :], start=True, stop=True)
            mm(bank[6][0:1, 8:8 + NPASS], part[0:NE, 0:1], esel[0:NE, :], start=True, stop=True)
            mm(bank[6][0:1, 8 + NPASS:9 + NPASS], cnt[:, 4:5], ones[0:NE, 0:1], start=True, stop=True).then_inc(s["plan_ps"], 1)

            def gather():
                for k in range(KT):
                    for t in range(TT):
                        ins = mm(bank[0][:, k * SLOTS:(k + 1) * SLOTS], X[:, t, k * P:(k + 1) * P], pick[:, t, :],
                                 start=(t == 0), stop=(t == TT - 1))
                ins.then_inc(s["gath_done"], 1)

            def scatter():
                for q in range(4):
                    mm(bank[4 + q][:, :], putT[:, (q // 2) * P:(q // 2 + 1) * P], ysb[:, (q % 2) * 512:(q % 2 + 1) * 512],
                       start=True, stop=True).then_inc(s["scat_done"], 1)

            pe.wait_ge(s["picked"], TT + 1)
            pe.wait_ge(s["plan_ready"], 2)
            gather()
            pe.wait_ge(s["bias_in"], 32)
            npass = pe.value_load(plan[0:1, NPASS:NPASS + 1], min_val=NE, max_val=NPASS - 1)
            NPICK = 2 * TT + 1
            pe.sem_inc(s["put_ps"], 1)
            with pe.Fori(0, npass) as p:
                pe.wait_ge(s["xT_ready"], p + 1)
                for n in range(2):
                    for c in range(2):
                        mm(bank[n][c * SLOTS:(c + 1) * SLOTS, :], bsel[:, :], bup[:, c * FF + n * 512:c * FF + (n + 1) * 512],
                           start=True, stop=False)
                for k in range(KT):
                    pe.wait_ge(chunk_in[k], 16 * p + 16)
                    for n in range(2):
                        for c in range(2):
                            ins = mm(bank[n][c * SLOTS:(c + 1) * SLOTS, :], xT[:, k, :],
                                     ring[:, k, c * FF + n * 512:c * FF + (n + 1) * 512], start=False, stop=(k == KT - 1))
                    ins.then_inc(s["chunk_used"], 1)
                pe.wait_ge(s["scat_read"], 4 * p + 1)
                pe.wait_ge(s["y_ready"], 2 * p + 2)
                pe.wait_ge(s["put_ready"], p + 1)
                scatter()
                pe.wait_ge(s["picked"], NPICK * p + TT + 1 + TT)
                for t in range(TT):
                    ins = tr(bank[2][:, t * P:(t + 1) * P], gpick[:, t, :], ident[:, :])
                ins.then_inc(s["put_ps"], 1)
                pe.wait_ge(s["act_ready"], 2 * p + 2)
                for i in range(4):
                    ins = tr(bank[3][:, i * P:(i + 1) * P], act_[:, i * P:(i + 1) * P], ident[:, :])
                ins.then_inc(s["actT_ps"], 1)
                pe.wait_ge(s["picked"], NPICK * p + 2 * TT + 2 + TT)
                gather()
                pe.wait_ge(s["actT_ready"], p + 1)
                pe.wait_ge(s["put_ready"], p + 2)
                for i in range(DNC):
                    pe.wait_ge(chunk_in[UPC + i], 16 * p + 16)
                    for n in range(2):
                        for c in range(2):
                            ins = mm(bank[2 + n][c * SLOTS:(c + 1) * SLOTS, :], actT[:, i * P + c * SLOTS:i * P + (c + 1) * SLOTS],
                                     ring[:, UPC + i, c * D + n * 512:c * D + (n + 1) * 512],
                                     start=(i == 0), stop=(i == DNC - 1))
                    ins.then_inc(s["chunk_used"], 1)
            pe.wait_ge(s["scat_read"], 4 * npass + 1)
            pe.wait_ge(s["y_ready"], 2 * npass + 2)
            pe.wait_ge(s["put_ready"], npass + 1)
            scatter()


_INS = ['x', 'emb_ln_g', 'emb_ln_b', 'w_in', 'attn_sink', 'hgrn_lb_logits', 'hgrn_norm_g', 'w_out', 'ln1_g', 'ln1_b',
        'w_router', 'b_router', 'w_up', 'b_up', 'w_down', 'b_down', 'ln2_g', 'ln2_b']
_OUTS = [((1, 256, 1024), 'float32')]


def kernel(**inputs):
    import numpy as _np
    import concourse.bacc as _bacc
    from concourse import mybir as _mybir
    from concourse.bass_utils import run_bass_kernel_spmd as _run

    nc = _bacc.Bacc("TRN2", target_bir_lowering=False, num_devices=1)
    arrays, args = {}, []
    for name in _INS:
        a = _np.ascontiguousarray(inputs[name])
        arrays[f"in_{name}_dram"] = a
        args.append(nc.dram_tensor(f"in_{name}_dram", a.shape, _mybir.dt.from_np(a.dtype), kind="ExternalInput").ap())
    for i, (shape, dtype) in enumerate(_OUTS):
        dt = _mybir.dt.from_np(_np.dtype(dtype))
        args.append(nc.dram_tensor(f"out_{i}_dram", shape, dt, kind="ExternalOutput").ap())
    encoder_layer(nc, *args)
    r = _run(nc, [arrays], core_ids=[0])
    got = tuple(r.results[0][f"out_{i}_dram"] for i in range(len(_OUTS)))
    return got[0]
```

```python
from contextlib import ExitStack

import concourse.bass as bass
from concourse import mybir

F32 = mybir.dt.float32
I32 = mybir.dt.int32
U32 = mybir.dt.uint32
ALU = mybir.AluOpType
ACT = mybir.ActivationFunctionType
AX_X = mybir.AxisListType.X

P = 128
TOPK = 4
WINDOW = 128
HG_CHUNK = 64
LIMIT, SIG_ALPHA = 7.0, 1.702
LN_EPS, RMS_EPS = 1e-5, 1e-6
DEEP_ALPHA = 2.0 ** 0.25
FAR = 1e30
NOT_HERE = 4096.0
SLOTS = 64


def counted(eng, sem):
    state = {"n": 0}

    def tick(ins):
        state["n"] += 1
        ins.then_inc(sem, 1)

    def settle():
        eng.wait_ge(sem, state["n"])

    def link(ins):
        tick(ins)
        settle()

    return link, tick, settle, state


def encoder_layer(nc, x, emb_ln_g, emb_ln_b, w_in, attn_sink, hgrn_lb_logits, hgrn_norm_g, w_out,
                  ln1_g, ln1_b, w_router, b_router, w_up, b_up, w_down, b_down, ln2_g, ln2_b, out):
    D = x.shape[2]
    KT = D // P
    TT = x.shape[1] // P
    TOK = TT * P
    NE = w_router.shape[2]
    FF = w_down.shape[2]
    HQ = attn_sink.shape[1]
    DH, NG = 64, 2
    QPG = HQ // NG
    HW = hgrn_norm_g.shape[1]
    NH = HW // P
    NC = TOK // HG_CHUNK
    NPASS = NE + TOK * TOPK // (SLOTS + 1) + 1
    NPASS += NPASS % 2
    UPC, DNC = KT, KT // 2
    CHUNKS = UPC + DNC
    CW = 2 * FF

    A0, K0, Q0 = 0, HQ * DH, HQ * DH + 2 * NG * DH
    GROUPS = [("qa", A0, HQ * DH), ("kv", K0, 2 * NG * DH), ("zf0", Q0 + 2 * HW, HW), ("zf1", Q0 + 3 * HW, HW),
              ("qh", Q0, HW), ("ih", Q0 + HW, HW), ("zg", Q0 + 4 * HW, HW)]
    GI = {g[0]: n for n, g in enumerate(GROUPS)}
    WBUF = 3

    with ExitStack() as ctx:
        def sb(name, shape, dt=F32):
            return ctx.enter_context(nc.sbuf_tensor(name, shape, dt))

        def sem(name):
            return ctx.enter_context(nc.semaphore(name))

        bank = [ctx.enter_context(nc.psum_tensor(f"bank{i}", [P, 512], F32)) for i in range(8)]

        ring = sb("ring", [P, CHUNKS, CW])
        wbuf = sb("wbuf", [P, WBUF, 4096])
        half = ring[:, :, :].rearrange("p c (a n) -> p (c a) n", a=2)

        def wide(i):
            return half[:, i, :]

        hg = [dict(k=wide(8 + d * 8), C=wide(9 + d * 8), A=wide(10 + d * 8), Dl=wide(11 + d * 8),
                   qrel=wide(12 + d * 8), krel=wide(13 + d * 8), kp=wide(14 + d * 8), qe=wide(15 + d * 8))
              for d in range(2)]
        score = [wide(0), wide(1)]
        probT = [wide(2), wide(3)]
        state = ring[:, 2, :].rearrange("p (d i n) -> p d i n", d=2, i=2)
        state3 = ring[:, 3, 0:1024].rearrange("p (d n) -> p d n", d=2)

        scanm = wide(7)

        def S(d, i):
            return state[:, d, i, :] if i < 2 else state3[:, d, :]

        bup = wbuf[:, 0, 0:2 * FF]
        ysb = wbuf[:, 0, 2048:3072]
        xT = wbuf[:, 0, 3072:3584].rearrange("p (k s) -> p k s", k=KT)
        actT = wbuf[:, 0, 3584:4096]
        acc = wbuf[:, 2, 0:TT * D].rearrange("p (t n) -> p t n", t=TT)
        glu, lin, sig, act_ = (wbuf[:, 2, TT * D + i * 512:TT * D + (i + 1) * 512] for i in range(4))
        hot = wbuf[:, 1, 0:2 * TT * TOPK * NE].rearrange("p (m t j e) -> p m t j e", m=2, t=TT, j=TOPK)
        pick = wbuf[:, 1, 512:512 + TT * SLOTS].rearrange("p (t n) -> p t n", t=TT)
        gpick = wbuf[:, 1, 1024:1024 + TT * 2 * SLOTS].rearrange("p (t n) -> p t n", t=TT)
        keyp, gatep = (wbuf[:, 1, o:o + TT * NPASS].rearrange("p (t n) -> p t n", t=TT) for o in (1536, 1792))
        keyT = wbuf[0:NE, 1, 2048:2048 + TOK]
        dlt = wbuf[0:NE, 1, 2304:2304 + 3 * NPASS].rearrange("p (i n) -> p i n", i=3)

        X = sb("X", [P, TT, D])
        hT = sb("hT", [P, KT, TOK])
        lnp = sb("lnp", [P, 2, D])
        kpad = lnp[:, 0, :].rearrange("p (g o n) -> p g o n", g=NG, o=2)
        catm = sb("cat", [P, TT * D])
        cat = catm[:, :].rearrange("p (t n) -> p t n", t=TT)
        mixa = sb("mixa", [P, 4 * NH * TOK])
        qhT = mixa[:, 0:1024]
        ih = mixa[:, 1024:2048].rearrange("p (t n) -> p t n", t=TT)
        gz = mixa[:, 2048:3072].rearrange("p (t n) -> p t n", t=TT)
        qaT = mixa[:, 3072:4096].rearrange("p (j n) -> p j n", j=HQ // 2)
        side = [catm[:, :], mixa[:, 0:CW], mixa[:, CW:2 * CW]]
        SIDE = len(side)
        va = sb("va", [P, TT, P])
        ident = sb("ident", [P, P])
        ones = sb("ones", [P, P])
        below = sb("below", [P, P])
        maskF = sb("maskF", [P, P])
        maskB = sb("maskB", [P, P])
        dist = sb("dist", [P, TT, TOK])
        iota_s = sb("iota_s", [P, 2, SLOTS])
        part = sb("part", [P, 1])
        epsc = sb("epsc", [P, 2])
        normg = sb("normg", [P, HW])
        wr = sb("wr", [P, KT, NE])
        br = sb("br", [P, NE])
        sink = sb("sink", [P, HQ])
        lbrow = sb("lbrow", [16, P])
        lbt = sb("lbt", [P, 2, 2, NH])
        lb = sb("lb", [P, 2, NH])
        oml = sb("oml", [P, 2, NH])
        lbs = sb("lbs", [P, 2, NH])
        lbe = sb("lbe", [P, 2, 2, NH])
        st = sb("st", [P, TT, 2, 6])
        mv = sb("mv", [P, TT, 2])
        rstd = sb("rstd", [P, TT])
        mx = sb("mx", [P, QPG])
        nm, den, es, rden = (sb(n, [P, 2, QPG]) for n in ("nm", "den", "es", "rden"))
        decay = sb("decay", [P, 2, NH * NC])
        ssq = sb("ssq", [P, TT, NH])
        rr = sb("rr", [P, TT, NH])
        lg = sb("lg", [P, TT, NE])
        m8 = sb("m8", [P, TT, 8])
        i8 = sb("i8", [P, TT, 8], U32)
        i8f = sb("i8f", [P, TT, 8])
        nm0 = sb("nm0", [P, TT])
        g4 = sb("g4", [P, TT, TOPK])
        gs = sb("gs", [P, TT])
        mask = sb("mask", [P, TT, NE])
        gate = sb("gate", [P, TT, NE])
        key = sb("key", [P, TT, NE])
        cnt = sb("cnt", [NE, 8])
        esel = sb("esel", [P, NPASS])
        base = sb("base", [NE, NPASS])
        plan = sb("plan", [1, NPASS + 2], I32)
        bsel = sb("bsel", [P, SLOTS])
        putT = sb("putT", [P, TOK])

        names = ("x_in0 x_in1 emb_in ln1_in ln2_in par_in wout_in bias_in zeroed consts h_ready  "
                 "lb_ps proj_done job_done  logf_ready logf_in exps_in k_ready rms_sum "
                 "var_ready std_ready qh_ready qa_ready kv_ready ih_ready zg_sig gz_ready score_ready mx_ready "
                 "prob_ready sink_ready attn_cat rec_cat sq_ready rms_in rms_std mix_done x1_ready "
                 "logit_done top_ready g4_ready mask_ready gate_ready rank_done ex_ready route_done "
                 "key_ready sel_ready plan_ps plan_ready lbm_ready lb_exp kpT_ready aT_ready S_ready "
                 "chunk_used picked put_ps gath_done actT_ps scat_done scat_read put_ready xT_ready "
                 "actT_ready y_ready glu_ready sig_ready act_ready acc_ready stored dve_step act_step pool_step tail_step").split()
        s = {n: sem(n) for n in names}
        win_in = [sem(f"win_in{i}") for i in range(WBUF)]
        proj_read = [sem(f"proj_read{i}") for i in range(len(GROUPS))]
        job_read = [sem(f"job_read{i}") for i in range(4)]
        chunk_in = [sem(f"chunk_in{i}") for i in range(CHUNKS)]

        side_in = [sem(f"side_in{i}") for i in range(SIDE)]

        BATCH = [(t, g) for t in range(TT) for g in range(NG)]

        def two(kind, b):
            return [(kind, b, 0), (kind, b, 1)]

        STEPS = [("hT", t, i) for t in range(TT) for i in range(2)]
        STEPS += [("proj", "qa", 0), ("proj", "kv", 0), ("proj", "zf0", 0)] + two("score", 0) + two("score", 1)
        STEPS += [("proj", "zf1", 0)] + two("pT", 0) + [("pv", 0, 0)] + two("score", 2)
        STEPS += [("proj", "qh", 0)] + two("pT", 1) + [("pv", 1, 0)] + two("score", 3)
        STEPS += [("proj", "ih", 0)] + two("pT", 2) + [("pv", 2, 0)] + two("kpT", 0) + two("kpT", 1)
        STEPS += [("proj", "zg", 0)] + two("aT", 0) + two("aT", 1) + two("pT", 3) + [("pv", 3, 0)]
        STEPS += [("proj", "zg", 1)] + [("catT", 0, 0), ("catT", 1, 0), ("kv", 0, 0), ("kv", 1, 0), ("mix", 0, 0)]
        STEPS += [("kv", 0, 1), ("kv", 1, 1), ("mix", 1, 0), ("kv", 0, 2), ("kv", 1, 2), ("o", 0, 0), ("o", 1, 0)]
        STEPS += [("catT", 2, 0), ("catT", 3, 0), ("mix", 0, 1), ("mix", 1, 1)]
        STEPS += two("x1T", 0) + [("logit", 0, 0)] + two("x1T", 1) + [("logit", 1, 0)]
        jobs = [x for x in STEPS if x[0] not in ("proj", "mix", "logit")]
        J = {j: n for n, j in enumerate(jobs)}

        def job_is_done(eng, j):
            eng.wait_ge(s["job_done"], J[j] + 1)

        def job_is_read(eng, j):
            eng.wait_ge(job_read[J[j] % 4], J[j] // 4 + 1)

        def job_bank(j):
            return bank[J[j] % 4]

        def read(ins, j):
            ins.then_inc(job_read[J[j] % 4], 1)

        def proj_bank(name, i):
            return bank[4 + 2 * (GI[name] % 2) + i]

        def chunk_of(d, i):
            return i if d == 0 else NC - 1 - i

        w_in_v = w_in[0].rearrange("(k p) n -> p k n", p=P)
        w_out_v = w_out[0].rearrange("(k p) n -> p k n", p=P)
        up_v = w_up[0].rearrange("e (k p) n -> e k p n", p=P)
        dn_v = w_down[0].rearrange("e (a i p) n -> e i p a n", a=2, p=P)
        x_v = x[0].rearrange("(t p) n -> p t n", p=P)
        out_v = out[0].rearrange("(t p) n -> p t n", p=P)

        block = ctx.enter_context(nc.Block())

        def load_chunk(sp, e, c):
            dst = ring[:, c, :]
            if c < UPC:
                src = up_v[e, c] if isinstance(e, int) else up_v[bass.ds(e, 1), c].rearrange("a p n -> (a p) n")
            else:
                dst = dst.rearrange("p (a n) -> p a n", a=2)
                src = dn_v[e, c - UPC] if isinstance(e, int) else \
                    dn_v[bass.ds(e, 1), c - UPC].rearrange("o p a n -> (o p) a n")
            sp.dma_start(dst, src).then_inc(chunk_in[c], 16)

        @block.sync
        def _(sp):
            for t in range(TT):
                sp.dma_start(X[:, t, :], x_v[:, t, :]).then_inc(s[f"x_in{t}"], 16)
            for i, v in enumerate((emb_ln_g, emb_ln_b)):
                sp.dma_start(lnp[:, i, :], v.partition_broadcast(P)).then_inc(s["emb_in"], 16)
            for g, (_, c0, w) in enumerate(GROUPS):
                if g >= WBUF:
                    sp.wait_ge(s["proj_done"], g - WBUF + 1)
                sp.dma_start(wbuf[:, g % WBUF, 0:KT * w].rearrange("p (k n) -> p k n", k=KT),
                             w_in_v[:, :, c0:c0 + w]).then_inc(win_in[g % WBUF], 16)
            for i in range(2):
                sp.wait_ge(s["proj_done"], 5 + i)
                sp.dma_start(wbuf[:, 1 + i, :].rearrange("p (k n) -> p k n", k=4),
                             w_out_v[:, 4 * i:4 * i + 4, :]).then_inc(s["wout_in"], 16)
            sp.wait_ge(s["attn_cat"], len(BATCH))
            sp.dma_start(lnp[:, 0, :], ln1_g[0].partition_broadcast(P)).then_inc(s["ln1_in"], 16)
            sp.dma_start(lnp[:, 1, :], ln1_b[0].partition_broadcast(P)).then_inc(s["ln1_in"], 16)
            sp.wait_ge(s["rec_cat"], TT)
            for c in range(SIDE, UPC):
                load_chunk(sp, 0, c)
            sp.wait_ge(s["job_done"], J["catT", 3, 0] + 1)
            for c in range(SIDE):
                sp.dma_start(side[c], up_v[0, c]).then_inc(side_in[c], 16)
            sp.wait_ge(s["zeroed"], 3)
            sp.dma_start(bup[0:NE, :], b_up[0]).then_inc(s["bias_in"], 16)
            sp.dma_start(ysb[0:NE, :], b_down[0]).then_inc(s["bias_in"], 16)
            for c in range(UPC, CHUNKS):
                load_chunk(sp, 0, c)
            for c in range(SIDE):
                load_chunk(sp, 1, c)
            sp.wait_ge(s["x1_ready"], TT)
            sp.dma_start(lnp[:, 0, :], ln2_g[0].partition_broadcast(P)).then_inc(s["ln2_in"], 16)
            sp.dma_start(lnp[:, 1, :], ln2_b[0].partition_broadcast(P)).then_inc(s["ln2_in"], 16)
            for c in range(SIDE, CHUNKS):
                sp.wait_ge(s["chunk_used"], c + 1)
                load_chunk(sp, 1, c)
            sp.wait_ge(s["plan_ready"], 2)
            npass = sp.value_load(plan[0:1, NPASS:NPASS + 1], min_val=NE, max_val=NPASS - 1)
            with sp.Fori(2, npass) as p:
                e = sp.value_load(plan[0:1, bass.ds(p, 1)], min_val=0, max_val=NE - 1)
                for c in range(CHUNKS):
                    sp.wait_ge(s["chunk_used"], (p - 1) * CHUNKS + c + 1)
                    load_chunk(sp, e, c)
            for t in range(TT):
                sp.wait_ge(s["acc_ready"], t + 1)
                sp.dma_start(out_v[:, t, :], acc[:, t, :]).then_inc(s["stored"], 16)
            sp.wait_ge(s["stored"], 16 * TT)

        @block.gpsimd
        def _(pool):
            link, _, _, _ = counted(pool, s["pool_step"])
            const, _, _, _ = counted(pool, s["consts"])
            g = nc.gpsimd
            const(g.memset(epsc[:, 0:1], LN_EPS))
            const(g.memset(epsc[:, 1:2], RMS_EPS))
            link(g.memset(ident[:, :], 0.0))
            const(g.affine_select(out=ident[:, :], in_=ident[:, :], compare_op=ALU.not_equal, fill=1.0, base=0,
                            pattern=[[-1, P]], channel_multiplier=1))
            link(g.memset(ones[:, :], 1.0))
            link(g.memset(scanm, 1.0))
            const(g.memset(scanm.rearrange("p (c n) -> p c n", n=HG_CHUNK)[:, :, 0:1], 0.0))
            link(g.affine_select(out=maskF[:, :], in_=ones[:, :], compare_op=ALU.is_ge, fill=0.0, base=0,
                                 pattern=[[1, P]], channel_multiplier=-1))
            const(g.memset(maskF[0:HG_CHUNK, HG_CHUNK:P], 0.0))
            link(g.affine_select(out=maskB[:, :], in_=ones[:, :], compare_op=ALU.is_ge, fill=0.0, base=0,
                                 pattern=[[-1, P]], channel_multiplier=1))
            const(g.memset(maskB[HG_CHUNK:P, 0:HG_CHUNK], 0.0))
            const(g.affine_select(out=below[:, :], in_=ones[:, :], compare_op=ALU.is_gt, fill=0.0, base=0,
                            pattern=[[1, P]], channel_multiplier=-1))
            link(g.iota(dist[:, :, :], pattern=[[-P, TT], [1, TOK]], base=0, channel_multiplier=-1,
                        allow_small_or_imprecise_dtypes=True))
            link(g.affine_select(out=dist[:, :, :], in_=dist[:, :, :], compare_op=ALU.is_ge, fill=FAR,
                                 base=WINDOW, pattern=[[P, TT], [-1, TOK]], channel_multiplier=1))
            const(g.affine_select(out=dist[:, :, :], in_=dist[:, :, :], compare_op=ALU.is_ge, fill=-FAR,
                            base=WINDOW, pattern=[[-P, TT], [1, TOK]],
                            channel_multiplier=-1))
            const(g.iota(iota_s[:, :, :], pattern=[[0, 2], [1, SLOTS]], base=0, channel_multiplier=0,
                   allow_small_or_imprecise_dtypes=True))
            const(g.iota(part[:, :], pattern=[[0, 1]], base=0, channel_multiplier=1,
                   allow_small_or_imprecise_dtypes=True))
            const(g.memset(esel[:, :], 0.0))
            const(g.memset(putT[:, :], 0.0))
            zero, _, _, _ = counted(pool, s["zeroed"])
            pool.wait_ge(s["h_ready"], TT)
            zero(g.memset(kpad, 0.0))
            pool.wait_ge(s["proj_done"], len(GROUPS) + 1)
            zero(g.memset(bup, 0.0))
            zero(g.memset(ysb, 0.0))

        CONSTS, EPS_CONSTS, IDENT_CONSTS = 12, 2, 3

        @block.scalar
        def _(act):
            a = nc.scalar
            link, tick, settle, _ = counted(act, s["act_step"])
            act.dma_start(lbrow[:, :], hgrn_lb_logits.rearrange("d i (h p) -> (d i h) p", p=P)).then_inc(s["par_in"], 16)
            act.dma_start(sink[:, :], attn_sink[0].partition_broadcast(P)).then_inc(s["par_in"], 16)
            act.dma_start(normg[:, :], hgrn_norm_g[0].partition_broadcast(P)).then_inc(s["par_in"], 16)
            act.dma_start(wr[:, :, :], w_router[0].rearrange("(k p) n -> p k n", p=P)).then_inc(s["par_in"], 16)
            act.dma_start(br[:, :], b_router[0].partition_broadcast(P)).then_inc(s["par_in"], 16)

            def ln_std(n, t):
                act.wait_ge(s["var_ready"], 2 * n + t + 1)
                a.activation(rstd[:, t:t + 1], mv[:, t, 1:2], ACT.Sqrt, bias=epsc[:, 0:1]).then_inc(s["std_ready"], 1)

            def turned(kind, t, i):
                job_is_done(act, (kind, t, i))
                read(a.copy(hT[:, 4 * i:4 * i + 4, t * P:(t + 1) * P],
                            job_bank((kind, t, i))[:, :].rearrange("p (k n) -> p k n", k=4)), (kind, t, i))

            act.wait_ge(s["consts"], EPS_CONSTS)
            for t in range(TT):
                ln_std(0, t)
            for t, i in ((0, 0), (0, 1), (1, 0)):
                turned("hT", t, i)
            act.wait_ge(s["lbm_ready"], 1)
            a.activation(lbe[:, :, :, :], lbe[:, :, :, :], ACT.Exp).then_inc(s["lb_exp"], 1)

            def sig_gate(d):
                name = f"zf{d}"
                act.wait_ge(s["proj_done"], GI[name] + 1)
                tick(a.activation(hg[d]["k"][:, 0:512], proj_bank(name, 0)[:, :], ACT.Sigmoid))
                a.activation(hg[d]["k"][:, 512:1024], proj_bank(name, 1)[:, :], ACT.Sigmoid).then_inc(proj_read[GI[name]], 1)

            def log_gate(d):
                act.wait_ge(s["logf_ready"], d + 1)
                a.activation(hg[d]["C"], hg[d]["qe"], ACT.Ln).then_inc(s["logf_in"], 1)

            def exps(d):
                act.wait_ge(s["exps_in"], 2 * d + 1)
                a.activation(hg[d]["qrel"], hg[d]["A"], ACT.Exp).then_inc(s["k_ready"], 1)
                a.activation(hg[d]["krel"], hg[d]["A"], ACT.Exp, scale=-1.0).then_inc(s["k_ready"], 1)
                act.wait_ge(s["exps_in"], 2 * d + 2)
                a.activation(hg[d]["kp"], hg[d]["Dl"], ACT.Exp).then_inc(s["k_ready"], 1)
                a.activation(hg[d]["qe"], hg[d]["C"], ACT.Exp).then_inc(s["k_ready"], 1)

            def probs(b):
                act.wait_ge(s["mx_ready"], b + 1)
                for j in range(QPG):
                    sc = score[b % 2][:, j * TOK:(j + 1) * TOK]
                    tick(a.activation(sc, sc, ACT.Exp, bias=nm[:, b % 2, j:j + 1], scale=DH ** -0.5,
                                      accum_out=den[:, b % 2, j:j + 1]))
                settle()
                a.activation(es[:, b % 2, :], es[:, b % 2, :], ACT.Exp).then_inc(s["prob_ready"], 1)

            def probs_turned(b):
                if b >= 2:
                    job_is_done(act, ("pv", b - 2, 0))
                for h in range(2):
                    job_is_done(act, ("pT", b, h))
                    read(a.copy(probT[b % 2][:, h * 512:(h + 1) * 512], job_bank(("pT", b, h))[:, :]), ("pT", b, h))

            def k_turned(d):
                for t in range(TT):
                    job_is_done(act, ("kpT", d, t))
                    read(a.copy(hg[d]["Dl"].rearrange("p (t n) -> p t n", t=TT)[:, t, :], job_bank(("kpT", d, t))[:, :]),
                         ("kpT", d, t))

            def sig_out(t):
                act.wait_ge(s["proj_done"], GI["zg"] + 1 + t)
                a.activation(gz[:, t, :], proj_bank("zg", t)[:, :], ACT.Sigmoid).then_inc(s["zg_sig"], 1)

            act.wait_ge(s["proj_done"], GI["qa"] + 1)
            tick(a.copy(qaT[:, 0:2, :].rearrange("p k n -> p (k n)"), proj_bank("qa", 0)[:, :]))
            a.copy(qaT[:, 2:4, :].rearrange("p k n -> p (k n)"), proj_bank("qa", 1)[:, :]).then_inc(proj_read[GI["qa"]], 1)
            sig_gate(0)
            log_gate(0)
            probs(0)
            exps(0)
            probs(1)
            sig_gate(1)
            probs_turned(0)
            log_gate(1)
            probs(2)
            exps(1)
            probs_turned(1)
            probs(3)
            act.wait_ge(s["proj_done"], GI["ih"] + 1)
            tick(a.copy(ih[:, 0, :], proj_bank("ih", 0)[:, :]))
            a.copy(ih[:, 1, :], proj_bank("ih", 1)[:, :]).then_inc(proj_read[GI["ih"]], 1)
            probs_turned(2)
            k_turned(0)
            k_turned(1)
            sig_out(0)
            probs_turned(3)
            sig_out(1)

            def cat_turned(i):
                job_is_done(act, ("catT", i, 0))
                read(a.copy(hT[:, 2 * i:2 * i + 2, :].rearrange("p k n -> p (k n)"), job_bank(("catT", i, 0))[:, :]),
                     ("catT", i, 0))

            cat_turned(0)
            cat_turned(1)
            for t in range(TT):
                job_is_done(act, ("o", t, 0))
                for h in range(NH):
                    w = slice(h * P, (h + 1) * P)
                    ins = a.activation(hg[t]["k"][:, w], job_bank(("o", t, 0))[:, w], ACT.Square, accum_out=ssq[:, t, h:h + 1])
                    tick(ins)
                settle()
                a.activation(rr[:, t, :], ssq[:, t, :], ACT.Sqrt, bias=epsc[:, 1:2], scale=1.0 / P).then_inc(s["rms_std"], 1)
            cat_turned(3)
            ln_std(1, 0)
            turned("x1T", 0, 0)
            turned("x1T", 0, 1)
            ln_std(1, 1)
            turned("x1T", 1, 0)
            act.wait_ge(s["top_ready"], 1)
            for t in range(TT):
                a.activation(g4[:, t, :], m8[:, t, 0:TOPK], ACT.Exp, bias=nm0[:, t:t + 1],
                             accum_out=gs[:, t:t + 1]).then_inc(s["g4_ready"], 1)

            def tokens_in(p):
                act.wait_ge(s["gath_done"], p + 1)
                a.copy(xT, bank[0][:, :].rearrange("p (k s) -> p k s", k=KT)).then_inc(s["xT_ready"], 1)

            def expert_pass(p):
                for n in range(2):
                    act.wait_ge(s["glu_ready"], 2 * p + n + 1)
                    w = slice(n * 256, n * 256 + 256)
                    a.activation(sig[:, w], glu[:, w], ACT.Sigmoid, scale=SIG_ALPHA).then_inc(s["sig_ready"], 1)
                act.wait_ge(s["put_ps"], p + 2)
                a.copy(putT[:, :], bank[2][:, 0:TOK]).then_inc(s["put_ready"], 1)
                act.wait_ge(s["actT_ps"], p + 1)
                a.copy(actT, bank[3][:, :]).then_inc(s["actT_ready"], 1)
                tokens_in(p + 1)
                act.wait_ge(s["chunk_used"], (p + 1) * CHUNKS)
                for n in range(2):
                    a.copy(ysb[:, n * 512:(n + 1) * 512], bank[2 + n][:, :]).then_inc(s["y_ready"], 1)

            tokens_in(0)
            act.wait_ge(s["plan_ready"], 2)
            act.wait_ge(s["bias_in"], 32)
            act.sem_inc(s["put_ready"], 1)
            act.sem_inc(s["y_ready"], 2)
            npass = act.value_load(plan[0:1, NPASS:NPASS + 1], min_val=NE, max_val=NPASS - 1)
            expert_pass(0)
            with act.Fori(1, npass) as p:
                expert_pass(p)
            for t in range(TT):
                ln_std(2, t)

        @block.vector
        def _(dve):
            v = nc.vector
            link, tick, settle, vstate = counted(dve, s["dve_step"])

            def norm_stats(src, t, steps=(tick, settle, link)):
                for h in range(2):
                    steps[0](v.bn_stats(st[:, t, h, :], src[:, t, h * 512:(h + 1) * 512]))
                steps[1]()
                v.bn_aggr(mv[:, t, :], st[:, t, :, :]).then_inc(s["var_ready"], 1)

            def norm_apply(dst, n, t, params, ready, steps=(tick, settle, link)):
                dve.wait_ge(s["var_ready"], 2 * n + t + 1)
                dve.wait_ge(s[params], 32)
                steps[2](v.scalar_tensor_tensor(out=dst[:, t, :], in0=dst[:, t, :], scalar=mv[:, t, 0:1],
                                                in1=lnp[:, 0, :], op0=ALU.subtract, op1=ALU.mult))
                dve.wait_ge(s["std_ready"], 2 * n + t + 1)
                steps[2](v.reciprocal(rstd[:, t:t + 1], rstd[:, t:t + 1]))
                v.scalar_tensor_tensor(out=dst[:, t, :], in0=dst[:, t, :], scalar=rstd[:, t:t + 1],
                                       in1=lnp[:, 1, :], op0=ALU.mult, op1=ALU.add).then_inc(s[ready], 1)

            def turned(kind, t, i):
                job_is_done(dve, (kind, t, i))
                read(v.tensor_copy(hT[:, 4 * i:4 * i + 4, t * P:(t + 1) * P],
                                   job_bank((kind, t, i))[:, :].rearrange("p (k n) -> p k n", k=4)), (kind, t, i))

            for t in range(TT):
                dve.wait_ge(s[f"x_in{t}"], 16)
                norm_stats(X, t)
            for t in range(TT):
                norm_apply(X, 0, t, "emb_in", "h_ready")
            turned("hT", 1, 1)
            dve.wait_ge(s["lb_ps"], 1)
            link(v.tensor_copy(lbt[:, :, :, :], bank[7][:, 0:16].rearrange("p (d i h) -> p d i h", d=2, i=2)))
            link(v.tensor_tensor(lbs[:, :, :], lbt[:, :, 0, :], lbt[:, :, 1, :], ALU.max))
            v.tensor_tensor(lbe[:, :, :, :], lbt[:, :, :, :],
                            lbs[:, :, :].unsqueeze(2).broadcast_to([P, 2, 2, NH]), ALU.subtract).then_inc(s["lbm_ready"], 1)
            dve.wait_ge(s["consts"], CONSTS)
            link(v.scalar_tensor_tensor(out=dist[:, :, :], in0=dist[:, :, :], scalar=-1.0, in1=dist[:, :, :],
                                        op0=ALU.mult, op1=ALU.min))
            dve.wait_ge(s["lb_exp"], 1)
            link(v.tensor_tensor(lbs[:, :, :], lbe[:, :, 0, :], lbe[:, :, 1, :], ALU.add))
            link(v.reciprocal(lbs[:, :, :], lbs[:, :, :]))
            link(v.tensor_tensor(lb[:, :, :], lbe[:, :, 0, :], lbs[:, :, :], ALU.mult))
            link(v.tensor_scalar(oml[:, :, :], lb[:, :, :], -1.0, 1.0, ALU.mult, ALU.add))
            dve.wait_ge(s["proj_done"], GI["kv"] + 1)
            dve.wait_ge(s["zeroed"], 1)
            for g in range(NG):
                for o in range(2):
                    r = slice(o * DH, (o + 1) * DH)
                    tick(v.tensor_copy(kpad[r, g, o, :], proj_bank("kv", 0)[r, g * TOK:(g + 1) * TOK]))
            tick(v.tensor_copy(va[:, :, :], proj_bank("kv", 1)[:, 0:TOK].rearrange("p (t n) -> p t n", t=TT)))
            settle()
            dve.sem_inc(proj_read[GI["kv"]], 1)

            def cseq(ap):
                return ap.rearrange("p (c n) -> p c n", n=HG_CHUNK)

            def gates(d):
                dve.wait_ge(proj_read[GI[f"zf{d}"]], 1)
                B = hg[d]
                for h in range(NH):
                    w = slice(h * TOK, (h + 1) * TOK)
                    tick(v.tensor_scalar(B["qe"][:, w], B["k"][:, w], oml[:, d, h:h + 1], lb[:, d, h:h + 1], ALU.mult, ALU.add))
                settle()
                v.tensor_scalar(B["k"], B["qe"], -1.0, 1.0, ALU.mult, ALU.add).then_inc(s["logf_ready"], 1)

            def rescaled(d):
                B = hg[d]
                dve.wait_ge(s["logf_in"], d + 1)
                way = slice(None, None, -1) if d else slice(None)
                link(v.tensor_tensor_scan(B["C"][:, way], scanm, B["C"][:, way], 0.0, ALU.mult, ALU.add))
                last, ref = (HG_CHUNK - 1, HG_CHUNK // 2) if d == 0 else (0, HG_CHUNK - 1 - HG_CHUNK // 2)
                C3 = cseq(B["C"])
                shape = [P, NH * NC, HG_CHUNK]
                v.tensor_tensor(cseq(B["A"]), C3, C3[:, :, ref:ref + 1].broadcast_to(shape),
                                ALU.subtract).then_inc(s["exps_in"], 1)
                v.tensor_tensor(cseq(B["Dl"]), C3[:, :, last:last + 1].broadcast_to(shape), C3,
                                ALU.subtract).then_inc(s["exps_in"], 1)

            def q_in():
                dve.wait_ge(s["proj_done"], GI["qh"] + 1)
                tick(v.tensor_copy(qhT[:, 0:512], proj_bank("qh", 0)[:, :]))
                tick(v.tensor_copy(qhT[:, 512:1024], proj_bank("qh", 1)[:, :]))
                settle()
                dve.sem_inc(proj_read[GI["qh"]], 1)

            def scaled(d):
                B = hg[d]
                dve.wait_ge(s["k_ready"], 4 * d + 4)
                last = HG_CHUNK - 1 if d == 0 else 0
                tick(v.tensor_copy(decay[:, d, :], cseq(B["qe"])[:, :, last]))
                v.tensor_tensor(B["kp"], B["kp"], B["k"], ALU.mult).then_inc(s["kpT_ready"], 1)
                v.tensor_tensor(B["qrel"], B["qrel"], qhT, ALU.mult).then_inc(s["aT_ready"], 1)
                v.tensor_tensor(B["krel"], B["krel"], B["k"], ALU.mult).then_inc(s["aT_ready"], 1)
                tick(v.memset(B["A"], 0.0))
                settle()
                v.tensor_tensor(B["qe"], B["qe"], qhT, ALU.mult).then_inc(s["S_ready"], 1)

            def scores(b):
                t, g = BATCH[b]
                if b >= 2:
                    job_is_done(dve, ("pT", b - 2, 1))
                for h in range(2):
                    job_is_done(dve, ("score", b, h))
                    for q in range(2):
                        head = g * QPG + 2 * h + q
                        slope = 2.0 ** (-8.0 * (head + 1) / HQ)
                        ins = v.scalar_tensor_tensor(
                            out=score[b % 2][:, (2 * h + q) * TOK:(2 * h + q + 1) * TOK], in0=dist[:, t, :],
                            scalar=slope * DH ** 0.5, in1=job_bank(("score", b, h))[:, q * TOK:(q + 1) * TOK],
                            op0=ALU.mult, op1=ALU.add)
                        if q == 0:
                            tick(ins)
                    read(ins, ("score", b, h))
                settle()
                for h in range(2):
                    job_is_read(dve, ("score", b, h))
                link(v.tensor_reduce(mx[:, :], score[b % 2].rearrange("p (j n) -> p j n", j=QPG), AX_X, ALU.max))
                link(v.scalar_tensor_tensor(out=mx[:, :], in0=mx[:, :], scalar=DH ** -0.5,
                                            in1=sink[:, g * QPG:(g + 1) * QPG], op0=ALU.mult, op1=ALU.max))
                link(v.tensor_tensor(es[:, b % 2, :], sink[:, g * QPG:(g + 1) * QPG], mx[:, :], ALU.subtract))
                v.tensor_scalar(nm[:, b % 2, :], mx[:, :], -1.0, None, ALU.mult).then_inc(s["mx_ready"], 1)

            def mixed(b):
                t, g = BATCH[b]
                dve.wait_ge(s["prob_ready"], b + 1)
                link(v.tensor_tensor(den[:, b % 2, :], den[:, b % 2, :], es[:, b % 2, :], ALU.add))
                link(v.reciprocal(rden[:, b % 2, :], den[:, b % 2, :]))
                job_is_done(dve, ("pv", b, 0))
                w = slice(g * QPG * DH, (g + 1) * QPG * DH)
                tick(v.tensor_tensor(cat[:, t, w].rearrange("p (j n) -> p j n", j=QPG),
                                     job_bank(("pv", b, 0))[:, 0:QPG * DH].rearrange("p (j n) -> p j n", j=QPG),
                                     rden[:, b % 2, :].unsqueeze(2).broadcast_to([P, QPG, DH]), ALU.mult))
                settle()
                dve.sem_inc(s["attn_cat"], 1)
                dve.sem_inc(job_read[J["pv", b, 0] % 4], 1)

            def masked(d):
                for t in range(TT):
                    job_is_done(dve, ("aT", d, t))
                    read(v.copy_predicated(hg[d]["A"].rearrange("p (t h n) -> p t h n", t=TT, h=NH)[:, t, :, :],
                                           (maskF, maskB)[d][:, :].bitcast(I32).unsqueeze(1).broadcast_to([P, NH, P]),
                                           job_bank(("aT", d, t))[:, :].rearrange("p (h n) -> p h n", h=NH)), ("aT", d, t))

            def states(d, i):
                job_is_done(dve, ("kv", d, i))
                ps, c = job_bank(("kv", d, i)), chunk_of(d, i)
                if i == 0:
                    ins = v.tensor_copy(S(d, 0), ps[:, :])
                else:
                    job_is_read(dve, ("kv", d, i - 1))
                    for h in range(NH):
                        w = slice(h * P, (h + 1) * P)
                        ins = v.scalar_tensor_tensor(out=S(d, i)[:, w], in0=S(d, i - 1)[:, w],
                                                     scalar=decay[:, d, h * NC + c:h * NC + c + 1], in1=ps[:, w],
                                                     op0=ALU.mult, op1=ALU.add)
                        if h < NH - 1:
                            tick(ins)
                read(ins, ("kv", d, i))

            gates(0)
            scores(0)
            rescaled(0)
            scores(1)
            gates(1)
            mixed(0)
            scores(2)
            rescaled(1)
            q_in()
            scaled(0)
            mixed(1)
            scores(3)
            scaled(1)
            mixed(2)
            masked(0)
            masked(1)
            mixed(3)
            dve.wait_ge(s["par_in"], 80)
            for t in range(TT):
                dve.wait_ge(s["zg_sig"], t + 1)
                link(v.tensor_tensor(gz[:, t, :], gz[:, t, :], proj_bank("zg", t)[:, :], ALU.mult))
                link(v.tensor_tensor(gz[:, t, :], gz[:, t, :], normg[:, :], ALU.mult))
            dve.sem_inc(proj_read[GI["zg"]], 1)
            for i in range(NC - 1):
                for d in range(2):
                    states(d, i)
            for t in range(TT):
                dve.wait_ge(s["rms_std"], t + 1)
                link(v.reciprocal(rr[:, t, :], rr[:, t, :]))
                for h in range(NH):
                    tick(v.scalar_tensor_tensor(
                        out=cat[:, t, HQ * DH + h * P:HQ * DH + (h + 1) * P],
                        in0=job_bank(("o", t, 0))[:, h * P:(h + 1) * P],
                        scalar=rr[:, t, h:h + 1], in1=gz[:, t, h * P:(h + 1) * P], op0=ALU.mult, op1=ALU.mult))
                settle()
                dve.sem_inc(s["rec_cat"], 1)
                dve.sem_inc(job_read[J["o", t, 0] % 4], 1)
            job_is_done(dve, ("catT", 2, 0))
            read(v.tensor_copy(hT[:, 4:6, :].rearrange("p k n -> p (k n)"), job_bank(("catT", 2, 0))[:, :]), ("catT", 2, 0))

            def logits(t):
                dve.wait_ge(s["logit_done"], t + 1)
                link(v.tensor_tensor(lg[:, t, :], bank[4 + t][:, 0:NE], br[:, :], ALU.add))
                link(v.max(m8[:, t, :], lg[:, t, :]))
                tick(v.max_index(i8[:, t, :], m8[:, t, :], lg[:, t, :]))

            for t in range(TT):
                for n in range(2):
                    dve.wait_ge(s["mix_done"], 2 * t + n + 1)
                    w = slice(n * 512, n * 512 + 512)
                    tick(v.scalar_tensor_tensor(out=X[:, t, w], in0=X[:, t, w], scalar=DEEP_ALPHA,
                                                in1=bank[4 + 2 * t + n][:, :], op0=ALU.mult, op1=ALU.add))
                settle()
                norm_stats(X, t)
                norm_apply(X, 1, t, "ln1_in", "x1_ready")
            logits(0)
            turned("x1T", 1, 1)
            logits(1)
            settle()
            tick(v.tensor_scalar(nm0[:, :], m8[:, :, 0], -1.0, None, ALU.mult))
            link(v.tensor_copy(i8f[:, :, :], i8[:, :, :]))
            dve.sem_inc(s["top_ready"], 1)
            four = [P, TT, TOPK, NE]
            for t in range(TT):
                tick(v.tensor_tensor(hot[:, 0, t, :, :], iota_s[:, 0:1, 0:NE].broadcast_to([P, TOPK, NE]),
                                     i8f[:, t, 0:TOPK].unsqueeze(2).broadcast_to([P, TOPK, NE]), ALU.is_equal))
            settle()
            v.tensor_reduce(mask[:, :, :], hot[:, 0, :, :, :].rearrange("p t j e -> p t e j"), AX_X,
                            ALU.add).then_inc(s["mask_ready"], 1)
            dve.wait_ge(s["mask_ready"], 1)
            dve.wait_ge(s["rank_done"], 1)
            link(v.scalar_tensor_tensor(out=key[:, :, :], in0=bank[6][:, 0:TT * NE].rearrange("p (t e) -> p t e", t=TT),
                                        scalar=NOT_HERE, in1=mask[:, :, :], op0=ALU.add, op1=ALU.mult))
            v.tensor_scalar(key[:, :, :], key[:, :, :], -NOT_HERE, None, ALU.add).then_inc(s["key_ready"], 1)
            dve.wait_ge(s["key_ready"], 1)
            for t in range(TT):
                v.tensor_scalar(pick[:, t, :], iota_s[:, 0, :], key[:, t, 0:1], None, ALU.is_equal).then_inc(s["picked"], 1)
            v.tensor_copy(bsel[:, :], ident[:, 0:1].broadcast_to([P, SLOTS])).then_inc(s["picked"], 1)
            dve.wait_ge(s["g4_ready"], TT)
            link(v.reciprocal(gs[:, :], gs[:, :]))
            link(v.tensor_tensor(g4[:, :, :], g4[:, :, :], gs[:, :].unsqueeze(2).broadcast_to([P, TT, TOPK]), ALU.mult))
            for t in range(TT):
                tick(v.tensor_tensor(hot[:, 1, t, :, :], hot[:, 0, t, :, :],
                                     g4[:, t, :].unsqueeze(2).broadcast_to([P, TOPK, NE]), ALU.mult))
            settle()
            v.tensor_reduce(gate[:, :, :], hot[:, 1, :, :, :].rearrange("p t j e -> p t e j"), AX_X,
                            ALU.add).then_inc(s["gate_ready"], 1)
            link(v.tensor_copy(cnt[:, 0:1], bank[7][0:NE, 0:1]))
            for i in range(1, TOK // SLOTS):
                tick(v.tensor_scalar(cnt[:, i:i + 1], cnt[:, 0:1], float(SLOTS * i + 1), None, ALU.is_ge))
            settle()
            v.tensor_reduce(cnt[:, 4:5], cnt[:, 1:4], AX_X, ALU.add).then_inc(s["ex_ready"], 1)
            dve.wait_ge(s["route_done"], 1)
            tick(v.tensor_copy(keyT, bank[5][0:NE, 0:TOK]))
            tick(v.tensor_copy(putT[0:NE, :], bank[5][0:NE, TOK:2 * TOK]))
            link(v.tensor_scalar(cnt[:, 5:6], bank[7][0:NE, 1:2], float(NE), None, ALU.add))
            link(v.tensor_scalar(dlt[:, 0, :], iota_s[0:NE, 0, 0:NPASS], cnt[:, 5:6], None, ALU.subtract))
            link(v.tensor_scalar(dlt[:, 1, :], dlt[:, 0, :], 0.0, None, ALU.is_ge))
            link(v.scalar_tensor_tensor(out=dlt[:, 2, :], in0=dlt[:, 0, :], scalar=cnt[:, 4:5], in1=dlt[:, 1, :],
                                        op0=ALU.is_lt, op1=ALU.mult))
            link(v.tensor_scalar(dlt[:, 0, :], dlt[:, 0, :], 1.0, -float(SLOTS), ALU.add, ALU.mult))
            tick(v.tensor_tensor(base[:, :], dlt[:, 0, :], dlt[:, 2, :], ALU.mult))
            tick(v.tensor_copy(esel[0:NE, NE:NPASS], dlt[:, 2, NE:NPASS]))
            tick(v.tensor_copy(esel[0:NE, 0:NE], ident[0:NE, 0:NE]))
            settle()
            dve.sem_inc(s["sel_ready"], 1)
            for t in range(TT):
                tick(v.tensor_scalar(acc[:, t, :], X[:, t, :], DEEP_ALPHA, None, ALU.mult))
            dve.wait_ge(s["plan_ps"], 1)
            v.tensor_copy(plan[0:1, 0:NPASS], bank[4][0:1, 0:NPASS]).then_inc(s["plan_ready"], 1)
            v.tensor_scalar(plan[0:1, NPASS:NPASS + 1], bank[4][0:1, NPASS:NPASS + 1], float(NE), None,
                            ALU.add).then_inc(s["plan_ready"], 1)
            tick(v.tensor_copy(keyp[:, :, :], bank[6][:, 128:128 + TT * NPASS].rearrange("p (t n) -> p t n", t=TT)))
            tick(v.tensor_copy(gatep[:, :, :], bank[6][:, 256:256 + TT * NPASS].rearrange("p (t n) -> p t n", t=TT)))
            settle()
            dve.sem_inc(s["scat_read"], 1)

            done = vstate["n"]

            def scattered(p, q):
                dve.wait_ge(s["scat_done"], 4 * p + q + 1)
                w = slice((q % 2) * 512, (q % 2) * 512 + 512)
                v.tensor_tensor(acc[:, q // 2, w], acc[:, q // 2, w], bank[4 + q][:, :], ALU.add).then_inc(s["scat_read"], 1)

            def expert_pass(p, here, following):
                dve.wait_ge(s["put_ps"], p + 1)
                for t in range(TT):
                    v.tensor_scalar(gpick[:, t, :], iota_s[:, :, :].rearrange("p a n -> p (a n)"),
                                    keyp[:, t, here], gatep[:, t, here],
                                    ALU.is_equal, ALU.mult).then_inc(s["picked"], 1)
                dve.wait_ge(s["gath_done"], p + 1)
                dve.wait_ge(s["chunk_used"], p * CHUNKS + 1)
                for t in range(TT):
                    v.tensor_scalar(pick[:, t, :], iota_s[:, 0, :], keyp[:, t, following], None,
                                    ALU.is_equal).then_inc(s["picked"], 1)
                v.tensor_copy(bsel[:, :], esel[:, following].broadcast_to([P, SLOTS])).then_inc(s["picked"], 1)
                for n in range(2):
                    dve.wait_ge(s["chunk_used"], p * CHUNKS + UPC)
                    pair = bank[n][:, :].rearrange("p (f two) -> p f two", two=2)
                    w = slice(n * 256, n * 256 + 256)
                    v.tensor_scalar(glu[:, w], pair[:, :, 0], LIMIT, None, ALU.min).then_inc(s["glu_ready"], 1)
                    v.tensor_scalar(lin[:, w], pair[:, :, 1], LIMIT, -LIMIT, ALU.min, ALU.max).then_inc(s["dve_step"], 1)
                for n in range(2):
                    w = slice(n * 256, n * 256 + 256)
                    dve.wait_ge(s["dve_step"], done + 4 * p + 2 + n)
                    dve.wait_ge(s["glu_ready"], 2 * p + n + 1)
                    v.scalar_tensor_tensor(out=lin[:, w], in0=lin[:, w], scalar=1.0, in1=glu[:, w],
                                           op0=ALU.add, op1=ALU.mult).then_inc(s["dve_step"], 1)
                    dve.wait_ge(s["dve_step"], done + 4 * p + 3 + n)
                    dve.wait_ge(s["sig_ready"], 2 * p + n + 1)
                    v.tensor_tensor(act_[:, w], lin[:, w], sig[:, w], ALU.mult).then_inc(s["act_ready"], 1)
                dve.wait_ge(s["scat_read"], 4 * p + 1)
                for q in range(4):
                    scattered(p, q)

            dve.wait_ge(s["plan_ready"], 2)
            npass = dve.value_load(plan[0:1, NPASS:NPASS + 1], min_val=NE, max_val=NPASS - 1)
            expert_pass(0, slice(0, 1), slice(1, 2))
            with dve.Fori(1, npass) as p:
                expert_pass(p, bass.ds(p, 1), bass.ds(p + 1, 1))
            l3, t3, s3, _ = counted(dve, s["tail_step"])
            dve.wait_ge(s["scat_read"], 4 * npass + 1)
            for t in range(TT):
                for n in range(2):
                    scattered(npass, 2 * t + n)
                dve.wait_ge(s["scat_read"], 4 * npass + 2 * t + 3)
                norm_stats(acc, t, (t3, s3, l3))
            for t in range(TT):
                norm_apply(acc, 2, t, "ln2_in", "acc_ready", (t3, s3, l3))

        @block.tensor
        def _(pe):
            mm = nc.tensor.matmul
            tr = nc.tensor.transpose
            pe.wait_ge(s["consts"], IDENT_CONSTS)
            pe.wait_ge(s["par_in"], 80)
            tr(bank[7][:, 0:16], lbrow[:, :], ident[0:16, 0:16]).then_inc(s["lb_ps"], 1)

            def turn(b, src, tiles):
                for n, (t, k) in enumerate(tiles):
                    ins = tr(b[:, n * P:(n + 1) * P], src[:, t, k * P:(k + 1) * P], ident[:, :])
                return ins

            def project(name, part_):
                g, w = GI[name], GROUPS[GI[name]][2]
                if part_ == 0:
                    pe.wait_ge(win_in[g % WBUF], 16 * (g // WBUF + 1))
                    if g == 1:
                        pe.wait_ge(s["lbm_ready"], 1)
                    if g >= 2:
                        pe.wait_ge(proj_read[g - 2], 1)
                wv = wbuf[:, g % WBUF, 0:KT * w].rearrange("p (k n) -> p k n", k=KT)
                if name in ("zf0", "zf1", "qh", "qa"):
                    for c in range(4):
                        for k in range(KT):
                            ins = mm(proj_bank(name, c // 2)[:, (c % 2) * TOK:(c % 2 + 1) * TOK],
                                     wv[:, k, c * P:(c + 1) * P], hT[:, k, :], start=(k == 0), stop=(k == KT - 1))
                elif name == "kv":
                    for gr in range(NG):
                        for k in range(KT):
                            for o in range(2):
                                mm(proj_bank(name, 0)[o * DH:(o + 1) * DH, gr * TOK:(gr + 1) * TOK],
                                   wv[:, k, gr * DH:(gr + 1) * DH], hT[:, k, :], start=(k == 0), stop=(k == KT - 1))
                    for t in range(TT):
                        for k in range(KT):
                            ins = mm(proj_bank(name, 1)[:, t * P:(t + 1) * P], hT[:, k, t * P:(t + 1) * P],
                                     wv[:, k, P:2 * P], start=(k == 0), stop=(k == KT - 1))
                else:
                    for t in ((part_,) if name == "zg" else range(TT)):
                        for k in range(KT):
                            ins = mm(proj_bank(name, t)[:, :], hT[:, k, t * P:(t + 1) * P], wv[:, k, :],
                                     start=(k == 0), stop=(k == KT - 1))
                ins.then_inc(s["proj_done"], 1)

            def mix_out(t, part_):
                if part_ == 0:
                    pe.wait_ge(proj_read[GI["zg" if t == 0 else "ih"]], 1)
                    pe.wait_ge(s["wout_in"], 32)
                for i in (2 * part_, 2 * part_ + 1):
                    job_is_read(pe, ("catT", i, 0))
                for n in range(2):
                    for k in range(4 * part_, 4 * part_ + 4):
                        ins = mm(bank[4 + 2 * t + n][:, :], hT[:, k, t * P:(t + 1) * P],
                                 wbuf[:, 1 + k // 4, (k % 4) * D + n * 512:(k % 4) * D + (n + 1) * 512],
                                 start=(k == 0), stop=(k == KT - 1))
                    if part_ == 1:
                        ins.then_inc(s["mix_done"], 1)

            def recur(o, t):
                for d in range(2):
                    job_is_read(pe, ("aT", d, t))
                for d, i in ((0, NC - 2), (1, NC - 2)):
                    job_is_read(pe, ("kv", d, i))
                pe.wait_ge(s["S_ready"], 2)
                for h in range(NH):
                    w = slice(h * P, (h + 1) * P)
                    aT = [hg[d]["A"].rearrange("p (t h n) -> p t h n", t=TT, h=NH)[:, t, h, :] for d in range(2)]
                    mm(o[:, w], aT[0], ih[:, t, w], start=True, stop=False)
                    for d, i in [(d, i) for d in range(2) for i in range(1, NC) if chunk_of(d, i) // 2 == t]:
                        c = chunk_of(d, i)
                        r = slice(HG_CHUNK * (c % 2), HG_CHUNK * (c % 2) + HG_CHUNK)
                        mm(o[r, w], hg[d]["qe"][:, h * TOK + c * HG_CHUNK:h * TOK + (c + 1) * HG_CHUNK],
                           S(d, i - 1)[:, w], start=False, stop=False)
                    ins = mm(o[:, w], aT[1], ih[:, t, w], start=False, stop=True)
                return ins

            for step in STEPS:
                kind, d, i = step
                if kind == "proj":
                    if (d, i) == ("qa", 0):
                        for t in range(TT):
                            for hh in range(2):
                                job_is_read(pe, ("hT", t, hh))
                    project(d, i)
                    continue
                if kind == "mix":
                    mix_out(d, i)
                    continue
                if kind == "logit":
                    for hh in range(2):
                        job_is_read(pe, ("x1T", d, hh))
                    for k in range(KT):
                        ins = mm(bank[4 + d][:, 0:NE], hT[:, k, d * P:(d + 1) * P], wr[:, k, :],
                                 start=(k == 0), stop=(k == KT - 1))
                    ins.then_inc(s["logit_done"], 1)
                    continue
                b = job_bank(step)
                if J[step] >= 4:
                    pe.wait_ge(job_read[J[step] % 4], J[step] // 4)
                if kind == "hT":
                    pe.wait_ge(s["h_ready"], d + 1)
                    ins = turn(b, X, [(d, 4 * i + k) for k in range(4)])
                elif kind == "x1T":
                    pe.wait_ge(s["x1_ready"], d + 1)
                    ins = turn(b, X, [(d, 4 * i + k) for k in range(4)])
                elif kind == "catT":
                    pe.wait_ge(*((s["attn_cat"], len(BATCH)) if d < 2 else (s["rec_cat"], TT)))
                    ins = turn(b, cat, [(t, 2 * d + k) for k in range(2) for t in range(TT)])
                elif kind == "score":
                    if step == ("score", 0, 0):
                        pe.wait_ge(proj_read[GI["qa"]], 1)
                        pe.wait_ge(proj_read[GI["kv"]], 1)
                    t, g = BATCH[d]
                    for q in range(2):
                        head = g * QPG + 2 * i + q
                        ins = mm(b[:, q * TOK:(q + 1) * TOK], qaT[:, head // 2, t * P:(t + 1) * P],
                                 kpad[:, g, head % 2, :], start=True, stop=True)
                elif kind == "pT":
                    pe.wait_ge(s["prob_ready"], d + 1)
                    for q in range(2):
                        for kt in range(TT):
                            src = score[d % 2][:, (2 * i + q) * TOK + kt * P:(2 * i + q) * TOK + (kt + 1) * P]
                            ins = tr(b[:, q * TOK + kt * P:q * TOK + (kt + 1) * P], src, ident[:, :])
                elif kind == "pv":
                    t, g = BATCH[d]
                    for hh in range(2):
                        job_is_read(pe, ("pT", d, hh))
                    for q in range(QPG):
                        for kt in range(TT):
                            ins = mm(b[:, q * DH:(q + 1) * DH],
                                     probT[d % 2][:, q * TOK + kt * P:q * TOK + (kt + 1) * P],
                                     va[:, kt, g * DH:(g + 1) * DH], start=(kt == 0), stop=(kt == TT - 1))
                elif kind == "kpT":
                    pe.wait_ge(s["kpT_ready"], d + 1)
                    for h in range(NH):
                        ins = tr(b[:, h * P:(h + 1) * P], hg[d]["kp"][:, h * TOK + i * P:h * TOK + (i + 1) * P], ident[:, :])
                elif kind == "aT":
                    pe.wait_ge(s["aT_ready"], 2 * d + 2)
                    for h in range(NH):
                        w = slice(h * TOK + i * P, h * TOK + (i + 1) * P)
                        ins = mm(b[:, h * P:(h + 1) * P], hg[d]["krel"][:, w], hg[d]["qrel"][:, w], start=True, stop=True)
                elif kind == "kv":
                    c = chunk_of(d, i)
                    job_is_read(pe, ("kpT", d, c // 2))
                    pe.wait_ge(proj_read[GI["ih"]], 1)
                    r = slice(HG_CHUNK * (c % 2), HG_CHUNK * (c % 2) + HG_CHUNK)
                    kpt = hg[d]["Dl"].rearrange("p (t n) -> p t n", t=TT)
                    for h in range(NH):
                        w = slice(h * P, (h + 1) * P)
                        ins = mm(b[:, w], kpt[r, c // 2, w], ih[r, c // 2, w], start=True, stop=True)
                elif kind == "o":
                    ins = recur(b, d)
                ins.then_inc(s["job_done"], 1)

            pe.wait_ge(s["mask_ready"], 1)
            pe.wait_ge(s["consts"], CONSTS)
            mm(bank[6][:, 0:NE], below[:, :], mask[:, 0, :], start=True, stop=True)
            mm(bank[6][:, NE:2 * NE], ones[:, :], mask[:, 0, :], start=True, stop=False)
            mm(bank[6][:, NE:2 * NE], below[:, :], mask[:, 1, :], start=False, stop=True)
            for t in range(TT):
                ins = mm(bank[7][0:NE, 0:1], mask[:, t, :], ones[:, 0:1], start=(t == 0), stop=(t == TT - 1))
            ins.then_inc(s["rank_done"], 1)

            def places():
                pe.wait_ge(s["gate_ready"], 1)
                pe.wait_ge(s["ex_ready"], 1)
                for t in range(TT):
                    tr(bank[5][0:NE, t * P:(t + 1) * P], key[:, t, :], ident[:, :])
                    tr(bank[5][0:NE, TOK + t * P:TOK + (t + 1) * P], gate[:, t, :], ident[:, :])
                mm(bank[7][0:NE, 1:2], below[0:NE, 0:NE], cnt[:, 4:5], start=True, stop=True).then_inc(s["route_done"], 1)

            def passes():
                pe.wait_ge(s["sel_ready"], 1)
                for t in range(TT):
                    w = slice(t * P, (t + 1) * P)
                    o = slice(128 + t * NPASS, 128 + (t + 1) * NPASS)
                    mm(bank[6][:, o], keyT[:, w], esel[0:NE, :], start=True, stop=False)
                    mm(bank[6][:, o], ones[0:NE, :], base[:, :], start=False, stop=True)
                    mm(bank[6][:, 256 + t * NPASS:256 + (t + 1) * NPASS], putT[0:NE, w], esel[0:NE, :], start=True, stop=True)
                mm(bank[4][0:1, 0:NPASS], part[0:NE, 0:1], esel[0:NE, :], start=True, stop=True)
                mm(bank[4][0:1, NPASS:NPASS + 1], cnt[:, 4:5], ones[0:NE, 0:1], start=True, stop=True).then_inc(s["plan_ps"], 1)

            def gather():
                for k in range(KT):
                    for t in range(TT):
                        ins = mm(bank[0][:, k * SLOTS:(k + 1) * SLOTS], X[:, t, k * P:(k + 1) * P], pick[:, t, :],
                                 start=(t == 0), stop=(t == TT - 1))
                ins.then_inc(s["gath_done"], 1)

            def scatter():
                for q in range(4):
                    mm(bank[4 + q][:, :], putT[:, (q // 2) * P:(q // 2 + 1) * P], ysb[:, (q % 2) * 512:(q % 2 + 1) * 512],
                       start=True, stop=True).then_inc(s["scat_done"], 1)

            NPICK = 2 * TT + 1

            def weights(p, c):
                if isinstance(p, int) and c < SIDE:
                    pe.wait_ge(side_in[c], 16)
                    return side[c]
                pe.wait_ge(chunk_in[c], 16 * p + (0 if c < SIDE else 16))
                return ring[:, c, :]

            def hidden(p):
                pe.wait_ge(s["xT_ready"], p + 1)
                for n in range(2):
                    for c in range(2):
                        mm(bank[n][c * SLOTS:(c + 1) * SLOTS, :], bsel[:, :], bup[:, c * FF + n * 512:c * FF + (n + 1) * 512],
                           start=True, stop=False)
                for k in range(KT):
                    wk = weights(p, k)
                    for n in range(2):
                        for c in range(2):
                            ins = mm(bank[n][c * SLOTS:(c + 1) * SLOTS, :], xT[:, k, :],
                                     wk[:, c * FF + n * 512:c * FF + (n + 1) * 512], start=False, stop=(k == KT - 1))
                    ins.then_inc(s["chunk_used"], 1)
                    if isinstance(p, int) and k == 2:
                        passes()

            def expert_pass(p):
                hidden(p)
                pe.wait_ge(s["scat_read"], 4 * p + 1)
                pe.wait_ge(s["y_ready"], 2 * p + 2)
                pe.wait_ge(s["put_ready"], p + 1)
                scatter()
                pe.wait_ge(s["picked"], NPICK * p + TT + 1 + TT)
                for t in range(TT):
                    ins = tr(bank[2][:, t * P:(t + 1) * P], gpick[:, t, :], ident[:, :])
                ins.then_inc(s["put_ps"], 1)
                pe.wait_ge(s["act_ready"], 2 * p + 2)
                for i in range(4):
                    ins = tr(bank[3][:, i * P:(i + 1) * P], act_[:, i * P:(i + 1) * P], ident[:, :])
                ins.then_inc(s["actT_ps"], 1)
                pe.wait_ge(s["picked"], NPICK * p + 2 * TT + 2 + TT)
                gather()
                pe.wait_ge(s["actT_ready"], p + 1)
                pe.wait_ge(s["put_ready"], p + 2)
                for i in range(DNC):
                    wk = weights(p, UPC + i)
                    for n in range(2):
                        for c in range(2):
                            ins = mm(bank[2 + n][c * SLOTS:(c + 1) * SLOTS, :], actT[:, i * P + c * SLOTS:i * P + (c + 1) * SLOTS],
                                     wk[:, c * D + n * 512:c * D + (n + 1) * 512],
                                     start=(i == 0), stop=(i == DNC - 1))
                    ins.then_inc(s["chunk_used"], 1)

            for t in range(TT):
                for hh in range(2):
                    job_is_read(pe, ("x1T", t, hh))
            pe.wait_ge(s["picked"], TT + 1)
            gather()
            places()
            pe.sem_inc(s["put_ps"], 1)
            pe.wait_ge(s["bias_in"], 32)
            expert_pass(0)
            npass = pe.value_load(plan[0:1, NPASS:NPASS + 1], min_val=NE, max_val=NPASS - 1)
            with pe.Fori(1, npass) as p:
                expert_pass(p)
            pe.wait_ge(s["scat_read"], 4 * npass + 1)
            pe.wait_ge(s["y_ready"], 2 * npass + 2)
            pe.wait_ge(s["put_ready"], npass + 1)
            scatter()


_INS = ['x', 'emb_ln_g', 'emb_ln_b', 'w_in', 'attn_sink', 'hgrn_lb_logits', 'hgrn_norm_g', 'w_out', 'ln1_g', 'ln1_b',
        'w_router', 'b_router', 'w_up', 'b_up', 'w_down', 'b_down', 'ln2_g', 'ln2_b']
_OUTS = [((1, 256, 1024), 'float32')]


def kernel(**inputs):
    import numpy as _np
    import concourse.bacc as _bacc
    from concourse import mybir as _mybir
    from concourse.bass_utils import run_bass_kernel_spmd as _run

    nc = _bacc.Bacc("TRN2", target_bir_lowering=False, num_devices=1)
    arrays, args = {}, []
    for name in _INS:
        a = _np.ascontiguousarray(inputs[name])
        arrays[f"in_{name}_dram"] = a
        args.append(nc.dram_tensor(f"in_{name}_dram", a.shape, _mybir.dt.from_np(a.dtype), kind="ExternalInput").ap())
    for i, (shape, dtype) in enumerate(_OUTS):
        dt = _mybir.dt.from_np(_np.dtype(dtype))
        args.append(nc.dram_tensor(f"out_{i}_dram", shape, dt, kind="ExternalOutput").ap())
    encoder_layer(nc, *args)
    r = _run(nc, [arrays], core_ids=[0])
    got = tuple(r.results[0][f"out_{i}_dram"] for i in range(len(_OUTS)))
    return got[0]
```

```python
from contextlib import ExitStack

import concourse.bass as bass
from concourse import mybir

F32 = mybir.dt.float32
F32R = mybir.dt.float32r
I32 = mybir.dt.int32
U32 = mybir.dt.uint32
ALU = mybir.AluOpType
ACT = mybir.ActivationFunctionType
AX_X = mybir.AxisListType.X

P = 128
TOPK = 4
WINDOW = 128
HG_CHUNK = 64
LIMIT, SIG_ALPHA = 7.0, 1.702
LN_EPS, RMS_EPS = 1e-5, 1e-6
DEEP_ALPHA = 2.0 ** 0.25
FAR = 1e30
NOT_HERE = 4096.0
SLOTS = 64


def counted(eng, sem):
    state = {"n": 0}

    def tick(ins):
        state["n"] += 1
        ins.then_inc(sem, 1)

    def settle():
        eng.wait_ge(sem, state["n"])

    def link(ins):
        tick(ins)
        settle()

    return link, tick, settle, state


def encoder_layer(nc, x, emb_ln_g, emb_ln_b, w_in, attn_sink, hgrn_lb_logits, hgrn_norm_g, w_out,
                  ln1_g, ln1_b, w_router, b_router, w_up, b_up, w_down, b_down, ln2_g, ln2_b, out):
    D = x.shape[2]
    KT = D // P
    TT = x.shape[1] // P
    TOK = TT * P
    NE = w_router.shape[2]
    FF = w_down.shape[2]
    HQ = attn_sink.shape[1]
    DH, NG = 64, 2
    QPG = HQ // NG
    HW = hgrn_norm_g.shape[1]
    NH = HW // P
    NC = TOK // HG_CHUNK
    NPASS = NE + TOK * TOPK // (SLOTS + 1) + 1
    NPASS += NPASS % 2
    UPC, DNC = KT, KT // 2
    CHUNKS = UPC + DNC
    CW = 2 * FF

    A0, K0, Q0 = 0, HQ * DH, HQ * DH + 2 * NG * DH
    GROUPS = [("qa", A0, HQ * DH), ("kv", K0, 2 * NG * DH), ("zf0", Q0 + 2 * HW, HW), ("zf1", Q0 + 3 * HW, HW),
              ("qh", Q0, HW), ("ih", Q0 + HW, HW), ("zg", Q0 + 4 * HW, HW)]
    GI = {g[0]: n for n, g in enumerate(GROUPS)}
    UNITS = [(n, h) for n, _, w in GROUPS for h in range(w // 256)]
    UI = {u: i for i, u in enumerate(UNITS)}
    WBUF = 3

    with ExitStack() as ctx:
        def sb(name, shape, dt=F32):
            return ctx.enter_context(nc.sbuf_tensor(name, shape, dt))

        def sem(name):
            return ctx.enter_context(nc.semaphore(name))

        bank = [ctx.enter_context(nc.psum_tensor(f"bank{i}", [P, 512], F32)) for i in range(8)]

        with nc.sbuf_tensor("ring_r", [P, CHUNKS, CW], F32R) as ring_r, \
                nc.sbuf_tensor("wbuf_r", [P, WBUF, 4096], F32R) as wbuf_r, \
                nc.sbuf_tensor("hT_r", [P, KT, TOK], F32R) as hT_r:
            pass
        ring = sb("ring", [P, CHUNKS, CW])
        wbuf = sb("wbuf", [P, WBUF, 4096])
        hT = sb("hT", [P, KT, TOK])
        half = ring[:, :, :].rearrange("p c (a n) -> p (c a) n", a=2)

        def wide(i):
            return half[:, i, :]

        hg = [dict(k=wide(8 + d * 8), C=wide(9 + d * 8), A=wide(10 + d * 8), Dl=wide(11 + d * 8),
                   qrel=wide(12 + d * 8), krel=wide(13 + d * 8), kp=wide(14 + d * 8), qe=wide(15 + d * 8))
              for d in range(2)]
        score = [wide(0), wide(1)]
        probT = [wide(2), wide(3)]
        state = ring[:, 2, :].rearrange("p (d i n) -> p d i n", d=2, i=2)
        state3 = ring[:, 3, 0:1024].rearrange("p (d n) -> p d n", d=2)

        scanm = wide(7)

        def S(d, i):
            return state[:, d, i, :] if i < 2 else state3[:, d, :]

        bup = wbuf[:, 0, 0:2 * FF]
        ysb = wbuf[:, 0, 2048:3072]
        xT = wbuf[:, 0, 3072:3584].rearrange("p (k s) -> p k s", k=KT)
        actT = wbuf[:, 0, 3584:4096]
        acc = wbuf[:, 2, 0:TT * D].rearrange("p (t n) -> p t n", t=TT)
        glu, lin, sig, act_ = (wbuf[:, 2, TT * D + i * 512:TT * D + (i + 1) * 512] for i in range(4))

        X = sb("X", [P, TT, D])
        route = hT[:, :, :].rearrange("p k n -> p (k n)")
        hot = route[:, 0:2 * TT * TOPK * NE].rearrange("p (m t j e) -> p m t j e", m=2, t=TT, j=TOPK)
        pick = route[:, 512:512 + TT * SLOTS].rearrange("p (t n) -> p t n", t=TT)
        gpick = route[:, 640:640 + TT * 2 * SLOTS].rearrange("p (t n) -> p t n", t=TT)
        keyp, gatep = (route[:, o:o + TT * NPASS].rearrange("p (t n) -> p t n", t=TT) for o in (1024, 1152))
        keyT = route[0:NE, 1280:1280 + TOK]
        dlt = route[0:NE, 1536:1536 + 3 * NPASS].rearrange("p (i n) -> p i n", i=3)
        h_high = ring_r[:, 2, :].rearrange("p (k n) -> p k n", k=KT)
        h_low = hT_r

        def w_part(u, which):
            return wbuf_r[:, u % WBUF, which * 2048:(which + 1) * 2048]

        def w_raw(u):
            return wbuf[:, u % WBUF, 0:2048]

        lnp = sb("lnp", [P, 2, D])
        kpad = lnp[:, 0, :].rearrange("p (g o n) -> p g o n", g=NG, o=2)
        catm = sb("cat", [P, TT * D])
        cat = catm[:, :].rearrange("p (t n) -> p t n", t=TT)
        mixa = sb("mixa", [P, 4 * NH * TOK])
        qhT = mixa[:, 0:1024]
        ih = mixa[:, 3072:4096].rearrange("p (t n) -> p t n", t=TT)
        gz = mixa[:, 2048:3072].rearrange("p (t n) -> p t n", t=TT)
        qaT = mixa[:, 1024:2048].rearrange("p (j n) -> p j n", j=HQ // 2)
        side = [mixa[:, 0:CW], wbuf[:, 1, 0:CW], wbuf[:, 1, CW:2 * CW], mixa[:, CW:2 * CW], catm[:, :]]
        SIDE = CHUNKS - len(side)
        va = sb("va", [P, TT, P])
        ident = sb("ident", [P, P])
        ones = sb("ones", [P, P])
        below = sb("below", [P, P])
        maskF = sb("maskF", [P, P])
        maskB = sb("maskB", [P, P])
        dist = sb("dist", [P, TT, TOK])
        iota_s = sb("iota_s", [P, 2, SLOTS])
        part = sb("part", [P, 1])
        epsc = sb("epsc", [P, 2])
        warm = sb("warm", [P, 1])
        normg = sb("normg", [P, HW])
        wr = sb("wr", [P, KT, NE])
        br = sb("br", [P, NE])
        sink = sb("sink", [P, HQ])
        rows = sb("rows", [32, P])
        embT = sb("embT", [P, 2, KT])
        lbt = sb("lbt", [P, 2, 2, NH])
        lb = sb("lb", [P, 2, NH])
        oml = sb("oml", [P, 2, NH])
        lbs = sb("lbs", [P, 2, NH])
        lbe = sb("lbe", [P, 2, 2, NH])
        st = sb("st", [P, TT, 2, 6])
        mv = sb("mv", [P, TT, 2])
        rstd = sb("rstd", [P, TT])
        mx = sb("mx", [P, QPG])
        nm, den, es, rden = (sb(n, [P, 2, QPG]) for n in ("nm", "den", "es", "rden"))
        decay = sb("decay", [P, 2, NH * NC])
        ssq = sb("ssq", [P, TT, NH])
        rr = sb("rr", [P, TT, NH])
        lg = sb("lg", [P, TT, NE])
        m8 = sb("m8", [P, TT, 8])
        i8 = sb("i8", [P, TT, 8], U32)
        i8f = sb("i8f", [P, TT, 8])
        nm0 = sb("nm0", [P, TT])
        g4 = sb("g4", [P, TT, TOPK])
        gs = sb("gs", [P, TT])
        mask = sb("mask", [P, TT, NE])
        gate = sb("gate", [P, TT, NE])
        key = sb("key", [P, TT, NE])
        cnt = sb("cnt", [NE, 8])
        esel = sb("esel", [P, NPASS])
        base = sb("base", [NE, NPASS])
        plan = sb("plan", [1, NPASS + 2], I32)
        xg = dist[:, :, :].rearrange("p t n -> p (t n)")
        bsel = sb("bsel", [P, SLOTS])
        putT = sb("putT", [P, TOK])

        names = ("x_in0 x_in1 emb_in rows_in high_act high_dve low_ready h_split ln1_in ln2_in par_in "
                 "wout_in bias_in zeroed consts h_ready lb_ps proj_done job_done logf_ready logf_in exps_in "
                 "k_ready var_ready std_ready zg_sig mx_ready prob_ready attn_cat rec_cat rms_std mix_half "
                 "pad_ready mix_done hT_params x1_ready logit_done top_ready g4_ready mask_ready gate_ready "
                 "rank_done ex_ready route_done key_ready sel_ready plan_ps plan_ready lbm_ready lb_exp "
                 "kpT_ready aT_ready S_ready chunk_used picked put_ps gath_done xg_ready xT_ps actT_ps "
                 "scat_done scat_read put_ready xT_ready actT_ready y_ready glu_ready sig_ready act_ready "
                 "acc_ready stored dve_step act_step pool_step tail_step").split()
        s = {n: sem(n) for n in names}
        win_in = [sem(f"win_in{i}") for i in range(WBUF)]
        proj_read = [sem(f"proj_read{i}") for i in range(len(GROUPS))]
        job_read = [sem(f"job_read{i}") for i in range(4)]
        chunk_in = [sem(f"chunk_in{i}") for i in range(CHUNKS)]

        side_in = [sem(f"side_in{i}") for i in range(len(side))]

        BATCH = [(t, g) for t in range(TT) for g in range(NG)]

        def two(kind, b):
            return [(kind, b, 0), (kind, b, 1)]

        def two_of(name):
            return [("proj", name, 0), ("proj", name, 1)]

        STEPS = [("hT", t, i) for t in range(TT) for i in range(2)]
        STEPS += two_of("qa") + [("proj", "kv", 0)] + two_of("zf0") + two("score", 0) + two("score", 1)
        STEPS += two_of("zf1") + two("pT", 0) + two("score", 2)
        STEPS += [("proj", "qh", 0), ("pv", 0, 0), ("proj", "qh", 1)] + two("pT", 1) + two("score", 3)
        STEPS += [("proj", "ih", 0), ("pv", 1, 0), ("proj", "ih", 1)] + two("pT", 2) + two("kpT", 0)
        STEPS += [("proj", "zg", 0), ("pv", 2, 0)] + two("kpT", 1) + two("aT", 0) + two("aT", 1) + two("pT", 3)
        STEPS += [("proj", "zg", 1), ("pv", 3, 0), ("kv", 0, 0), ("kv", 1, 0), ("catT", 0, 0), ("catT", 1, 0)]
        STEPS += [("kv", 0, 1), ("kv", 1, 1), ("mix", 1, (0, 0)), ("kv", 0, 2), ("kv", 1, 2), ("mix", 1, (0, 1))]
        STEPS += [("o", 0, 0), ("mix", 0, (0, 0)), ("mix", 0, (0, 1)), ("catT", 2, 0), ("o", 1, 0)]
        STEPS += [("mix", 0, (1, 0)), ("catT", 3, 0), ("mix", 0, (1, 1)), ("mix", 1, (1, 0)), ("mix", 1, (1, 1))]
        STEPS += two("x1T", 0) + [("logit", 0, 0)] + two("x1T", 1) + [("logit", 1, 0)]
        jobs = [x for x in STEPS if x[0] not in ("proj", "mix", "logit")]
        J = {j: n for n, j in enumerate(jobs)}

        def job_is_done(eng, j):
            eng.wait_ge(s["job_done"], J[j] + 1)

        def job_is_read(eng, j):
            eng.wait_ge(job_read[J[j] % 4], J[j] // 4 + 1)

        def job_bank(j):
            return bank[J[j] % 4]

        def read(ins, j):
            ins.then_inc(job_read[J[j] % 4], 1)

        def proj_bank(name, i):
            return bank[4 + 2 * (GI[name] % 2) + i]

        def kpt(d, o):
            return hg[d][("Dl", "kp")[o]].rearrange("p (t n) -> p t n", t=TT)

        def unit_is_done(eng, name, half=1):
            eng.wait_ge(s["proj_done"], UI[name, half if (name, 1) in UI else 0] + 1)

        BY_DVE = (9, 10)

        def high_is_ready(eng, u):
            if u in BY_DVE:
                eng.wait_ge(s["high_dve"], BY_DVE.index(u) + 1)
            else:
                eng.wait_ge(s["high_act"], u + 1 - sum(b < u for b in BY_DVE))

        def tiles_of(ap, c):
            return ap.rearrange("p (h c n) -> p c h n", h=2, c=2)[:, c]

        def pair(name, c):
            return proj_bank(name, c)[:, :].rearrange("p (h n) -> p h n", h=2)

        def chunk_of(d, i):
            return i if d == 0 else NC - 1 - i

        w_in_v = w_in[0].rearrange("(k p) n -> p k n", p=P)
        w_out_v = w_out[0].rearrange("(k p) n -> p k n", p=P)
        up_v = w_up[0].rearrange("e (k p) n -> e k p n", p=P)
        dn_v = w_down[0].rearrange("e (a i p) n -> e i p a n", a=2, p=P)
        x_v = x[0].rearrange("(t p) n -> p t n", p=P)
        out_v = out[0].rearrange("(t p) n -> p t n", p=P)

        block = ctx.enter_context(nc.Block())

        def load_chunk(sp, e, c, aside=False):
            dst = side[c - SIDE] if aside else ring[:, c, :]
            if c < UPC:
                src = up_v[e, c] if isinstance(e, int) else up_v[bass.ds(e, 1), c].rearrange("a p n -> (a p) n")
            else:
                dst = dst.rearrange("p (a n) -> p a n", a=2)
                src = dn_v[e, c - UPC] if isinstance(e, int) else \
                    dn_v[bass.ds(e, 1), c - UPC].rearrange("o p a n -> (o p) a n")
            sp.dma_start(dst, src).then_inc(side_in[c - SIDE] if aside else chunk_in[c], 16)

        @block.sync
        def _(sp):
            for t in range(TT):
                sp.dma_start(X[:, t, :], x_v[:, t, :]).then_inc(s[f"x_in{t}"], 16)
            for u, (name, h) in enumerate(UNITS):
                if u >= WBUF:
                    sp.wait_ge(s["proj_done"], u - WBUF + 1)
                if u == 2:
                    for i, v in enumerate((emb_ln_g, emb_ln_b)):
                        sp.dma_start(lnp[:, i, :], v.partition_broadcast(P)).then_inc(s["emb_in"], 16)
                c0 = GROUPS[GI[name]][1] + 256 * h
                sp.dma_start(w_raw(u).rearrange("p (k n) -> p k n", k=KT),
                             w_in_v[:, :, c0:c0 + 256]).then_inc(win_in[u % WBUF], 16)
            for i in range(2):
                sp.wait_ge(s["proj_done"], len(UNITS) - 2 + i)
                sp.dma_start(wbuf[:, 1 + i, :].rearrange("p (k n) -> p k n", k=4),
                             w_out_v[:, 4 * i:4 * i + 4, :]).then_inc(s["wout_in"], 16)
            sp.wait_ge(s["attn_cat"], len(BATCH))
            sp.dma_start(lnp[:, 0, :], ln1_g[0].partition_broadcast(P)).then_inc(s["ln1_in"], 16)
            sp.dma_start(lnp[:, 1, :], ln1_b[0].partition_broadcast(P)).then_inc(s["ln1_in"], 16)
            EARLY = (0, 1, 4, 6, 8, 10)
            for c in EARLY:
                load_chunk(sp, 0 if c < SIDE else 1, c)
            load_chunk(sp, 0, SIDE, aside=True)
            sp.wait_ge(s["mix_half"], TT)
            for c in (SIDE + 1, SIDE + 2):
                load_chunk(sp, 0, c, aside=True)
            sp.wait_ge(s["job_done"], J["o", 1, 0] + 1)
            for c in range(SIDE):
                if c not in EARLY + (3,):
                    load_chunk(sp, 0, c)
            sp.wait_ge(s["rec_cat"], TT)
            load_chunk(sp, 0, 3)
            load_chunk(sp, 0, SIDE + 3, aside=True)
            sp.wait_ge(s["job_done"], J["catT", 3, 0] + 1)
            load_chunk(sp, 0, SIDE + 4, aside=True)
            sp.wait_ge(s["zeroed"], 2)
            sp.dma_start(bup[0:NE, :], b_up[0]).then_inc(s["bias_in"], 16)
            sp.dma_start(ysb[0:NE, :], b_down[0]).then_inc(s["bias_in"], 16)
            for c in range(SIDE, CHUNKS):
                if c not in EARLY:
                    load_chunk(sp, 1, c)
            sp.wait_ge(s["x1_ready"], 2 * TT)
            sp.dma_start(lnp[:, 0, :], ln2_g[0].partition_broadcast(P)).then_inc(s["ln2_in"], 16)
            sp.dma_start(lnp[:, 1, :], ln2_b[0].partition_broadcast(P)).then_inc(s["ln2_in"], 16)
            def replaces(p, c):
                sp.wait_ge(s["chunk_used"], p * CHUNKS + c + 1)

            for c in range(SIDE):
                replaces(0, c)
                load_chunk(sp, 1, c)
            for c in range(SIDE, CHUNKS):
                replaces(0, c)
                load_chunk(sp, 2, c, aside=True)
            for c in range(SIDE):
                replaces(1, c)
                load_chunk(sp, 2, c)
            for c in range(SIDE, CHUNKS):
                replaces(1, c)
                load_chunk(sp, 3, c)
            for c in range(SIDE):
                replaces(2, c)
                load_chunk(sp, 3, c)
            sp.wait_ge(s["plan_ready"], 3)
            npass = sp.value_load(plan[0:1, NPASS:NPASS + 1], min_val=NE, max_val=NPASS - 1)
            with sp.Fori(4, npass) as p:
                e = sp.value_load(plan[0:1, bass.ds(p, 1)], min_val=0, max_val=NE - 1)
                for c in range(CHUNKS):
                    replaces(p - 1, c)
                    load_chunk(sp, e, c)
            for t in range(TT):
                for n in range(2):
                    w = slice(n * D // 2, (n + 1) * D // 2)
                    sp.wait_ge(s["acc_ready"], 2 * t + n + 1)
                    sp.dma_start(out_v[:, t, w], acc[:, t, w]).then_inc(s["stored"], 16)
            sp.wait_ge(s["stored"], 16 * 2 * TT)

        @block.gpsimd
        def _(pool):
            link, _, _, _ = counted(pool, s["pool_step"])
            const, _, _, _ = counted(pool, s["consts"])
            g = nc.gpsimd
            const(g.memset(epsc[:, 0:1], LN_EPS))
            const(g.memset(epsc[:, 1:2], RMS_EPS))
            link(g.memset(ident[:, :], 0.0))
            const(g.affine_select(out=ident[:, :], in_=ident[:, :], compare_op=ALU.not_equal, fill=1.0, base=0,
                            pattern=[[-1, P]], channel_multiplier=1))
            link(g.memset(ones[:, :], 1.0))
            link(g.memset(scanm, 1.0))
            const(g.memset(scanm.rearrange("p (c n) -> p c n", n=HG_CHUNK)[:, :, 0:1], 0.0))
            link(g.affine_select(out=maskF[:, :], in_=ones[:, :], compare_op=ALU.is_ge, fill=0.0, base=0,
                                 pattern=[[1, P]], channel_multiplier=-1))
            const(g.memset(maskF[0:HG_CHUNK, HG_CHUNK:P], 0.0))
            link(g.affine_select(out=maskB[:, :], in_=ones[:, :], compare_op=ALU.is_ge, fill=0.0, base=0,
                                 pattern=[[-1, P]], channel_multiplier=1))
            const(g.memset(maskB[HG_CHUNK:P, 0:HG_CHUNK], 0.0))
            const(g.affine_select(out=below[:, :], in_=ones[:, :], compare_op=ALU.is_gt, fill=0.0, base=0,
                            pattern=[[1, P]], channel_multiplier=-1))
            link(g.iota(dist[:, :, :], pattern=[[-P, TT], [1, TOK]], base=0, channel_multiplier=-1,
                        allow_small_or_imprecise_dtypes=True))
            link(g.affine_select(out=dist[:, :, :], in_=dist[:, :, :], compare_op=ALU.is_ge, fill=FAR,
                                 base=WINDOW, pattern=[[P, TT], [-1, TOK]], channel_multiplier=1))
            const(g.affine_select(out=dist[:, :, :], in_=dist[:, :, :], compare_op=ALU.is_ge, fill=-FAR,
                            base=WINDOW, pattern=[[-P, TT], [1, TOK]],
                            channel_multiplier=-1))
            const(g.iota(iota_s[:, :, :], pattern=[[0, 2], [1, SLOTS]], base=0, channel_multiplier=0,
                   allow_small_or_imprecise_dtypes=True))
            const(g.iota(part[:, :], pattern=[[0, 1]], base=0, channel_multiplier=1,
                   allow_small_or_imprecise_dtypes=True))
            const(g.memset(esel[:, :], 0.0))
            const(g.memset(putT[:, :], 0.0))
            low, _, _, _ = counted(pool, s["low_ready"])
            padded, _, _, _ = counted(pool, s["pad_ready"])
            for u in range(len(UNITS)):
                high_is_ready(pool, u)
                low(g.tensor_tensor(w_part(u, 0), w_raw(u), w_part(u, 1).bitcast(F32), ALU.subtract))
            for d in range(2):
                job_is_done(pool, ("kpT", d, TT - 1))
                for o in range(2):
                    padded(g.memset(kpt(d, o)[(1 - o) * HG_CHUNK:(2 - o) * HG_CHUNK, :, :], 0.0))
            zero, _, _, _ = counted(pool, s["zeroed"])
            pool.wait_ge(s["proj_done"], len(UNITS))
            zero(g.memset(bup, 0.0))
            zero(g.memset(ysb, 0.0))

        CONSTS, EPS_CONSTS, IDENT_CONSTS = 12, 2, 3

        @block.scalar
        def _(act):
            a = nc.scalar
            link, tick, settle, _ = counted(act, s["act_step"])
            act.dma_start(rows[0:16, :], hgrn_lb_logits.rearrange("d i (h p) -> (d i h) p", p=P)).then_inc(s["rows_in"], 16)
            act.dma_start(rows[16:24, :], emb_ln_g.rearrange("(k p) -> k p", p=P)).then_inc(s["rows_in"], 16)
            act.dma_start(rows[24:32, :], emb_ln_b.rearrange("(k p) -> k p", p=P)).then_inc(s["rows_in"], 16)

            def ln_std(n, t):
                act.wait_ge(s["var_ready"], 2 * n + t + 1)
                a.activation(rstd[:, t:t + 1], mv[:, t, 1:2], ACT.Sqrt, bias=epsc[:, 0:1]).then_inc(s["std_ready"], 1)

            def preload(f):
                link(a.activation(warm[:, :], epsc[:, 0:1], f))

            def turned(kind, t, i):
                job_is_done(act, (kind, t, i))
                read(a.copy(hT[:, 4 * i:4 * i + 4, t * P:(t + 1) * P],
                            job_bank((kind, t, i))[:, :].rearrange("p (k n) -> p k n", k=4)), (kind, t, i))

            act.wait_ge(s["consts"], EPS_CONSTS)
            preload(ACT.Sqrt)
            for t in range(TT):
                ln_std(0, t)
            def high(u):
                act.wait_ge(win_in[u % WBUF], 16 * (u // WBUF + 1))
                a.copy(w_part(u, 1), w_raw(u)).then_inc(s["high_act"], 1)

            high(0)
            act.wait_ge(s["hT_params"], 1)
            for t in range(TT):
                job_is_done(act, ("hT", t, 0))
                for k in range(4):
                    ins = a.activation(hT[:, k, t * P:(t + 1) * P], job_bank(("hT", t, 0))[:, k * P:(k + 1) * P],
                                       ACT.Identity, bias=embT[:, 1, k:k + 1], scale=embT[:, 0, k:k + 1])
                    tick(ins)
                settle()
                read(a.copy(h_high[:, 0:4, t * P:(t + 1) * P], hT[:, 0:4, t * P:(t + 1) * P]), ("hT", t, 0))
            high(1)
            preload(ACT.Exp)
            act.dma_start(sink[:, :], attn_sink[0].partition_broadcast(P)).then_inc(s["par_in"], 16)
            act.dma_start(normg[:, :], hgrn_norm_g[0].partition_broadcast(P)).then_inc(s["par_in"], 16)
            act.dma_start(wr[:, :, :], w_router[0].rearrange("(k p) n -> p k n", p=P)).then_inc(s["par_in"], 16)
            act.dma_start(br[:, :], b_router[0].partition_broadcast(P)).then_inc(s["par_in"], 16)
            act.wait_ge(s["lbm_ready"], 1)
            a.activation(lbe[:, :, :, :], lbe[:, :, :, :], ACT.Exp).then_inc(s["lb_exp"], 1)

            def sig_gate(d):
                name = f"zf{d}"
                unit_is_done(act, name)
                tick(a.activation(tiles_of(hg[d]["k"], 0), pair(name, 0), ACT.Sigmoid))
                a.activation(tiles_of(hg[d]["k"], 1), pair(name, 1), ACT.Sigmoid).then_inc(proj_read[GI[name]], 1)

            def log_gate(d):
                act.wait_ge(s["logf_ready"], d + 1)
                a.activation(hg[d]["C"], hg[d]["qe"], ACT.Ln).then_inc(s["logf_in"], 1)

            def exps(d):
                act.wait_ge(s["exps_in"], 2 * d + 1)
                a.activation(hg[d]["qrel"], hg[d]["A"], ACT.Exp).then_inc(s["k_ready"], 1)
                a.activation(hg[d]["krel"], hg[d]["A"], ACT.Exp, scale=-1.0).then_inc(s["k_ready"], 1)
                act.wait_ge(s["exps_in"], 2 * d + 2)
                a.activation(hg[d]["kp"], hg[d]["Dl"], ACT.Exp).then_inc(s["k_ready"], 1)
                a.activation(hg[d]["qe"], hg[d]["C"], ACT.Exp).then_inc(s["k_ready"], 1)

            def probs(b):
                act.wait_ge(s["mx_ready"], b + 1)
                for j in range(QPG):
                    sc = score[b % 2][:, j * TOK:(j + 1) * TOK]
                    tick(a.activation(sc, sc, ACT.Exp, bias=nm[:, b % 2, j:j + 1], scale=DH ** -0.5,
                                      accum_out=den[:, b % 2, j:j + 1]))
                settle()
                a.activation(es[:, b % 2, :], es[:, b % 2, :], ACT.Exp).then_inc(s["prob_ready"], 1)

            def probs_turned(b):
                if b >= 2:
                    job_is_done(act, ("pv", b - 2, 0))
                for h in range(2):
                    job_is_done(act, ("pT", b, h))
                    read(a.copy(probT[b % 2][:, h * 512:(h + 1) * 512], job_bank(("pT", b, h))[:, :]), ("pT", b, h))

            def k_turned(d):
                job_is_done(act, ("kpT", d, TT - 1))
                for t in range(TT):
                    for o in range(2):
                        r = slice(o * HG_CHUNK, (o + 1) * HG_CHUNK)
                        ins = a.copy(kpt(d, o)[r, t, :], job_bank(("kpT", d, t))[r, :])
                        if o == 0:
                            tick(ins)
                    settle()
                    read(ins, ("kpT", d, t))

            def sig_out(t):
                unit_is_done(act, "zg")
                a.activation(gz[:, t, :], proj_bank("zg", t)[:, :], ACT.Sigmoid).then_inc(s["zg_sig"], 1)

            high(2)
            unit_is_done(act, "qa")
            q4 = qaT.rearrange("p j n -> p (j n)")
            tick(a.copy(tiles_of(q4, 0), pair("qa", 0)))
            a.copy(tiles_of(q4, 1), pair("qa", 1)).then_inc(proj_read[GI["qa"]], 1)
            for u in (3, 4, 5, 6):
                high(u)
            sig_gate(0)
            high(7)
            log_gate(0)
            probs(0)
            high(8)
            sig_gate(1)
            probs_turned(0)
            probs(1)
            log_gate(1)
            exps(0)
            probs(2)
            probs_turned(1)
            exps(1)
            high(11)
            probs(3)
            probs_turned(2)
            k_turned(0)
            high(12)
            k_turned(1)
            probs_turned(3)
            sig_out(0)
            sig_out(1)

            def cat_turned(i):
                job_is_done(act, ("catT", i, 0))
                read(a.copy(hT[:, 2 * i:2 * i + 2, :].rearrange("p k n -> p (k n)"), job_bank(("catT", i, 0))[:, :]),
                     ("catT", i, 0))

            cat_turned(0)
            cat_turned(1)
            preload(ACT.Sqrt)
            for t in range(TT):
                job_is_done(act, ("o", t, 0))
                for h in range(NH):
                    w = slice(h * P, (h + 1) * P)
                    ins = a.activation(scanm[:, t * HW + h * P:t * HW + (h + 1) * P], job_bank(("o", t, 0))[:, w], ACT.Square,
                                       accum_out=ssq[:, t, h:h + 1])
                    tick(ins)
                settle()
                a.activation(rr[:, t, :], ssq[:, t, :], ACT.Sqrt, bias=epsc[:, 1:2], scale=1.0 / P).then_inc(s["rms_std"], 1)
                if t == 0:
                    job_is_done(act, ("catT", 2, 0))
                    read(a.copy(hT[:, 4:8, 0:P], job_bank(("catT", 2, 0))[:, :].rearrange("p (k n) -> p k n", k=4)),
                         ("catT", 2, 0))
            ln_std(1, 0)
            turned("x1T", 0, 0)
            turned("x1T", 0, 1)
            ln_std(1, 1)
            turned("x1T", 1, 0)
            preload(ACT.Exp)
            act.wait_ge(s["top_ready"], 1)
            for t in range(TT):
                a.activation(g4[:, t, :], m8[:, t, 0:TOPK], ACT.Exp, bias=nm0[:, t:t + 1],
                             accum_out=gs[:, t:t + 1]).then_inc(s["g4_ready"], 1)

            def tokens_in(p):
                act.wait_ge(s["gath_done"], p + 1)
                a.copy(xg, bank[0][:, :]).then_inc(s["xg_ready"], 1)
                act.wait_ge(s["xT_ps"], p + 1)
                a.copy(xT.rearrange("p (c i) s -> p i c s", c=2),
                       bank[1][:, :].rearrange("p (i c s) -> p i c s", i=4, c=2)).then_inc(s["xT_ready"], 1)

            def expert_pass(p, last=False):
                for n in range(2):
                    act.wait_ge(s["glu_ready"], 2 * p + n + 1)
                    w = slice(n * 256, n * 256 + 256)
                    a.activation(sig[:, w], glu[:, w], ACT.Sigmoid, scale=SIG_ALPHA).then_inc(s["sig_ready"], 1)
                if last:
                    preload(ACT.Sqrt)
                act.wait_ge(s["put_ps"], p + 2)
                a.copy(putT[:, :], bank[2][:, 0:TOK]).then_inc(s["put_ready"], 1)
                act.wait_ge(s["actT_ps"], p + 1)
                a.copy(actT, bank[3][:, :]).then_inc(s["actT_ready"], 1)
                if not last:
                    tokens_in(p + 1)
                act.wait_ge(s["chunk_used"], (p + 1) * CHUNKS)
                for n in range(1 if last else 2):
                    a.copy(ysb[:, n * 512:(n + 1) * 512], bank[2 + n][:, :]).then_inc(s["y_ready"], 1)

            tokens_in(0)
            preload(ACT.Sigmoid)
            act.wait_ge(s["plan_ready"], 3)
            act.wait_ge(s["bias_in"], 32)
            act.sem_inc(s["put_ready"], 1)
            act.sem_inc(s["y_ready"], 2)
            last_pass = act.value_load(plan[0:1, NPASS + 1:NPASS + 2], min_val=NE - 1, max_val=NPASS - 2)
            expert_pass(0)
            with act.Fori(1, last_pass) as p:
                expert_pass(p)
            expert_pass(last_pass, last=True)
            for t in range(TT):
                ln_std(2, t)

        @block.vector
        def _(dve):
            v = nc.vector
            link, tick, settle, vstate = counted(dve, s["dve_step"])

            def norm_stats(src, t):
                for h in range(2):
                    tick(v.bn_stats(st[:, t, h, :], src[:, t, h * 512:(h + 1) * 512]))
                settle()
                v.bn_aggr(mv[:, t, :], st[:, t, :, :]).then_inc(s["var_ready"], 1)

            def turned(kind, t, i):
                job_is_done(dve, (kind, t, i))
                read(v.tensor_copy(hT[:, 4 * i:4 * i + 4, t * P:(t + 1) * P],
                                   job_bank((kind, t, i))[:, :].rearrange("p (k n) -> p k n", k=4)), (kind, t, i))

            for t in range(TT):
                dve.wait_ge(s[f"x_in{t}"], 16)
                norm_stats(X, t)
                dve.wait_ge(s["std_ready"], t + 1)
                link(v.reciprocal(rstd[:, t:t + 1], rstd[:, t:t + 1]))
                v.tensor_scalar(X[:, t, :], X[:, t, :], mv[:, t, 0:1], rstd[:, t:t + 1], ALU.subtract,
                                ALU.mult).then_inc(s["h_ready"], 1)
            dve.wait_ge(s["lb_ps"], 1)
            v.tensor_copy(embT[:, :, :], bank[7][:, 16:32].rearrange("p (m k) -> p m k", m=2)).then_inc(s["hT_params"], 1)
            tick(v.tensor_copy(lbt[:, :, :, :], bank[7][:, 0:16].rearrange("p (d i h) -> p d i h", d=2, i=2)))
            dve.wait_ge(s["hT_params"], 1)
            for t in range(TT):
                job_is_done(dve, ("hT", t, 1))
                for k in range(4):
                    tick(v.tensor_scalar(hT[:, 4 + k, t * P:(t + 1) * P], job_bank(("hT", t, 1))[:, k * P:(k + 1) * P],
                                         embT[:, 0, 4 + k:5 + k], embT[:, 1, 4 + k:5 + k], ALU.mult, ALU.add))
                settle()
                tt = slice(t * P, (t + 1) * P)
                read(v.tensor_copy(h_high[:, 4:8, tt], hT[:, 4:8, tt]), ("hT", t, 1))
            for t in range(TT):
                tt = slice(t * P, (t + 1) * P)
                for i in range(2):
                    k4 = slice(4 * i, 4 * i + 4)
                    job_is_read(dve, ("hT", t, i))
                    v.tensor_tensor(h_low[:, k4, tt], hT[:, k4, tt], h_high[:, k4, tt].bitcast(F32),
                                    ALU.subtract).then_inc(s["h_split"], 1)
            link(v.tensor_tensor(lbs[:, :, :], lbt[:, :, 0, :], lbt[:, :, 1, :], ALU.max))
            v.tensor_tensor(lbe[:, :, :, :], lbt[:, :, :, :],
                            lbs[:, :, :].unsqueeze(2).broadcast_to([P, 2, 2, NH]), ALU.subtract).then_inc(s["lbm_ready"], 1)
            dve.wait_ge(s["consts"], CONSTS)
            link(v.scalar_tensor_tensor(out=dist[:, :, :], in0=dist[:, :, :], scalar=-1.0, in1=dist[:, :, :],
                                        op0=ALU.mult, op1=ALU.min))
            dve.wait_ge(s["lb_exp"], 1)
            link(v.tensor_tensor(lbs[:, :, :], lbe[:, :, 0, :], lbe[:, :, 1, :], ALU.add))
            link(v.reciprocal(lbs[:, :, :], lbs[:, :, :]))
            link(v.tensor_tensor(lb[:, :, :], lbe[:, :, 0, :], lbs[:, :, :], ALU.mult))
            link(v.tensor_scalar(oml[:, :, :], lb[:, :, :], -1.0, 1.0, ALU.mult, ALU.add))
            job_is_done(dve, ("hT", 1, 1))
            dve.wait_ge(s["emb_in"], 32)
            for t in range(TT):
                link(v.tensor_tensor(X[:, t, :], X[:, t, :], lnp[:, 0, :], ALU.mult))
                link(v.tensor_tensor(X[:, t, :], X[:, t, :], lnp[:, 1, :], ALU.add))
            link(v.memset(kpad, 0.0))
            unit_is_done(dve, "kv")
            for g in range(NG):
                for o in range(2):
                    tick(v.tensor_copy(kpad[o * DH:(o + 1) * DH, g, o, :], proj_bank("kv", 0)[g * DH:(g + 1) * DH, 0:TOK]))
            tick(v.tensor_copy(va[:, :, :], proj_bank("kv", 1)[:, 0:TOK].rearrange("p (t n) -> p t n", t=TT)))
            settle()
            dve.sem_inc(proj_read[GI["kv"]], 1)

            def cseq(ap):
                return ap.rearrange("p (c n) -> p c n", n=HG_CHUNK)

            def gates(d):
                dve.wait_ge(proj_read[GI[f"zf{d}"]], 1)
                B = hg[d]
                for h in range(NH):
                    w = slice(h * TOK, (h + 1) * TOK)
                    tick(v.tensor_scalar(B["qe"][:, w], B["k"][:, w], oml[:, d, h:h + 1], lb[:, d, h:h + 1], ALU.mult, ALU.add))
                settle()
                v.tensor_scalar(B["k"], B["qe"], -1.0, 1.0, ALU.mult, ALU.add).then_inc(s["logf_ready"], 1)

            def rescaled(d):
                B = hg[d]
                dve.wait_ge(s["logf_in"], d + 1)
                way = slice(None, None, -1) if d else slice(None)
                link(v.tensor_tensor_scan(B["C"][:, way], scanm, B["C"][:, way], 0.0, ALU.mult, ALU.add))
                last, ref = (HG_CHUNK - 1, HG_CHUNK // 2) if d == 0 else (0, HG_CHUNK - 1 - HG_CHUNK // 2)
                C3 = cseq(B["C"])
                shape = [P, NH * NC, HG_CHUNK]
                v.tensor_tensor(cseq(B["A"]), C3, C3[:, :, ref:ref + 1].broadcast_to(shape),
                                ALU.subtract).then_inc(s["exps_in"], 1)
                v.tensor_tensor(cseq(B["Dl"]), C3[:, :, last:last + 1].broadcast_to(shape), C3,
                                ALU.subtract).then_inc(s["exps_in"], 1)

            def q_in():
                high(10)
                unit_is_done(dve, "qh")
                tick(v.tensor_copy(tiles_of(qhT, 0), pair("qh", 0)))
                tick(v.tensor_copy(tiles_of(qhT, 1), pair("qh", 1)))
                settle()
                dve.sem_inc(proj_read[GI["qh"]], 1)

            def scaled(d):
                B = hg[d]
                dve.wait_ge(s["k_ready"], 4 * d + 4)
                last = HG_CHUNK - 1 if d == 0 else 0
                tick(v.tensor_copy(decay[:, d, :], cseq(B["qe"])[:, :, last]))
                v.tensor_tensor(B["kp"], B["kp"], B["k"], ALU.mult).then_inc(s["kpT_ready"], 1)
                v.tensor_tensor(B["qrel"], B["qrel"], qhT, ALU.mult).then_inc(s["aT_ready"], 1)
                v.tensor_tensor(B["krel"], B["krel"], B["k"], ALU.mult).then_inc(s["aT_ready"], 1)
                tick(v.memset(B["A"], 0.0))
                settle()
                v.tensor_tensor(B["qe"], B["qe"], qhT, ALU.mult).then_inc(s["S_ready"], 1)

            def scores(b):
                t, g = BATCH[b]
                if b >= 2:
                    job_is_done(dve, ("pT", b - 2, 1))
                for h in range(2):
                    job_is_done(dve, ("score", b, h))
                    for q in range(2):
                        head = g * QPG + 2 * h + q
                        slope = 2.0 ** (-8.0 * (head + 1) / HQ)
                        ins = v.scalar_tensor_tensor(
                            out=score[b % 2][:, (2 * h + q) * TOK:(2 * h + q + 1) * TOK], in0=dist[:, t, :],
                            scalar=slope * DH ** 0.5, in1=job_bank(("score", b, h))[:, q * TOK:(q + 1) * TOK],
                            op0=ALU.mult, op1=ALU.add)
                        if q == 0:
                            tick(ins)
                    read(ins, ("score", b, h))
                settle()
                for h in range(2):
                    job_is_read(dve, ("score", b, h))
                link(v.tensor_reduce(mx[:, :], score[b % 2].rearrange("p (j n) -> p j n", j=QPG), AX_X, ALU.max))
                link(v.scalar_tensor_tensor(out=mx[:, :], in0=mx[:, :], scalar=DH ** -0.5,
                                            in1=sink[:, g * QPG:(g + 1) * QPG], op0=ALU.mult, op1=ALU.max))
                link(v.tensor_tensor(es[:, b % 2, :], sink[:, g * QPG:(g + 1) * QPG], mx[:, :], ALU.subtract))
                v.tensor_scalar(nm[:, b % 2, :], mx[:, :], -1.0, None, ALU.mult).then_inc(s["mx_ready"], 1)

            def mixed(b):
                t, g = BATCH[b]
                dve.wait_ge(s["prob_ready"], b + 1)
                link(v.tensor_tensor(den[:, b % 2, :], den[:, b % 2, :], es[:, b % 2, :], ALU.add))
                link(v.reciprocal(rden[:, b % 2, :], den[:, b % 2, :]))
                job_is_done(dve, ("pv", b, 0))
                w = slice(g * QPG * DH, (g + 1) * QPG * DH)
                tick(v.tensor_tensor(cat[:, t, w].rearrange("p (j n) -> p j n", j=QPG),
                                     job_bank(("pv", b, 0))[:, 0:QPG * DH].rearrange("p (j n) -> p j n", j=QPG),
                                     rden[:, b % 2, :].unsqueeze(2).broadcast_to([P, QPG, DH]), ALU.mult))
                settle()
                dve.sem_inc(s["attn_cat"], 1)
                dve.sem_inc(job_read[J["pv", b, 0] % 4], 1)

            def masked(d):
                for t in range(TT):
                    job_is_done(dve, ("aT", d, t))
                    read(v.copy_predicated(hg[d]["A"].rearrange("p (t h n) -> p t h n", t=TT, h=NH)[:, t, :, :],
                                           (maskF, maskB)[d][:, :].bitcast(I32).unsqueeze(1).broadcast_to([P, NH, P]),
                                           job_bank(("aT", d, t))[:, :].rearrange("p (h n) -> p h n", h=NH)), ("aT", d, t))

            def states(d, i):
                job_is_done(dve, ("kv", d, i))
                ps, c = job_bank(("kv", d, i)), chunk_of(d, i)
                if i == 0:
                    ins = v.tensor_copy(S(d, 0), ps[:, :])
                else:
                    job_is_read(dve, ("kv", d, i - 1))
                    for h in range(NH):
                        w = slice(h * P, (h + 1) * P)
                        ins = v.scalar_tensor_tensor(out=S(d, i)[:, w], in0=S(d, i - 1)[:, w],
                                                     scalar=decay[:, d, h * NC + c:h * NC + c + 1], in1=ps[:, w],
                                                     op0=ALU.mult, op1=ALU.add)
                        if h < NH - 1:
                            tick(ins)
                read(ins, ("kv", d, i))

            dve.wait_ge(s["par_in"], 64)
            def high(u):
                dve.wait_ge(win_in[u % WBUF], 16 * (u // WBUF + 1))
                v.tensor_copy(w_part(u, 1), w_raw(u)).then_inc(s["high_dve"], 1)

            gates(0)
            scores(0)
            rescaled(0)
            scores(1)
            gates(1)
            high(9)
            mixed(0)
            scores(2)
            rescaled(1)
            q_in()
            scaled(0)
            mixed(1)
            scores(3)
            scaled(1)
            unit_is_done(dve, "ih")
            tick(v.tensor_copy(ih[:, 0, :], proj_bank("ih", 0)[:, :]))
            v.tensor_copy(ih[:, 1, :], proj_bank("ih", 1)[:, :]).then_inc(proj_read[GI["ih"]], 1)
            mixed(2)
            masked(0)
            masked(1)
            mixed(3)
            states(0, 0)
            states(1, 0)
            for t in range(TT):
                dve.wait_ge(s["zg_sig"], t + 1)
                link(v.tensor_tensor(gz[:, t, :], gz[:, t, :], proj_bank("zg", t)[:, :], ALU.mult))
                link(v.tensor_tensor(gz[:, t, :], gz[:, t, :], normg[:, :], ALU.mult))
            dve.sem_inc(proj_read[GI["zg"]], 1)
            for i in range(1, NC - 1):
                for d in range(2):
                    states(d, i)
            for t in range(TT):
                dve.wait_ge(s["rms_std"], t + 1)
                link(v.reciprocal(rr[:, t, :], rr[:, t, :]))
                for h in range(NH):
                    tick(v.scalar_tensor_tensor(
                        out=cat[:, t, HQ * DH + h * P:HQ * DH + (h + 1) * P],
                        in0=job_bank(("o", t, 0))[:, h * P:(h + 1) * P],
                        scalar=rr[:, t, h:h + 1], in1=gz[:, t, h * P:(h + 1) * P], op0=ALU.mult, op1=ALU.mult))
                settle()
                dve.sem_inc(s["rec_cat"], 1)
                dve.sem_inc(job_read[J["o", t, 0] % 4], 1)
            job_is_done(dve, ("catT", 3, 0))
            read(v.tensor_copy(hT[:, 4:8, P:2 * P], job_bank(("catT", 3, 0))[:, :].rearrange("p (k n) -> p k n", k=4)),
                 ("catT", 3, 0))

            def logits(t):
                dve.wait_ge(s["logit_done"], t + 1)
                link(v.tensor_tensor(lg[:, t, :], bank[4 + t][:, 0:NE], br[:, :], ALU.add))
                link(v.max(m8[:, t, :], lg[:, t, :]))
                link(v.max_index(i8[:, t, :], m8[:, t, :], lg[:, t, :]))
                tick(v.tensor_scalar(nm0[:, t:t + 1], m8[:, t, 0:1], -1.0, None, ALU.mult))
                link(v.tensor_copy(i8f[:, t, :], i8[:, t, :]))

            for t in range(TT):
                for n in range(2):
                    dve.wait_ge(s["mix_done"], 2 * t + n + 1)
                    w = slice(n * 512, n * 512 + 512)
                    tick(v.scalar_tensor_tensor(out=X[:, t, w], in0=X[:, t, w], scalar=DEEP_ALPHA,
                                                in1=bank[4 + 2 * t + n][:, :], op0=ALU.mult, op1=ALU.add))
                settle()
                norm_stats(X, t)
                dve.wait_ge(s["var_ready"], TT + t + 1)
                dve.wait_ge(s["ln1_in"], 32)
                for n in range(2):
                    w = slice(n * 512, n * 512 + 512)
                    tick(v.scalar_tensor_tensor(out=X[:, t, w], in0=X[:, t, w], scalar=mv[:, t, 0:1],
                                                in1=lnp[:, 0, w], op0=ALU.subtract, op1=ALU.mult))
                    if n == 0:
                        dve.wait_ge(s["std_ready"], TT + t + 1)
                        tick(v.reciprocal(rstd[:, t:t + 1], rstd[:, t:t + 1]))
                    settle()
                    v.scalar_tensor_tensor(out=X[:, t, w], in0=X[:, t, w], scalar=rstd[:, t:t + 1],
                                           in1=lnp[:, 1, w], op0=ALU.mult, op1=ALU.add).then_inc(s["x1_ready"], 1)
            turned("x1T", 1, 1)
            logits(0)
            logits(1)
            dve.sem_inc(s["top_ready"], 1)
            four = [P, TT, TOPK, NE]
            for t in range(TT):
                tick(v.tensor_tensor(hot[:, 0, t, :, :], iota_s[:, 0:1, 0:NE].broadcast_to([P, TOPK, NE]),
                                     i8f[:, t, 0:TOPK].unsqueeze(2).broadcast_to([P, TOPK, NE]), ALU.is_equal))
            settle()
            v.tensor_reduce(mask[:, :, :], hot[:, 0, :, :, :].rearrange("p t j e -> p t e j"), AX_X,
                            ALU.add).then_inc(s["mask_ready"], 1)
            dve.wait_ge(s["mask_ready"], 1)
            dve.wait_ge(s["rank_done"], 1)
            link(v.scalar_tensor_tensor(out=key[:, :, :], in0=bank[6][:, 0:TT * NE].rearrange("p (t e) -> p t e", t=TT),
                                        scalar=NOT_HERE, in1=mask[:, :, :], op0=ALU.add, op1=ALU.mult))
            v.tensor_scalar(key[:, :, :], key[:, :, :], -NOT_HERE, None, ALU.add).then_inc(s["key_ready"], 1)
            dve.wait_ge(s["key_ready"], 1)
            for t in range(TT):
                v.tensor_scalar(pick[:, t, :], iota_s[:, 0, :], key[:, t, 0:1], None, ALU.is_equal).then_inc(s["picked"], 1)
            v.tensor_copy(bsel[:, :], ident[:, 0:1].broadcast_to([P, SLOTS])).then_inc(s["picked"], 1)
            dve.wait_ge(s["g4_ready"], TT)
            link(v.reciprocal(gs[:, :], gs[:, :]))
            link(v.tensor_tensor(g4[:, :, :], g4[:, :, :], gs[:, :].unsqueeze(2).broadcast_to([P, TT, TOPK]), ALU.mult))
            for t in range(TT):
                tick(v.tensor_tensor(hot[:, 1, t, :, :], hot[:, 0, t, :, :],
                                     g4[:, t, :].unsqueeze(2).broadcast_to([P, TOPK, NE]), ALU.mult))
            settle()
            v.tensor_reduce(gate[:, :, :], hot[:, 1, :, :, :].rearrange("p t j e -> p t e j"), AX_X,
                            ALU.add).then_inc(s["gate_ready"], 1)
            link(v.tensor_copy(cnt[:, 0:1], bank[7][0:NE, 0:1]))
            for i in range(1, TOK // SLOTS):
                tick(v.tensor_scalar(cnt[:, i:i + 1], cnt[:, 0:1], float(SLOTS * i + 1), None, ALU.is_ge))
            settle()
            v.tensor_reduce(cnt[:, 4:5], cnt[:, 1:4], AX_X, ALU.add).then_inc(s["ex_ready"], 1)
            dve.wait_ge(s["route_done"], 1)
            tick(v.tensor_copy(keyT, bank[5][0:NE, 0:TOK]))
            tick(v.tensor_copy(putT[0:NE, :], bank[5][0:NE, TOK:2 * TOK]))
            link(v.tensor_scalar(cnt[:, 5:6], bank[7][0:NE, 1:2], float(NE), None, ALU.add))
            link(v.tensor_scalar(dlt[:, 0, :], iota_s[0:NE, 0, 0:NPASS], cnt[:, 5:6], None, ALU.subtract))
            link(v.tensor_scalar(dlt[:, 1, :], dlt[:, 0, :], 0.0, None, ALU.is_ge))
            link(v.scalar_tensor_tensor(out=dlt[:, 2, :], in0=dlt[:, 0, :], scalar=cnt[:, 4:5], in1=dlt[:, 1, :],
                                        op0=ALU.is_lt, op1=ALU.mult))
            link(v.tensor_scalar(dlt[:, 0, :], dlt[:, 0, :], 1.0, -float(SLOTS), ALU.add, ALU.mult))
            tick(v.tensor_tensor(base[:, :], dlt[:, 0, :], dlt[:, 2, :], ALU.mult))
            tick(v.tensor_copy(esel[0:NE, NE:NPASS], dlt[:, 2, NE:NPASS]))
            tick(v.tensor_copy(esel[0:NE, 0:NE], ident[0:NE, 0:NE]))
            settle()
            dve.sem_inc(s["sel_ready"], 1)
            for t in range(TT):
                tick(v.tensor_scalar(acc[:, t, :], X[:, t, :], DEEP_ALPHA, None, ALU.mult))
            dve.wait_ge(s["plan_ps"], 1)
            v.tensor_copy(plan[0:1, 0:NPASS], bank[4][0:1, 0:NPASS]).then_inc(s["plan_ready"], 1)
            v.tensor_scalar(plan[0:1, NPASS:NPASS + 1], bank[4][0:1, NPASS:NPASS + 1], float(NE), None,
                            ALU.add).then_inc(s["plan_ready"], 1)
            v.tensor_scalar(plan[0:1, NPASS + 1:NPASS + 2], bank[4][0:1, NPASS:NPASS + 1], float(NE - 1), None,
                            ALU.add).then_inc(s["plan_ready"], 1)
            tick(v.tensor_copy(keyp[:, :, :], bank[6][:, 128:128 + TT * NPASS].rearrange("p (t n) -> p t n", t=TT)))
            tick(v.tensor_copy(gatep[:, :, :], bank[6][:, 256:256 + TT * NPASS].rearrange("p (t n) -> p t n", t=TT)))
            settle()
            dve.sem_inc(s["scat_read"], 1)

            done = vstate["n"]

            def scattered(p, q):
                dve.wait_ge(s["scat_done"], 4 * p + q + 1)
                w = slice((q % 2) * 512, (q % 2) * 512 + 512)
                v.tensor_tensor(acc[:, q // 2, w], acc[:, q // 2, w], bank[4 + q][:, :], ALU.add).then_inc(s["scat_read"], 1)

            def expert_pass(p, here, following, last=False):
                dve.wait_ge(s["put_ps"], p + 1)
                for t in range(TT):
                    v.tensor_scalar(gpick[:, t, :], iota_s[:, :, :].rearrange("p a n -> p (a n)"),
                                    keyp[:, t, here], gatep[:, t, here],
                                    ALU.is_equal, ALU.mult).then_inc(s["picked"], 1)
                dve.wait_ge(s["gath_done"], p + 1)
                dve.wait_ge(s["chunk_used"], p * CHUNKS + 2)
                for t in range(0 if last else TT):
                    v.tensor_scalar(pick[:, t, :], iota_s[:, 0, :], keyp[:, t, following], None,
                                    ALU.is_equal).then_inc(s["picked"], 1)
                if not last:
                    v.tensor_copy(bsel[:, :], esel[:, following].broadcast_to([P, SLOTS])).then_inc(s["picked"], 1)
                for n in range(2):
                    dve.wait_ge(s["chunk_used"], p * CHUNKS + UPC)
                    pair = bank[n][:, :].rearrange("p (f two) -> p f two", two=2)
                    w = slice(n * 256, n * 256 + 256)
                    v.tensor_scalar(glu[:, w], pair[:, :, 0], LIMIT, None, ALU.min).then_inc(s["glu_ready"], 1)
                    v.tensor_scalar(lin[:, w], pair[:, :, 1], LIMIT, -LIMIT, ALU.min, ALU.max).then_inc(s["dve_step"], 1)
                for n in range(2):
                    w = slice(n * 256, n * 256 + 256)
                    dve.wait_ge(s["dve_step"], done + 4 * p + 2 + n)
                    dve.wait_ge(s["glu_ready"], 2 * p + n + 1)
                    v.scalar_tensor_tensor(out=lin[:, w], in0=lin[:, w], scalar=1.0, in1=glu[:, w],
                                           op0=ALU.add, op1=ALU.mult).then_inc(s["dve_step"], 1)
                    dve.wait_ge(s["dve_step"], done + 4 * p + 3 + n)
                    dve.wait_ge(s["sig_ready"], 2 * p + n + 1)
                    v.tensor_tensor(act_[:, w], lin[:, w], sig[:, w], ALU.mult).then_inc(s["act_ready"], 1)
                if last:
                    dve.wait_ge(s["chunk_used"], (p + 1) * CHUNKS)
                    v.tensor_copy(ysb[:, 512:1024], bank[3][:, :]).then_inc(s["y_ready"], 1)
                    return
                dve.wait_ge(s["scat_read"], 4 * p + 1)
                for q in range(4):
                    scattered(p, q)

            dve.wait_ge(s["plan_ready"], 3)
            npass = dve.value_load(plan[0:1, NPASS:NPASS + 1], min_val=NE, max_val=NPASS - 1)
            expert_pass(0, slice(0, 1), slice(1, 2))
            last_pass = dve.value_load(plan[0:1, NPASS + 1:NPASS + 2], min_val=NE - 1, max_val=NPASS - 2)
            with dve.Fori(1, last_pass) as p:
                expert_pass(p, bass.ds(p, 1), bass.ds(p + 1, 1))
            expert_pass(last_pass, bass.ds(last_pass, 1), None, last=True)
            _, t3, s3, _ = counted(dve, s["tail_step"])
            dve.wait_ge(s["ln2_in"], 32)
            for t in range(TT):
                for n in range(2):
                    dve.wait_ge(s["scat_done"], 4 * npass + 2 * t + n + 1)
                    t3(v.bn_stats(st[:, t, n, :], bank[4 + 2 * t + n][:, :]))
                s3()
                v.bn_aggr(mv[:, t, :], st[:, t, :, :]).then_inc(s["var_ready"], 1)
            for t in range(TT):
                dve.wait_ge(s["var_ready"], 2 * TT + t + 1)
                for n in range(2):
                    w = slice(n * 512, n * 512 + 512)
                    t3(v.scalar_tensor_tensor(out=acc[:, t, w], in0=bank[4 + 2 * t + n][:, :], scalar=mv[:, t, 0:1],
                                              in1=lnp[:, 0, w], op0=ALU.subtract, op1=ALU.mult))
                dve.wait_ge(s["std_ready"], 2 * TT + t + 1)
                t3(v.reciprocal(rstd[:, t:t + 1], rstd[:, t:t + 1]))
                s3()
                for n in range(2):
                    w = slice(n * 512, n * 512 + 512)
                    v.scalar_tensor_tensor(out=acc[:, t, w], in0=acc[:, t, w], scalar=rstd[:, t:t + 1],
                                           in1=lnp[:, 1, w], op0=ALU.mult, op1=ALU.add).then_inc(s["acc_ready"], 1)

        @block.tensor
        def _(pe):
            mm = nc.tensor.matmul
            tr = nc.tensor.transpose
            pe.wait_ge(s["consts"], IDENT_CONSTS)

            def turn(b, src, tiles):
                for n, (t, k) in enumerate(tiles):
                    ins = tr(b[:, n * P:(n + 1) * P], src[:, t, k * P:(k + 1) * P], ident[:, :])
                return ins

            def keep_warm(b, n):
                for _ in range(n):
                    mm(b[:, 0:P], ident[:, :], ident[:, :], start=True, stop=True)

            WARM = {("hT", 0, 0): 14, ("x1T", 1, 0): 3, ("x1T", 1, 1): 4}

            def project(name, half):
                u, g = UI[name, half], GI[name]
                if half == 0 and g == 1:
                    pe.wait_ge(s["lbm_ready"], 1)
                if half == 0 and g >= 2:
                    pe.wait_ge(proj_read[g - 2], 1)
                w_low, w_high = (w_part(u, i).rearrange("p (k n) -> p k n", k=KT) for i in range(2))

                def products(outs, columns=True):
                    for i, (wp, hp) in enumerate(((w_high, h_high), (w_high, h_low), (w_low, h_high))):
                        if i == 0:
                            high_is_ready(pe, u)
                        elif i == 1 and u == 0:
                            pe.wait_ge(s["h_split"], 2 * TT)
                        elif i == 2:
                            pe.wait_ge(s["low_ready"], u + 1)
                        for k in range(KT):
                            for out, wc, hc in outs:
                                ops = (wp[:, k, wc], hp[:, k, hc])
                                ins = mm(out, *(ops if columns else ops[::-1]), start=(i == 0 and k == 0),
                                         stop=(i == 2 and k == KT - 1))
                    return ins

                tiles = [slice(i * P, (i + 1) * P) for i in range(2)]
                side_by = slice(half * 256, half * 256 + 256)
                if name in ("zf0", "zf1", "qh", "qa"):
                    ins = products([(proj_bank(name, c)[:, side_by], tiles[c], slice(0, TOK)) for c in range(2)])
                elif name == "kv":
                    products([(proj_bank(name, 0)[:, 0:TOK], tiles[0], slice(0, TOK))])
                    for t in range(TT):
                        ins = products([(proj_bank(name, 1)[:, tiles[t]], tiles[1], tiles[t])], columns=False)
                else:
                    ins = products([(proj_bank(name, t)[:, side_by], slice(0, 256), tiles[t]) for t in range(TT)],
                                   columns=False)
                ins.then_inc(s["proj_done"], 1)

            def mix_out(t, part_, n):
                if part_ == 0 and n == 0:
                    pe.wait_ge(proj_read[GI["zg" if t == 0 else "ih"]], 1)
                    pe.wait_ge(s["wout_in"], 32)
                if n == 0:
                    for i in ((0, 1), (2 + t,))[part_]:
                        job_is_read(pe, ("catT", i, 0))
                for k in range(4 * part_, 4 * part_ + 4):
                    ins = mm(bank[4 + 2 * t + n][:, :], hT[:, k, t * P:(t + 1) * P],
                             wbuf[:, 1 + k // 4, (k % 4) * D + n * 512:(k % 4) * D + (n + 1) * 512],
                             start=(k == 0), stop=(k == KT - 1))
                if part_ == 1:
                    ins.then_inc(s["mix_done"], 1)
                elif n == 1:
                    ins.then_inc(s["mix_half"], 1)

            def recur(o, t):
                for d in range(2):
                    job_is_read(pe, ("aT", d, t))
                for d, i in ((0, NC - 2), (1, NC - 2)):
                    job_is_read(pe, ("kv", d, i))
                pe.wait_ge(s["S_ready"], 2)
                for h in range(NH):
                    w = slice(h * P, (h + 1) * P)
                    aT = [hg[d]["A"].rearrange("p (t h n) -> p t h n", t=TT, h=NH)[:, t, h, :] for d in range(2)]
                    mm(o[:, w], aT[0], ih[:, t, w], start=True, stop=False)
                    for d, i in [(d, i) for d in range(2) for i in range(1, NC) if chunk_of(d, i) // 2 == t]:
                        c = chunk_of(d, i)
                        r = slice(HG_CHUNK * (c % 2), HG_CHUNK * (c % 2) + HG_CHUNK)
                        mm(o[r, w], hg[d]["qe"][:, h * TOK + c * HG_CHUNK:h * TOK + (c + 1) * HG_CHUNK],
                           S(d, i - 1)[:, w], start=False, stop=False)
                    ins = mm(o[:, w], aT[1], ih[:, t, w], start=False, stop=True)
                return ins

            for step in STEPS:
                kind, d, i = step
                if kind == "proj":
                    if (d, i) == ("qa", 0):
                        for t in range(TT):
                            for hh in range(2):
                                job_is_read(pe, ("hT", t, hh))
                    project(d, i)
                    continue
                if kind == "mix":
                    mix_out(d, *i)
                    continue
                if kind == "logit":
                    keep_warm(bank[4 + d], 5 * d)
                    for hh in range(2):
                        job_is_read(pe, ("x1T", d, hh))
                    for k in range(KT):
                        ins = mm(bank[4 + d][:, 0:NE], hT[:, k, d * P:(d + 1) * P], wr[:, k, :],
                                 start=(k == 0), stop=(k == KT - 1))
                    ins.then_inc(s["logit_done"], 1)
                    continue
                b = job_bank(step)
                if J[step] >= 4:
                    pe.wait_ge(job_read[J[step] % 4], J[step] // 4)
                keep_warm(b, WARM.get(step, 0))
                if step == ("hT", 1, 0):
                    pe.wait_ge(s["rows_in"], 48)
                    tr(bank[7][:, 0:32], rows[:, :], ident[0:32, 0:32]).then_inc(s["lb_ps"], 1)
                if kind == "hT":
                    pe.wait_ge(s["h_ready"], d + 1)
                    ins = turn(b, X, [(d, 4 * i + k) for k in range(4)])
                elif kind == "x1T":
                    pe.wait_ge(s["x1_ready"], 2 * d + i + 1)
                    ins = turn(b, X, [(d, 4 * i + k) for k in range(4)])
                elif kind == "catT":
                    if d < 2:
                        pe.wait_ge(s["attn_cat"], len(BATCH))
                        ins = turn(b, cat, [(t, 2 * d + k) for k in range(2) for t in range(TT)])
                    else:
                        pe.wait_ge(s["rec_cat"], d - 1)
                        ins = turn(b, cat, [(d - 2, 4 + k) for k in range(4)])
                elif kind == "score":
                    if step == ("score", 0, 0):
                        pe.wait_ge(proj_read[GI["qa"]], 1)
                        pe.wait_ge(proj_read[GI["kv"]], 1)
                    t, g = BATCH[d]
                    for q in range(2):
                        head = g * QPG + 2 * i + q
                        ins = mm(b[:, q * TOK:(q + 1) * TOK], qaT[:, head // 2, t * P:(t + 1) * P],
                                 kpad[:, g, head % 2, :], start=True, stop=True)
                elif kind == "pT":
                    pe.wait_ge(s["prob_ready"], d + 1)
                    for q in range(2):
                        for kt in range(TT):
                            src = score[d % 2][:, (2 * i + q) * TOK + kt * P:(2 * i + q) * TOK + (kt + 1) * P]
                            ins = tr(b[:, q * TOK + kt * P:q * TOK + (kt + 1) * P], src, ident[:, :])
                elif kind == "pv":
                    t, g = BATCH[d]
                    for hh in range(2):
                        job_is_read(pe, ("pT", d, hh))
                    for q in range(QPG):
                        for kt in range(TT):
                            ins = mm(b[:, q * DH:(q + 1) * DH],
                                     probT[d % 2][:, q * TOK + kt * P:q * TOK + (kt + 1) * P],
                                     va[:, kt, g * DH:(g + 1) * DH], start=(kt == 0), stop=(kt == TT - 1))
                elif kind == "kpT":
                    pe.wait_ge(s["kpT_ready"], d + 1)
                    for h in range(NH):
                        ins = tr(b[:, h * P:(h + 1) * P], hg[d]["kp"][:, h * TOK + i * P:h * TOK + (i + 1) * P], ident[:, :])
                elif kind == "aT":
                    pe.wait_ge(s["aT_ready"], 2 * d + 2)
                    for h in range(NH):
                        w = slice(h * TOK + i * P, h * TOK + (i + 1) * P)
                        ins = mm(b[:, h * P:(h + 1) * P], hg[d]["krel"][:, w], hg[d]["qrel"][:, w], start=True, stop=True)
                elif kind == "kv":
                    c = chunk_of(d, i)
                    job_is_read(pe, ("kpT", d, c // 2))
                    pe.wait_ge(proj_read[GI["ih"]], 1)
                    pe.wait_ge(s["pad_ready"], 2 * d + 2)
                    for h in range(NH):
                        w = slice(h * P, (h + 1) * P)
                        ins = mm(b[:, w], kpt(d, c % 2)[:, c // 2, w], ih[:, c // 2, w], start=True, stop=True)
                elif kind == "o":
                    ins = recur(b, d)
                ins.then_inc(s["job_done"], 1)

            keep_warm(bank[6], 7)
            pe.wait_ge(s["mask_ready"], 1)
            pe.wait_ge(s["consts"], CONSTS)
            mm(bank[6][:, 0:NE], below[:, :], mask[:, 0, :], start=True, stop=True)
            mm(bank[6][:, NE:2 * NE], ones[:, :], mask[:, 0, :], start=True, stop=False)
            mm(bank[6][:, NE:2 * NE], below[:, :], mask[:, 1, :], start=False, stop=True)
            for t in range(TT):
                ins = mm(bank[7][0:NE, 0:1], mask[:, t, :], ones[:, 0:1], start=(t == 0), stop=(t == TT - 1))
            ins.then_inc(s["rank_done"], 1)

            def places():
                pe.wait_ge(s["gate_ready"], 1)
                pe.wait_ge(s["ex_ready"], 1)
                for t in range(TT):
                    tr(bank[5][0:NE, t * P:(t + 1) * P], key[:, t, :], ident[:, :])
                    tr(bank[5][0:NE, TOK + t * P:TOK + (t + 1) * P], gate[:, t, :], ident[:, :])
                mm(bank[7][0:NE, 1:2], below[0:NE, 0:NE], cnt[:, 4:5], start=True, stop=True).then_inc(s["route_done"], 1)

            def passes():
                pe.wait_ge(s["sel_ready"], 1)
                for t in range(TT):
                    w = slice(t * P, (t + 1) * P)
                    o = slice(128 + t * NPASS, 128 + (t + 1) * NPASS)
                    mm(bank[6][:, o], keyT[:, w], esel[0:NE, :], start=True, stop=False)
                    mm(bank[6][:, o], ones[0:NE, :], base[:, :], start=False, stop=True)
                    mm(bank[6][:, 256 + t * NPASS:256 + (t + 1) * NPASS], putT[0:NE, w], esel[0:NE, :], start=True, stop=True)
                mm(bank[4][0:1, 0:NPASS], part[0:NE, 0:1], esel[0:NE, :], start=True, stop=True)
                mm(bank[4][0:1, NPASS:NPASS + 1], cnt[:, 4:5], ones[0:NE, 0:1], start=True, stop=True).then_inc(s["plan_ps"], 1)

            def gather():
                for t in range(TT):
                    for c in range(2):
                        ins = mm(bank[0][c * SLOTS:(c + 1) * SLOTS, :], pick[:, t, :], X[:, t, c * 512:(c + 1) * 512],
                                 start=(t == 0), stop=(t == TT - 1))
                ins.then_inc(s["gath_done"], 1)

            def gather_turned(p):
                pe.wait_ge(s["xg_ready"], p + 1)
                for i in range(4):
                    ins = tr(bank[1][:, i * P:(i + 1) * P], xg[:, i * P:(i + 1) * P], ident[:, :])
                ins.then_inc(s["xT_ps"], 1)

            def scatter(start=True, stop=True):
                for q in range(4):
                    mm(bank[4 + q][:, :], putT[:, (q // 2) * P:(q // 2 + 1) * P], ysb[:, (q % 2) * 512:(q % 2 + 1) * 512],
                       start=start, stop=stop).then_inc(s["scat_done"], 1)

            NPICK = 2 * TT + 1

            def weights(p, c):
                if c >= SIDE and isinstance(p, int) and p in (0, 2):
                    pe.wait_ge(side_in[c - SIDE], 16 if p == 0 else 32)
                    return side[c - SIDE]
                pe.wait_ge(chunk_in[c], 16 * p + 16 if c < SIDE or not isinstance(p, int) else 16)
                return ring[:, c, :]

            def hidden(p, last):
                pe.wait_ge(s["xT_ready"], p + 1)
                for k in range(KT):
                    wk = weights(p, k)
                    for n in range(2):
                        for c in range(2):
                            ins = mm(bank[n][c * SLOTS:(c + 1) * SLOTS, :], xT[:, k, :],
                                     wk[:, c * FF + n * 512:c * FF + (n + 1) * 512], start=(k == 0), stop=(k == KT - 1))
                    ins.then_inc(s["chunk_used"], 1)
                    if k == 0:
                        if isinstance(p, int) and p == 0:
                            places()
                            pe.wait_ge(s["bias_in"], 32)
                        for n in range(2):
                            for c in range(2):
                                mm(bank[n][c * SLOTS:(c + 1) * SLOTS, :], bsel[:, :],
                                   bup[:, c * FF + n * 512:c * FF + (n + 1) * 512], start=False, stop=False)
                    if isinstance(p, int) and (p, k) == (0, 4):
                        passes()
                    if last and k == 3:
                        pe.wait_ge(s["scat_read"], 4 * p + 1)
                        for q in range(4):
                            mm(bank[4 + q][:, :], ident[:, :], acc[:, q // 2, (q % 2) * 512:(q % 2 + 1) * 512],
                               start=True, stop=False)
                        pe.wait_ge(s["y_ready"], 2 * p + 2)
                        pe.wait_ge(s["put_ready"], p + 1)
                        scatter(start=False, stop=False)

            def expert_pass(p, last=False):
                hidden(p, last)
                if not last:
                    pe.wait_ge(s["scat_read"], 4 * p + 1)
                    pe.wait_ge(s["y_ready"], 2 * p + 2)
                    pe.wait_ge(s["put_ready"], p + 1)
                    scatter()
                pe.wait_ge(s["picked"], NPICK * p + TT + 1 + TT)
                for t in range(TT):
                    ins = tr(bank[2][:, t * P:(t + 1) * P], gpick[:, t, :], ident[:, :])
                ins.then_inc(s["put_ps"], 1)
                if last:
                    keep_warm(bank[3], 12)
                pe.wait_ge(s["act_ready"], 2 * p + 2)
                for i in range(4):
                    ins = tr(bank[3][:, i * P:(i + 1) * P], act_[:, i * P:(i + 1) * P], ident[:, :])
                ins.then_inc(s["actT_ps"], 1)
                if not last:
                    pe.wait_ge(s["picked"], NPICK * p + 2 * TT + 2 + TT)
                    gather()
                else:
                    keep_warm(bank[0], 4)
                pe.wait_ge(s["actT_ready"], p + 1)
                pe.wait_ge(s["put_ready"], p + 2)
                for i in range(DNC):
                    wk = weights(p, UPC + i)
                    for n in range(2):
                        for c in range(2):
                            ins = mm(bank[2 + n][c * SLOTS:(c + 1) * SLOTS, :], actT[:, i * P + c * SLOTS:i * P + (c + 1) * SLOTS],
                                     wk[:, c * D + n * 512:c * D + (n + 1) * 512],
                                     start=(i == 0), stop=(i == DNC - 1))
                    ins.then_inc(s["chunk_used"], 1)
                    if i == 1 and not last:
                        gather_turned(p + 1)

            for t in range(TT):
                for hh in range(2):
                    job_is_read(pe, ("x1T", t, hh))
            keep_warm(bank[0], 4)
            pe.wait_ge(s["picked"], TT + 1)
            gather()
            pe.sem_inc(s["put_ps"], 1)
            keep_warm(bank[1], 3)
            gather_turned(0)
            keep_warm(bank[0], 3)
            for p in range(3):
                expert_pass(p)
            for c in range(SIDE, CHUNKS):
                pe.sem_inc(chunk_in[c], 32)
            npass = pe.value_load(plan[0:1, NPASS:NPASS + 1], min_val=NE, max_val=NPASS - 1)
            last_pass = pe.value_load(plan[0:1, NPASS + 1:NPASS + 2], min_val=NE - 1, max_val=NPASS - 2)
            with pe.Fori(3, last_pass) as p:
                expert_pass(p)
            expert_pass(last_pass, last=True)
            pe.wait_ge(s["y_ready"], 2 * npass + 2)
            pe.wait_ge(s["put_ready"], npass + 1)
            scatter(start=False)


_INS = ['x', 'emb_ln_g', 'emb_ln_b', 'w_in', 'attn_sink', 'hgrn_lb_logits', 'hgrn_norm_g', 'w_out', 'ln1_g', 'ln1_b',
        'w_router', 'b_router', 'w_up', 'b_up', 'w_down', 'b_down', 'ln2_g', 'ln2_b']
_OUTS = [((1, 256, 1024), 'float32')]


def kernel(**inputs):
    import numpy as _np
    import concourse.bacc as _bacc
    from concourse import mybir as _mybir
    from concourse.bass_utils import run_bass_kernel_spmd as _run

    nc = _bacc.Bacc("TRN2", target_bir_lowering=False, num_devices=1)
    arrays, args = {}, []
    for name in _INS:
        a = _np.ascontiguousarray(inputs[name])
        arrays[f"in_{name}_dram"] = a
        args.append(nc.dram_tensor(f"in_{name}_dram", a.shape, _mybir.dt.from_np(a.dtype), kind="ExternalInput").ap())
    for i, (shape, dtype) in enumerate(_OUTS):
        dt = _mybir.dt.from_np(_np.dtype(dtype))
        args.append(nc.dram_tensor(f"out_{i}_dram", shape, dt, kind="ExternalOutput").ap())
    encoder_layer(nc, *args)
    r = _run(nc, [arrays], core_ids=[0])
    got = tuple(r.results[0][f"out_{i}_dram"] for i in range(len(_OUTS)))
    return got[0]
```
